# Optimizing a Trainium2 kernel written in Bass

```python
import math, functools
import jax, jax.numpy as jnp
from jax import lax
import numpy as np

D_MODEL = 1024
BATCH = 1
SEQ = 512
DEPTH = 2
DEC_BATCH = 8
DEC_SEQ = 1
PAST_LEN = 2048
PAGE_SIZE = 128

N_A_LAYERS = DEPTH // 2
N_B_LAYERS = DEPTH - N_A_LAYERS
SSM_GROUP = 16
SSM_GROUPS = D_MODEL // SSM_GROUP
SSM_STATE = 64
DT_MIN = 0.001
DT_MAX = 0.1
N_HEADS = 16
QK_NOPE = 64
QK_ROPE = 32
V_HEAD = 64
Q_LORA = 512
KV_LORA = 256
ROPE_THETA = 10000.0
Q_BLOCK = 128
SM_SCALE = 1.0 / math.sqrt(QK_NOPE + QK_ROPE)
NEG_INF = -1e30
PEER_HEADS = 8
N_KEYS = 128
N_EXPERTS = N_KEYS * N_KEYS
PEER_D_KEY = 256
PEER_TOPK = 16
PEER_TOKEN_BLOCK = 128
EPS = 1e-6

kernel_name = "yoco_s5_mla_peer_adaln_step"

def rmsnorm(x, g):
    xf = x.astype(jnp.float32)
    y = xf * lax.rsqrt(jnp.mean(xf * xf, axis=-1, keepdims=True) + EPS)
    return (y * g.astype(jnp.float32)).astype(x.dtype)

def modulate(h, shift, scale):
    return h * (1.0 + scale[:, None, :]) + shift[:, None, :]

def split_mod(c, w, b, n):
    mod = jnp.einsum("bd,de->be", jax.nn.silu(c), w) + b
    return jnp.split(mod, n, axis=-1)

def rope(x, pos):
    half = QK_ROPE // 2
    inv = ROPE_THETA ** (-jnp.arange(0, QK_ROPE, 2, dtype=jnp.float32) / QK_ROPE)
    ang = pos.astype(jnp.float32)[..., None] * inv
    cos, sin = jnp.cos(ang), jnp.sin(ang)
    xf = x.astype(jnp.float32)
    x1, x2 = xf[..., :half], xf[..., half:]
    return jnp.concatenate([x1 * cos - x2 * sin, x1 * sin + x2 * cos], axis=-1).astype(x.dtype)

def _linear_combine(left, right):
    a_l, b_l = left
    a_r, b_r = right
    return a_r * a_l, a_r * b_l + b_r

def s5_mixer(u, h0_re, h0_im, a_re, a_im, log_dt, b_re, b_im, c_re, c_im, d_skip, w_glu):
    f32 = jnp.float32
    bsz, length, _ = u.shape
    uf = u.astype(f32).reshape(bsz, length, SSM_GROUPS, SSM_GROUP)
    lam = lax.complex(a_re.astype(f32), a_im.astype(f32))
    dt = jnp.exp(log_dt.astype(f32))[:, None]
    lam_bar = jnp.exp(lam * dt)
    b_mat = lax.complex(b_re.astype(f32), b_im.astype(f32))
    b_bar = ((lam_bar - 1.0) / lam)[:, :, None] * b_mat
    c_mat = lax.complex(c_re.astype(f32), c_im.astype(f32))
    bu = jnp.einsum("blgp,gnp->blgn", uf.astype(jnp.complex64), b_bar)
    h0 = lax.complex(h0_re.astype(f32), h0_im.astype(f32))
    bu = bu.at[:, 0].add(lam_bar * h0)
    a_seq = jnp.broadcast_to(lam_bar, bu.shape)
    _, h = lax.associative_scan(_linear_combine, (a_seq, bu), axis=1)
    y = jnp.real(jnp.einsum("blgn,gpn->blgp", h, c_mat)) + d_skip.astype(f32).reshape(SSM_GROUPS, SSM_GROUP) * uf
    z = jax.nn.gelu(y.reshape(bsz, length, D_MODEL))
    a, g = jnp.split(z @ w_glu.astype(f32), 2, axis=-1)
    out = (a * jax.nn.sigmoid(g)).astype(u.dtype)
    h_last = h[:, -1]
    return out, jnp.real(h_last).astype(h0_re.dtype), jnp.imag(h_last).astype(h0_im.dtype)

def shared_kv(x, c, positions, w_mod_kv, b_mod_kv, g_kv_norm, w_dkv, g_ckv, w_kr):
    sh, sc = split_mod(c, w_mod_kv, b_mod_kv, 2)
    h = modulate(rmsnorm(x, g_kv_norm), sh, sc)
    ckv = rmsnorm(h @ w_dkv, g_ckv)
    kr = rope(h @ w_kr, positions)
    return ckv, kr

def mla_query(h, positions, w_dq, g_cq, w_uq, w_ukv):
    bsz, length, _ = h.shape
    cq = rmsnorm(h @ w_dq, g_cq)
    q = (cq @ w_uq).reshape(bsz, length, N_HEADS, QK_NOPE + QK_ROPE)
    q_nope, q_pe = q[..., :QK_NOPE], q[..., QK_NOPE:]
    q_pe = rope(q_pe, positions[:, None])
    q_lat = jnp.einsum("blhd,chd->blhc", q_nope, w_ukv[..., :QK_NOPE])
    return q_lat, q_pe

def mla_out(o_lat, w_ukv, w_o):
    o = jnp.einsum("blhc,chd->blhd", o_lat, w_ukv[..., QK_NOPE:])
    return o.reshape(o.shape[0], o.shape[1], N_HEADS * V_HEAD) @ w_o

def prompt_attention(q_lat, q_pe, ckv, kr):
    f32 = jnp.float32
    bsz, length = q_lat.shape[:2]
    nb = length // Q_BLOCK
    ql = q_lat.reshape(bsz, nb, Q_BLOCK, N_HEADS, KV_LORA).transpose(1, 0, 2, 3, 4)
    qp = q_pe.reshape(bsz, nb, Q_BLOCK, N_HEADS, QK_ROPE).transpose(1, 0, 2, 3, 4)
    kpos = jnp.arange(length)

    def block(args):
        i, qlb, qpb = args
        s = (jnp.einsum("bqhc,bkc->bhqk", qlb, ckv, preferred_element_type=f32)
             + jnp.einsum("bqhr,bkr->bhqk", qpb, kr, preferred_element_type=f32)) * SM_SCALE
        qpos = i * Q_BLOCK + jnp.arange(Q_BLOCK)
        s = jnp.where(kpos[None, :] <= qpos[:, None], s, NEG_INF)
        p = jax.nn.softmax(s, axis=-1).astype(ckv.dtype)
        return jnp.einsum("bhqk,bkc->bqhc", p, ckv, preferred_element_type=f32).astype(q_lat.dtype)

    o = lax.map(block, (jnp.arange(nb), ql, qp))
    return o.transpose(1, 0, 2, 3, 4).reshape(bsz, length, N_HEADS, KV_LORA)

def sample_attention(q_lat, q_pe, ckv_new, kr_new, cache_ckv, cache_kr, page_table):
    f32 = jnp.float32
    nb, s = q_lat.shape[:2]

    def scores(kc, kp):
        return (jnp.einsum("bqhc,bkc->bhqk", q_lat, kc, preferred_element_type=f32)
                + jnp.einsum("bqhr,bkr->bhqk", q_pe, kp, preferred_element_type=f32)) * SM_SCALE

    def update(carry, sc, kc):
        m, l, acc = carry
        m_new = jnp.maximum(m, sc.max(axis=-1))
        corr = jnp.exp(m - m_new)
        p = jnp.exp(sc - m_new[..., None])
        l = l * corr + p.sum(axis=-1)
        acc = acc * corr[..., None] + jnp.einsum("bhqk,bkc->bhqc", p, kc.astype(f32))
        return m_new, l, acc

    def page_step(carry, pages):
        kc = cache_ckv[pages]
        kp = cache_kr[pages]
        return update(carry, scores(kc, kp), kc), None

    init = (jnp.full((nb, N_HEADS, s), NEG_INF, f32),
            jnp.zeros((nb, N_HEADS, s), f32),
            jnp.zeros((nb, N_HEADS, s, KV_LORA), f32))
    carry, _ = lax.scan(page_step, init, page_table.T)
    causal = jnp.arange(s)[None, :] <= jnp.arange(s)[:, None]
    sc_new = jnp.where(causal, scores(ckv_new, kr_new), NEG_INF)
    _, l, acc = update(carry, sc_new, ckv_new)
    o = acc / l[..., None]
    return o.transpose(0, 2, 1, 3).astype(q_lat.dtype)

def peer(h, w_q, sub_keys, u_emb, v_emb):
    f32 = jnp.float32
    shape = h.shape
    xt = h.reshape(-1, D_MODEL)
    n_tok = xt.shape[0]
    nb = -(-n_tok // PEER_TOKEN_BLOCK)
    xt = jnp.pad(xt, ((0, nb * PEER_TOKEN_BLOCK - n_tok), (0, 0))).reshape(nb, PEER_TOKEN_BLOCK, D_MODEL)

    def block(xb):
        q = (xb @ w_q).reshape(PEER_TOKEN_BLOCK, PEER_HEADS, 2, PEER_D_KEY // 2)
        s = jnp.einsum("thsd,hsnd->thsn", q, sub_keys, preferred_element_type=f32)
        top_s, top_i = lax.top_k(s, PEER_TOPK)
        cand_s = top_s[:, :, 0, :, None] + top_s[:, :, 1, None, :]
        cand_i = top_i[:, :, 0, :, None] * N_KEYS + top_i[:, :, 1, None, :]
        best_s, best_pos = lax.top_k(cand_s.reshape(PEER_TOKEN_BLOCK, PEER_HEADS, PEER_TOPK * PEER_TOPK), PEER_TOPK)
        idx = jnp.take_along_axis(cand_i.reshape(PEER_TOKEN_BLOCK, PEER_HEADS, PEER_TOPK * PEER_TOPK), best_pos, axis=-1)
        g = jax.nn.softmax(best_s, axis=-1)
        u = u_emb[idx]
        v = v_emb[idx]
        act = jax.nn.gelu(jnp.einsum("td,thkd->thk", xb, u, preferred_element_type=f32))
        return jnp.einsum("thk,thkd->td", (g * act).astype(v.dtype), v)

    y = lax.map(block, xt).reshape(nb * PEER_TOKEN_BLOCK, D_MODEL)[:n_tok]
    return y.reshape(shape).astype(h.dtype)

def run_trunk(x, c, positions, h0_re, h0_im, attend,
              w_mod, b_mod, g_norm,
              ssm_a_re, ssm_a_im, ssm_log_dt, ssm_b_re, ssm_b_im, ssm_c_re, ssm_c_im, ssm_d, ssm_w_glu,
              w_mod_kv, b_mod_kv, g_kv_norm, w_dkv, g_ckv, w_kr, w_ukv,
              w_dq, g_cq, w_uq, w_o,
              peer_w_q, peer_keys, peer_u, peer_v,
              w_mod_final, b_mod_final, g_final):
    ssm_re, ssm_im = [], []
    ckv = kr = None
    for layer in range(DEPTH):
        sh1, sc1, ga1, sh2, sc2, ga2 = split_mod(c, w_mod[layer], b_mod[layer], 6)
        if layer == N_A_LAYERS:
            ckv, kr = shared_kv(x, c, positions, w_mod_kv, b_mod_kv, g_kv_norm, w_dkv, g_ckv, w_kr)
        h = modulate(rmsnorm(x, g_norm[layer, 0]), sh1, sc1)
        if layer < N_A_LAYERS:
            y, hr, hi = s5_mixer(h, h0_re[layer], h0_im[layer], ssm_a_re[layer], ssm_a_im[layer],
                                 ssm_log_dt[layer], ssm_b_re[layer], ssm_b_im[layer],
                                 ssm_c_re[layer], ssm_c_im[layer], ssm_d[layer], ssm_w_glu[layer])
            ssm_re.append(hr)
            ssm_im.append(hi)
        else:
            j = layer - N_A_LAYERS
            q_lat, q_pe = mla_query(h, positions, w_dq[j], g_cq[j], w_uq[j], w_ukv)
            y = mla_out(attend(q_lat, q_pe, ckv, kr), w_ukv, w_o[j])
        x = x + ga1[:, None, :] * y
        h = modulate(rmsnorm(x, g_norm[layer, 1]), sh2, sc2)
        x = x + ga2[:, None, :] * peer(h, peer_w_q[layer], peer_keys[layer], peer_u[layer], peer_v[layer])
    shf, scf = split_mod(c, w_mod_final, b_mod_final, 2)
    y_out = modulate(rmsnorm(x, g_final), shf, scf)
    return y_out, jnp.stack(ssm_re), jnp.stack(ssm_im), ckv, kr

def setup_inputs(seed: int = 0) -> dict:
    key = jax.random.key(seed)
    ks = iter(jax.random.split(key, 64))

    def normal(shape, scale):
        return jax.random.normal(next(ks), shape, jnp.float32) * scale

    n_pages = PAST_LEN // PAGE_SIZE
    used = DEC_BATCH * n_pages
    n_phys = used + max(1, used // 4)
    perm = jax.random.permutation(next(ks), n_phys)
    page_table = perm[:used].reshape(DEC_BATCH, n_pages).astype(jnp.int32)

    ssm_shape = (N_A_LAYERS, SSM_GROUPS, SSM_STATE)
    a_im = jnp.pi * jnp.arange(SSM_STATE, dtype=jnp.float32)
    u01 = jax.random.uniform(next(ks), (N_A_LAYERS, SSM_GROUPS), jnp.float32)
    log_dt = math.log(DT_MIN) + u01 * (math.log(DT_MAX) - math.log(DT_MIN))
    d = D_MODEL
    return {
        "x_prompt": normal((BATCH, SEQ, d), 1.0),
        "x_sample": normal((DEC_BATCH, DEC_SEQ, d), 1.0),
        "state_ssm_re": normal((N_A_LAYERS, DEC_BATCH, SSM_GROUPS, SSM_STATE), 0.5),
        "state_ssm_im": normal((N_A_LAYERS, DEC_BATCH, SSM_GROUPS, SSM_STATE), 0.5),
        "cache_kv_latent": normal((n_phys, PAGE_SIZE, KV_LORA), 1.0),
        "cache_k_rope": normal((n_phys, PAGE_SIZE, QK_ROPE), 1.0),
        "page_table": page_table,
        "c_prompt": normal((BATCH, d), 1.0),
        "c_sample": normal((DEC_BATCH, d), 1.0),
        "w_mod": normal((DEPTH, d, 6 * d), 0.5 * d ** -0.5),
        "b_mod": normal((DEPTH, 6 * d), 0.01),
        "g_norm": 1.0 + normal((DEPTH, 2, d), 0.02),
        "ssm_a_re": -0.5 + normal(ssm_shape, 0.01),
        "ssm_a_im": a_im + normal(ssm_shape, 0.01),
        "ssm_log_dt": log_dt,
        "ssm_b_re": normal((N_A_LAYERS, SSM_GROUPS, SSM_STATE, SSM_GROUP), (2 * SSM_GROUP) ** -0.5),
        "ssm_b_im": normal((N_A_LAYERS, SSM_GROUPS, SSM_STATE, SSM_GROUP), (2 * SSM_GROUP) ** -0.5),
        "ssm_c_re": normal((N_A_LAYERS, SSM_GROUPS, SSM_GROUP, SSM_STATE), (2 * SSM_STATE) ** -0.5),
        "ssm_c_im": normal((N_A_LAYERS, SSM_GROUPS, SSM_GROUP, SSM_STATE), (2 * SSM_STATE) ** -0.5),
        "ssm_d": normal((N_A_LAYERS, d), 1.0),
        "ssm_w_glu": normal((N_A_LAYERS, d, 2 * d), d ** -0.5),
        "w_mod_kv": normal((d, 2 * d), 0.5 * d ** -0.5),
        "b_mod_kv": normal((2 * d,), 0.01),
        "g_kv_norm": 1.0 + normal((d,), 0.02),
        "w_dkv": normal((d, KV_LORA), d ** -0.5),
        "g_ckv": 1.0 + normal((KV_LORA,), 0.02),
        "w_kr": normal((d, QK_ROPE), d ** -0.5),
        "w_ukv": normal((KV_LORA, N_HEADS, QK_NOPE + V_HEAD), KV_LORA ** -0.5),
        "w_dq": normal((N_B_LAYERS, d, Q_LORA), d ** -0.5),
        "g_cq": 1.0 + normal((N_B_LAYERS, Q_LORA), 0.02),
        "w_uq": normal((N_B_LAYERS, Q_LORA, N_HEADS * (QK_NOPE + QK_ROPE)), Q_LORA ** -0.5),
        "w_o": normal((N_B_LAYERS, N_HEADS * V_HEAD, d), (N_HEADS * V_HEAD) ** -0.5),
        "peer_w_q": normal((DEPTH, d, PEER_HEADS * PEER_D_KEY), d ** -0.5),
        "peer_keys": normal((DEPTH, PEER_HEADS, 2, N_KEYS, PEER_D_KEY // 2), (PEER_D_KEY // 2) ** -0.5),
        "peer_u": normal((DEPTH, N_EXPERTS, d), d ** -0.5),
        "peer_v": normal((DEPTH, N_EXPERTS, d), 0.5),
        "w_mod_final": normal((d, 2 * d), 0.5 * d ** -0.5),
        "b_mod_final": normal((2 * d,), 0.01),
        "g_final": 1.0 + normal((d,), 0.02),
    }

def reference(x_prompt, x_sample, state_ssm_re, state_ssm_im, cache_kv_latent, cache_k_rope, page_table,
              c_prompt, c_sample,
              w_mod, b_mod, g_norm,
              ssm_a_re, ssm_a_im, ssm_log_dt, ssm_b_re, ssm_b_im, ssm_c_re, ssm_c_im, ssm_d, ssm_w_glu,
              w_mod_kv, b_mod_kv, g_kv_norm, w_dkv, g_ckv, w_kr, w_ukv,
              w_dq, g_cq, w_uq, w_o,
              peer_w_q, peer_keys, peer_u, peer_v,
              w_mod_final, b_mod_final, g_final):
    weights = (w_mod, b_mod, g_norm,
               ssm_a_re, ssm_a_im, ssm_log_dt, ssm_b_re, ssm_b_im, ssm_c_re, ssm_c_im, ssm_d, ssm_w_glu,
               w_mod_kv, b_mod_kv, g_kv_norm, w_dkv, g_ckv, w_kr, w_ukv,
               w_dq, g_cq, w_uq, w_o,
               peer_w_q, peer_keys, peer_u, peer_v,
               w_mod_final, b_mod_final, g_final)
    pos_p = jnp.arange(x_prompt.shape[1], dtype=jnp.int32)
    h0_p = jnp.zeros((N_A_LAYERS, x_prompt.shape[0], SSM_GROUPS, SSM_STATE), state_ssm_re.dtype)
    y_prompt, ssm_re_p, ssm_im_p, kv_lat_p, k_rope_p = run_trunk(
        x_prompt, c_prompt, pos_p, h0_p, h0_p, prompt_attention, *weights)
    pos_s = PAST_LEN + jnp.arange(x_sample.shape[1], dtype=jnp.int32)
    attend_s = functools.partial(sample_attention, cache_ckv=cache_kv_latent, cache_kr=cache_k_rope,
                                 page_table=page_table)
    y_sample, ssm_re_s, ssm_im_s, kv_lat_s, k_rope_s = run_trunk(
        x_sample, c_sample, pos_s, state_ssm_re, state_ssm_im, attend_s, *weights)
    return (y_prompt, y_sample, ssm_re_p, ssm_im_p, kv_lat_p, k_rope_p, ssm_re_s, ssm_im_s, kv_lat_s, k_rope_s)


_drawn_inputs = setup_inputs


def setup_inputs(seed=0):
    import zlib

    import numpy as np

    out = dict(_drawn_inputs(seed))
    spreads = {}
    factors = {'cache_kv_latent': 4.608,
     'cache_k_rope': 6.315,
     'b_mod': 2.772,
     'g_norm': 3.189,
     'ssm_a_re': 3.74,
     'b_mod_kv': 4.093,
     'g_kv_norm': 2.877,
     'g_ckv': 3.031,
     'g_cq': 8.0,
     'b_mod_final': 4.376,
     'g_final': 2.984}
    for name, (base, spread) in spreads.items():
        noise = np.random.default_rng([zlib.crc32(name.encode()), seed]).standard_normal(out[name].shape)
        drawn = base * np.exp(spread * noise) if base else spread * noise
        out[name] = __import__('jax').numpy.asarray(drawn.astype(out[name].dtype))
    for name, factor in factors.items():
        out[name] = (out[name] * factor).astype(out[name].dtype)
    return out
```

```python
from contextlib import ExitStack

import numpy as np

import concourse.bass as bass
from concourse import mybir

F32 = mybir.dt.float32
I32 = mybir.dt.int32
U32 = mybir.dt.uint32
ALU = mybir.AluOpType
ACT = mybir.ActivationFunctionType
AX = mybir.AxisListType

P = 128
D = 1024
KD = D // P
SEQ = 512
NTILE = SEQ // P
NB = 8
NC9 = 1 + NB
EPS = 1e-6
G = 64
GP = 16
N = 64
TC = 8
CH = SEQ // TC
UC = CH + 2 * NB
RG = 16
PH = 8
N_KEYS = 128
TOPK = 16
HQ = PH * 2 * P
N_EXP = N_KEYS * N_KEYS
RING = 8
NH = 16
NOPE = 64
ROPE = 32
QKD = NOPE + ROPE
VH = 64
QL = 512
KVL = 256
PAST = 2048
SM_SCALE = QKD ** -0.5
NR = G // RG
MB = 512
NMB = 32
MOD_S5 = 6


def program(nc, a):
    with ExitStack() as ctx:
        sem_names = {}

        def sem(name):
            sem_names[name] = ctx.enter_context(nc.semaphore(name))
            return sem_names[name]

        ARENA = 53000
        arena = ctx.enter_context(nc.sbuf_tensor("arena", [P, ARENA], F32))
        psum = ctx.enter_context(nc.psum_tensor("psum", [P, 8, 512], F32))

        def at(off, n, p0=0, p1=P):
            assert off + n <= ARENA, (off, n)
            return arena[p0:p1, off:off + n]

        def scratch(name, shape):
            return nc.dram_tensor(name, shape, F32, kind="Internal").ap()

        mod_dram = scratch("mod_rows", (NC9, NMB * MB))
        hs_dram = scratch("s5_sample_in", (NB, D))
        x1_dram = scratch("x_after_mixer", (SEQ, D))
        x1s_dram = scratch("xs_after_mixer", (NB, D))
        x3_dram = scratch("x_after_attention", (SEQ, D))
        x3s_dram = scratch("xs_after_attention", (NB, D))
        x4_dram = scratch("x_after_layer1", (SEQ, D))
        x4s_dram = scratch("xs_after_layer1", (NB, D))
        x2_dram = scratch("x_after_layer0", (SEQ, D))
        x2s_dram = scratch("xs_after_layer0", (NB, D))

        o = 0
        IDENT = o; o += P
        IOTA = o; o += TOPK
        SEL = o; o += NB
        SILU = o; o += KD * NC9
        ONES = o; o += 16
        STAT = o; o += 64
        MODB = o; o += 2 * MB
        LAMT = o; o += 8 * (G // 2)
        ST0 = o; o += 2 * (G // 2) * NB
        MODO = MODB
        R32 = 32
        FIXED_END = o
        CL = o; o += G * (TC + 1) * GP
        TOEP = o; o += G * P
        BL = o; o += G * P
        MINB = o; o += 2 * RG * P
        U2 = o; o += G * UC
        HX = o; o += G * (CH + NB)
        SJ = o; o += CH * 2 * (G // 2) + NB * 2 * (G // 2)
        H5 = o; o += (TC // 2) * D
        MA = o; o += D
        MS = o; o += D
        assert o <= ARENA, o
        HPX = BL
        PARAM = U2
        NPAR = 3 * G + 4 * G * GP
        assert NPAR <= G * UC
        KSB = HX
        TAB = MINB
        TMP = SJ
        MODW0, MODW1 = TOEP, TOEP + 4096
        MODW2, MODW3 = MINB, HX

        ident = at(IDENT, P)
        silu = at(SILU, KD * NC9).rearrange("p (k r) -> p k r", k=KD)
        ones = at(ONES, 16)
        cl = at(CL, G * (TC + 1) * GP).rearrange("p (g t q) -> p g t q", g=G, t=TC + 1)
        bl = at(BL, G * P).rearrange("p (g s q) -> p g s q", g=G, s=TC)
        toep = at(TOEP, G * P).rearrange("p (g m) -> p g m", g=G)
        u2 = at(U2, G * UC).rearrange("p (g c) -> p g c", g=G)
        hx = at(HX, G * (CH + NB)).rearrange("p (g c) -> p g c", g=G)
        minb = [at(MINB + i * RG * P, RG * P).rearrange("p (g m) -> p g m", g=RG) for i in range(2)]
        ksb = [at(KSB + i * RG * P, RG * P, 0, GP).rearrange("p (g m) -> p g m", g=RG) for i in range(2)]
        sj = at(SJ, CH * G).rearrange("p (c k g) -> p c k g", c=CH, k=2)
        si = at(SJ + CH * G, NB * G).rearrange("p (k g b) -> p k g b", k=2, g=G // 2)
        hpx = at(HPX, (CH + 1) * 3 * (G // 2)).rearrange("p (c m) -> p c m", c=CH + 1)
        h5 = at(H5, (TC // 2) * D).rearrange("p (g j q) -> p g j q", g=G, j=TC // 2)
        x5 = at(U2, (TC // 2) * D).rearrange("p (j d) -> p j d", j=TC // 2)
        z5 = at(SJ, (TC // 2) * D).rearrange("p (j d) -> p j d", j=TC // 2)
        mod_a, mod_s = at(MA, D), at(MS, D)

        par = at(PARAM, NPAR)
        a_re, a_im, log_dt = par[:, 0:G], par[:, G:2 * G], par[:, 2 * G:3 * G]
        b_re, b_im, c_re, c_im = (par[:, 3 * G + i * D:3 * G + (i + 1) * D].rearrange("p (g q) -> p g q", g=G)
                                  for i in range(4))

        t9 = (TC + 1) * G
        pw_re = at(TAB, t9).rearrange("p (t g) -> p t g", t=TC + 1)
        pw_im = at(TAB + t9, t9).rearrange("p (t g) -> p t g", t=TC + 1)
        ca = at(TAB + 2 * t9, t9).rearrange("p (t g) -> p t g", t=TC + 1)
        cb = at(TAB + 3 * t9, t9).rearrange("p (t g) -> p t g", t=TC + 1)
        bb = at(TAB + 4 * t9, t9).rearrange("p (t g) -> p t g", t=TC + 1)
        small = [at(TAB + 5 * t9 + i * G, G) for i in range(16)]
        assert 5 * t9 + 16 * G <= 2 * RG * P
        bbar_re = at(TMP, D).rearrange("p (g q) -> p g q", g=G)
        bbar_im = at(TMP + D, D).rearrange("p (g q) -> p g q", g=G)
        tmp_v = at(TMP + 2 * D, D).rearrange("p (g q) -> p g q", g=G)
        tmp_g = at(TMP + 3 * D, D).rearrange("p (g q) -> p g q", g=G)
        HALF = G // 2
        lamt = at(LAMT, 8 * HALF)
        st0 = at(ST0, 2 * HALF * NB).rearrange("p (k g b) -> p k g b", k=2, g=HALF)
        stat = at(STAT, 64)

        s_in = sem("inputs_loaded")
        s_par = sem("s5_params_loaded")
        s_silu = sem("silu_ready")
        s_const = sem("constants_ready")
        s_modw = [sem(f"mod_weights_loaded{i}") for i in range(2)]
        s_modmm = [sem(f"mod_products_done{i}") for i in range(2)]
        s_modev = [sem(f"mod_rows_copied{i}") for i in range(2)]
        s_dt = sem("dt_ready")
        s_half = sem("half_angle_ready")
        s_sin = sem("half_angle_sines_ready")
        s_modst = [sem(f"mod_rows_stored{i}") for i in range(2)]
        vec = sem("vector_step")
        act_step = sem("scalar_step")
        pool_step = sem("pool_step")
        s_tabs = sem("b_factors_ready")
        s_blp = sem("bl_ready")
        s_clr = sem("cl_ready")
        s_x5 = sem("chunk_rows_loaded")
        s_mods5 = sem("s5_mods_loaded")
        s_sq = sem("row_squares_summed")
        s_ms = sem("row_means_ready")
        s_rt = sem("row_roots_ready")
        s_rld = [sem(f"rows_loaded{i}") for i in range(2)]
        s_rst = [sem(f"rows_stored{i}") for i in range(2)]
        s_h5 = sem("s5_input_ready")
        s_hst = sem("s5_sample_in_stored")
        s_us = sem("sample_columns_loaded")
        s_tz = sem("response_and_chunk_pad_cleared")
        s_toep = [sem(f"response_loaded{r}") for r in range(NR)]
        s_mm = sem("s5_round_products")
        s_evA = sem("s5_round_copied_by_scalar")
        s_evV = sem("s5_round_copied_by_vector")
        s_scan = sem("scan_step")
        s_scd = sem("scan_done")
        s_dld = sem("skip_loaded")
        s_st0 = sem("sample_state_loaded")
        s_hx = sem("states_placed")
        s_gelu = sem("gelu_ready")
        s_wglu = sem("glu_weights_loaded")
        s_zt = sem("glu_transposes")
        s_zc = sem("glu_transposes_copied")
        s_gm = sem("glu_products")
        s_sg = sem("glu_gate_ready")
        s_ga = sem("glu_block_ready")
        s_x1 = sem("mixer_out_ready")
        s_out = sem("outputs_stored")

        NORMS = {"s5": 0, "peer0": 1, "attention": 6, "peer1": 11, "final": 16}

        def norm_no(stage, j):
            return NORMS[stage] + j + 1

        LOADS = ("peer0", "attention", "residual", "peer1", "final")
        STORES = ("peer0", "residual", "peer1", "final")

        def row_slot(stage, j):
            return (j + (stage == "peer1")) % 2

        def row_no(passes, stage, j):
            slot = row_slot(stage, j)
            before = sum(row_slot(q, m) == slot for q in passes[:passes.index(stage)] for m in range(5))
            return 16 * (before + sum(row_slot(stage, m) == slot for m in range(j + 1)))

        ROUNDS = ([("u", r) for r in range(NR)] + [("k", r) for r in range(NR)]
                  + [("m", 0), ("m", 1), ("i", 0), ("m", 2), ("i", 1), ("m", 3), ("i", 2), ("i", 3)]
                  + [("y", r) for r in range(NR)])
        WHO = {"u": "A", "k": "A", "m": "A", "i": "V", "y": "V"}
        round_no = {key: n for n, key in enumerate(ROUNDS)}
        copied = {}
        for who in "AV":
            mine = [key for key in ROUNDS if WHO[key[0]] == who]
            for n, key in enumerate(mine):
                copied[key] = (who, n + 1)

        def wait_copied(eng, key):
            who, n = copied[key]
            eng.wait_ge(s_evA if who == "A" else s_evV, n)

        def half(n):
            return psum[:, 4 * (n % 2):4 * (n % 2) + 4, :]

        def pairs(eng, first, last, pair):
            if first == 0:
                for b in range(2):
                    pair(0, b, True)
            with eng.Fori(first // 2 + (first == 0), last // 2) as i:
                for b in range(2):
                    pair(i, b)

        hpv = hpx[:, 0:CH, :].rearrange("p c (k g) -> p k g c", k=3)
        hxv = hx[:, :, 0:CH].rearrange("p (g two) c -> p two g c", two=2)
        zt = [at(U2 + i * D, D).rearrange("p (k t) -> p k t", k=KD) for i in range(2)]
        gate = [at(U2 + 2 * D + i * 256, 256) for i in range(2)]
        glu_t = [at(U2 + 2 * D + 512 + i * D, D) for i in range(2)]
        scan_tmp = at(MA, 4 * HALF)
        sj_tmp = at(MA + 4 * HALF, HALF * NB).rearrange("p (g b) -> p g b", g=HALF)

        o = FIXED_END
        WQ = o; o += KD * HQ
        KEYS = o; o += 2 * PH * P
        RINGP = o; o += RING * D
        XT = o; o += 2 * D
        HT = o; o += 2 * D
        HTR = o; o += D
        QT = o; o += 2 * PH * P
        PMOD = o; o += 6 * D
        SSB = o; o += 2 * PH * P
        TOPV = o; o += 64
        TOPI = o; o += 64
        CAND = o; o += 256
        ONEH = o; o += 512
        BV = o; o += PH * TOPK
        BP = o; o += 32
        AB = o; o += 64
        IDXP = o; o += 2 * P
        PG = o; o += 2 * P
        DOTS = o; o += 2 * P
        DIAG = o; o += RING * P
        YACC = o; o += D
        PTMP = o; o += 2 * D
        IX8 = o; o += 2 * RING
        IXS = o; o += RING
        GS = o; o += RING
        assert o <= ARENA, o
        PEER_END = o

        def rows_of(t):
            return P if t % 5 < 4 else NB

        wq = at(WQ, KD * HQ).rearrange("p (k n) -> p k n", k=KD)
        keys = at(KEYS, 2 * PH * P).rearrange("p (h n) -> p h n", h=2 * PH)
        ring = [at(RINGP + r * D, D) for r in range(RING)]
        qt = at(QT, 2 * PH * P).rearrange("p (h t) -> p h t", h=2 * PH)
        htr = at(HTR, D).rearrange("p (k t) -> p k t", k=KD)
        ssb = at(SSB, 2 * PH * P).rearrange("p (h n) -> p h n", h=2 * PH)
        diag = at(DIAG, RING * P).rearrange("p (r n) -> p r n", r=RING)
        iota16, sel8 = at(IOTA, TOPK), at(SEL, NB)
        zrow = at(MODB, 512, 64, 65)
        idx_dram = nc.dram_tensor("sample_idx", (NB, P), I32, kind="Internal").ap()
        gw_dram = scratch("sample_gates", (NB, P))
        ph_dram = scratch("peer_sample_in", (NB, D))

        s_pw = sem("peer_weights_loaded")
        s_pmod = sem("peer_mods_loaded")
        s_pmr = sem("peer_mods_ready")
        s_ph = sem("peer_input_ready")
        s_pt = sem("peer_input_transposed")
        s_ptc = sem("peer_transposes_copied")
        s_pq = sem("query_products")
        s_pqc = sem("queries_copied")
        s_ps = sem("key_scores")
        s_psc = sem("key_scores_copied")
        s_idx = sem("head_experts_ready")
        s_bv = sem("expert_scores_shifted")
        s_ex = sem("expert_exps_ready")
        s_g = sem("gates_ready")
        s_dots = sem("expert_dots_ready")
        s_act = sem("expert_acts_ready")
        s_w = sem("expert_weights_ready")
        s_go = sem("gather_slot_found_free")
        s_ix8 = sem("group_indices_copied")
        landed = [sem(f"expert_row_landed{r}") for r in range(RING)]
        freed = [sem(f"expert_row_used{r}") for r in range(RING)]
        s_dg = sem("weight_diagonals_ready")
        s_yp = sem("peer_sum_closed")
        s_yr = sem("peer_sum_read")
        s_xn = sem("peer_out_ready")
        s_sdr = sem("sample_rows_stored")
        s_sld = sem("sample_columns_spread")
        s_shs = sem("sample_input_stored")
        s_shb = sem("sample_input_spread")
        s_z = sem("zero_row_ready")

        def group_base(t, phase):
            layer, b = divmod(t, 5)
            per = 2 * NTILE * P // RING + 2
            return layer * per + (b * 2 + phase) * (P // RING) if b < 4 else \
                layer * per + 2 * NTILE * P // RING + phase

        V_DVE = (1, 4, 7)
        V_PE = tuple(r for r in range(RING) if r not in V_DVE)

        def diag_base(t):
            layer, b = divmod(t, 5)
            return (layer * 4 + b) * (P // RING) * len(V_PE) + layer * RING

        def ix8_base(t, phase):
            layer, b = divmod(t, 5)
            return ((layer * 4 + b) * 2 + phase) * (P // RING)

        KVC = KVL + ROPE
        o = FIXED_END
        WDKV = o; o += KD * KVC
        WDQ = o; o += KD * QL
        WUQ = o; o += (QL // P) * NH * QKD
        MMOD = o; o += 4 * D
        KT = WDKV
        WO = KT + NH * SEQ
        assert WO + KD * D <= o
        QTM = o; o += NH * SEQ
        VV = o; o += NTILE * NH * VH
        WKT = VV
        WK = o; o += 2 * NH * NOPE
        WV = o; o += 2 * NH * VH
        CKVT = o; o += 2 * (SEQ + NB)
        KRT = o; o += SEQ + NB
        KVR = o; o += 2 * KVC
        MX = o; o += 2 * D
        MH = o; o += 2 * D
        MHT = o; o += 2 * D
        MCQ = o; o += QL
        MCQT = o; o += QL
        MQ = o; o += NH * QKD
        SC1 = MCQ
        CSN = o; o += 5 * ROPE
        MASK = o; o += P
        SMASK = o; o += NB * NB
        SUB = o; o += 1 + NB
        GCKV = o; o += KVL
        GCQ = o; o += QL
        PP = o; o += 2 * SEQ
        PTT = o; o += 2 * SEQ
        OO = o; o += D
        OTT = o; o += D
        QTS = o; o += NH * NB
        QLT = o; o += 2 * NB * NH
        SUMS = o; o += 32
        PTS = o; o += 17 * NH
        OL = o; o += KVL
        OLT = o; o += 2 * NH * NB
        RT = o; o += 1
        assert o <= ARENA, o
        ROWK = KVL * 16
        ROWR = ROPE * 16
        CK = [QTM, QTM + ROWK + ROWR]
        SC0 = QTM + 2 * (ROWK + ROWR)
        NKEY = PAST + NB
        assert SC0 + NKEY <= WK and NKEY <= 2 * QL + NH * QKD
        SCS = [SC0, SC1]
        KTS = KT
        KRTS = KT + 2 * PAST
        assert KRTS + PAST <= WO
        wdkv = at(WDKV, KD * KVC).rearrange("p (k n) -> p k n", k=KD)
        wdq = at(WDQ, KD * QL).rearrange("p (k n) -> p k n", k=KD)
        wuq = at(WUQ, (QL // P) * NH * QKD).rearrange("p (k n) -> p k n", k=QL // P)
        kt_ = at(KT, NH * SEQ).rearrange("p (h t) -> p h t", h=NH)
        wo = at(WO, KD * D).rearrange("p (k n) -> p k n", k=KD)
        qtm = at(QTM, NH * SEQ).rearrange("p (h t) -> p h t", h=NH)
        qts = at(QTS, NH * NB).rearrange("p (h b) -> p h b", h=NH)
        qlt = at(QLT, 2 * NB * NH).rearrange("p (c b h) -> p c b h", c=2, b=NB)
        vv = at(VV, NTILE * NH * VH).rearrange("p (i n) -> p i n", i=NTILE)
        wkt = at(WKT, NH * KVL, 0, NOPE).rearrange("p (h c) -> p h c", h=NH)
        wk = at(WK, 2 * NH * NOPE).rearrange("p (c h n) -> p c h n", c=2, h=NH)
        wv = at(WV, 2 * NH * VH).rearrange("p (c n) -> p c n", c=2)
        ckvt = at(CKVT, 2 * (SEQ + NB)).rearrange("p (c t) -> p c t", c=2)
        csn = at(CSN, 5 * ROPE).rearrange("p (i k m) -> p i k m", i=5, k=2)
        kts = at(KTS, 2 * PAST).rearrange("p (c t) -> p c t", c=2)
        krts = at(KRTS, PAST)
        pts = at(PTS, 17 * NH).rearrange("p (r h) -> p r h", r=17)
        olt = at(OLT, 2 * NH * NB).rearrange("p (c h b) -> p c h b", c=2, h=NH)
        mht = [at(MHT + i * D, D).rearrange("p (k t) -> p k t", k=KD) for i in range(2)]

        s_mw = sem("attention_weights_loaded")
        s_mm1 = sem("attention_mods_loaded")
        s_mmr = sem("attention_mods_ready")
        s_hin = sem("attention_inputs_ready")
        s_tx = sem("attention_inputs_transposed")
        s_txc = sem("attention_input_transposes_copied")
        s_pr = sem("latent_products")
        s_tl = sem("latents_transposed")
        s_tlc = sem("latent_transposes_copied")
        s_lsq = sem("latent_squares_ready")
        s_lmn = sem("latent_means_ready")
        s_lrt = sem("latent_roots_ready")
        s_kvr = sem("latents_ready")
        s_kvs = [sem(f"latents_stored{i}") for i in range(2)]
        s_q = sem("head_query_products")
        s_qc = sem("head_queries_copied")
        s_qr = sem("head_queries_rotated")
        s_tqh = sem("head_queries_transposed")
        s_tqhc = sem("head_transposes_copied")
        s_ql = sem("sample_latent_queries")
        s_qlc = sem("sample_latent_queries_copied")
        s_ktp = sem("head_key_products")
        s_kta = sem("head_keys_copied_by_scalar")
        s_ktv = sem("head_keys_copied_by_vector")
        s_ktr = sem("rotary_keys_spread")
        s_vp = sem("value_products")
        s_vc = sem("values_copied")
        s_S = sem("scores_ready")
        s_nm = sem("score_maximum_ready")
        s_e2 = sem("probabilities_ready")
        s_T = sem("probabilities_transposed")
        s_Tc = sem("probability_transposes_copied")
        s_pv = sem("head_outputs")
        s_on = sem("head_outputs_scaled")
        s_ot = sem("outputs_transposed")
        s_otc = sem("output_transposes_copied")
        s_yy = sem("output_products")
        s_x3 = sem("attention_out_ready")
        s_pix = sem("page_rows_ready")
        s_ck = [sem(f"cache_rows_landed{i}") for i in range(2)]
        s_ct = sem("cache_rows_transposed")
        s_cta = sem("cache_transposes_copied_by_scalar")
        s_ctv = sem("cache_transposes_copied_by_vector")
        s_cs = sem("sample_scores")
        s_csc = sem("sample_scores_copied")
        s_cnm = sem("sample_maximum_ready")
        s_ce = sem("sample_probabilities_ready")
        s_cT = sem("sample_probabilities_transposed")
        s_cTc = sem("sample_transposes_copied")
        s_cpv = sem("sample_latent_outputs")
        s_col = sem("sample_latent_outputs_scaled")
        s_cot = sem("sample_outputs_transposed")
        s_coc = sem("sample_output_transposes_copied")
        s_os = sem("sample_head_outputs")

        def rows5(j):
            return P if j < 4 else NB

        FMOD = FIXED_END
        FG = FMOD + 4 * D
        FX = FG + D
        FSQ = FX + 2 * D

        block = ctx.enter_context(nc.Block())

        @block.sync
        def _(sp):
            sp.dma_start(at(SILU, KD * NC9), a["c_t"]).then_inc(s_in, 16)
            sp.dma_start(at(IDENT, P + TOPK + NB), a["consts"]).then_inc(s_in, 16)
            sp.dma_start(par, a["s5_par"]).then_inc(s_par, 16)

            def mod_loads(first, last, slots):
                def pair(i, b, fresh=False):
                    if not fresh:
                        sp.wait_ge(s_modmm[b], i)
                    sp.dma_start(at(slots[b], KD * MB),
                                 a["w_mod"][bass.ds(2 * i + b, 1), :, :].rearrange("o p n -> (o p) n")
                                 ).then_inc(s_modw[b], 16)
                    sp.dma_start(at(MODB + b * MB, MB, 0, 1), a["b_mod"][bass.ds(2 * i + b, 1), :]
                                 ).then_inc(s_modw[b], 16)

                pairs(sp, first, last, pair)

            mod_loads(0, MOD_S5, (MODW0, MODW1))
            x5v = a["x_prompt"].rearrange("(c s j) d -> s c (j d)", s=2, j=TC // 2)
            sp.dma_start(at(ST0, 2 * HALF * NB), a["state_g"]).then_inc(s_x5, 16)
            for b in range(2):
                sp.wait_ge(s_modst[b], 16 * (MOD_S5 // 2))
            sp.dma_start(mod_s, mod_dram[0:1, 0:D].partition_broadcast(P)).then_inc(s_mods5, 16)
            sp.dma_start(mod_a, mod_dram[0:1, D:2 * D].partition_broadcast(P)).then_inc(s_mods5, 16)
            sp.wait_ge(s_clr, 1)
            sp.wait_ge(s_blp, 1)
            for s in range(2):
                sp.dma_start(at(U2, 4 * D, 64 * s, 64 * s + 64), x5v[s]).then_inc(s_x5, 16)
            sp.dma_start(at(TMP, D), a["g_norm"][0:1, :].partition_broadcast(P)).then_inc(s_mods5, 16)
            sp.dma_start(at(TMP + D, D, 0, NB), a["x_sample"]).then_inc(s_mods5, 16)
            sp.dma_start(at(TMP + 2 * D, D, 0, NB), mod_dram[1:NC9, 0:D]).then_inc(s_mods5, 16)
            sp.dma_start(at(TMP + 3 * D, D, 0, NB), mod_dram[1:NC9, D:2 * D]).then_inc(s_mods5, 16)
            sp.wait_ge(s_h5, 2)
            sp.dma_start(hs_dram, at(TMP + D, D, 0, NB)).then_inc(s_hst, 16)
            sp.dma_start(mod_a, a["ssm_d"].partition_broadcast(P)).then_inc(s_dld, 16)
            sp.wait_ge(s_hst, 16)
            sp.wait_ge(s_tz, 2)
            hsv = hs_dram.rearrange("b (g p) -> p g b", p=GP)
            for b in range(NB):
                for k, rows in enumerate((slice(0, GP), slice(P - GP, P))):
                    sp.dma_start(u2[rows, :, CH + k * NB + b], hsv[:, :, b],
                                 allow_slow_non_contiguous=True).then_inc(s_us, 16)
            sp.wait_ge(s_tz, 1)
            for r in range(NR):
                wait_copied(sp, ("k", r))
                for s in range(TC):
                    sp.dma_start(toep[GP * s:GP * (s + 1), RG * r:RG * (r + 1), GP * s:P],
                                 ksb[r % 2][:, :, 0:P - GP * s]).then_inc(s_toep[r], 16)
            wait_copied(sp, ("i", NR - 1))
            for r in range(NR):
                sp.wait_ge(s_toep[r], 16 * TC)
            mod_loads(MOD_S5, 12, (MODW2, MODW3))
            for b in range(2):
                sp.wait_ge(s_modmm[b], 6)
            sp.dma_start(hx[:, :, CH:CH + NB], a["state_x"]).then_inc(s_st0, 16)
            sp.wait_ge(s_scd, 1)
            sp.dma_start(a["out_ssm_p"], hpx[:, CH, 0:2 * HALF]).then_inc(s_out, 16)
            sp.wait_ge(s_scd, 2)
            sp.dma_start(a["out_ssm_s"], at(SJ + CH * G, NB * G)).then_inc(s_out, 16)
            wait_copied(sp, ("y", NR - 1))
            sp.dma_start(at(CL, KD * 2 * D), a["w_glu"]).then_inc(s_wglu, 16)
            sp.wait_ge(s_out, 32)
            for s in range(2):
                sp.dma_start(at(BL, 4 * D, 64 * s, 64 * s + 64), x5v[s]).then_inc(s_x5, 16)
            sp.dma_start(at(BL + 4 * D, D, 0, NB), a["x_sample"]).then_inc(s_x5, 16)
            sp.dma_start(at(BL + 5 * D, D, 0, NB), mod_dram[1:NC9, 2 * D:3 * D]).then_inc(s_x5, 16)
            sp.dma_start(mod_a, mod_dram[0:1, 2 * D:3 * D].partition_broadcast(P)).then_inc(s_x5, 16)
            x1v = x1_dram.rearrange("(c s j) d -> s j c d", s=2, j=TC // 2)
            for j in range(TC // 2):
                sp.wait_ge(s_x1, j + 1)
                for s in range(2):
                    sp.dma_start(x1v[s, j], at(BL + j * D, D, 64 * s, 64 * s + 64)).then_inc(s_out, 16)
            sp.wait_ge(s_x1, 5)
            sp.dma_start(x1s_dram, at(BL + 4 * D, D, 0, NB)).then_inc(s_out, 16)
            mod_loads(12, NMB, (MODW2, MODW3))
            sp.wait_ge(s_out, 32 + 16 * 9)
            for b in range(2):
                sp.wait_ge(s_modst[b], 16 * (NMB // 2))

            def peer_loads(layer):
                sp.dma_start(at(WQ, KD * HQ), a["peer_wq"][layer]).then_inc(s_pw, 16)
                sp.dma_start(at(KEYS, 2 * PH * P), a["peer_keys"][layer]).then_inc(s_pw, 16)
                c0 = (layer * 6 + 3) * D
                sp.dma_start(at(PMOD, 3 * D), mod_dram[0:1, c0:c0 + 3 * D].partition_broadcast(P)
                             ).then_inc(s_pmod, 16)
                sp.dma_start(at(PMOD + 3 * D, 3 * D, 0, NB), mod_dram[1:NC9, c0:c0 + 3 * D]).then_inc(s_pmod, 16)
                sp.dma_start(at(PTMP, D), a["g_norm"][2 * layer + 1:2 * layer + 2, :].partition_broadcast(P)
                             ).then_inc(s_pmod, 16)

            def peer_tiles(layer, x_in, xs_in, x_out, xs_out):
                stage = f"peer{layer}"

                def load(t):
                    b = t % 5
                    if t % 5 >= 2:
                        sp.wait_ge(s_rst[t % 2], row_no(STORES, stage, b - 2))
                    src = x_in[P * b:P * (b + 1)] if b < 4 else xs_in
                    sp.dma_start(at(XT + (t % 2) * D, D, 0, rows_of(t)), src).then_inc(s_rld[t % 2], 16)

                def store(t):
                    b = t % 5
                    sp.wait_ge(s_xn, t + 1)
                    dst = x_out[P * b:P * (b + 1)] if b < 4 else xs_out
                    sp.dma_start(dst, at(XT + (t % 2) * D, D, 0, rows_of(t))).then_inc(s_rst[t % 2], 16)

                t0 = 5 * layer
                load(t0)
                load(t0 + 1)
                for b in range(5):
                    t = t0 + b
                    if b == 3:
                        ts_ = t0 + 4
                        sp.wait_ge(s_ph, ts_ + 1)
                        sp.dma_start(ph_dram, at(HT + (ts_ % 2) * D, D, 0, NB)).then_inc(s_shs, 16)
                        sp.wait_ge(s_shs, 16 * (layer + 1))
                        sp.wait_ge(s_dots, t0 + 4)
                        for q in range(NB):
                            sp.dma_start(at(HT + ((ts_ + 1) % 2) * D, D, 16 * q, 16 * q + 16),
                                         ph_dram[q:q + 1, :].partition_broadcast(16)).then_inc(s_shb, 16)
                        sp.wait_ge(s_idx, 8 * (ts_ + 1))
                        sp.dma_start(idx_dram, at(IDXP + (ts_ % 2) * P, P, 0, NB).bitcast(I32)).then_inc(s_sdr, 16)
                        sp.wait_ge(s_g, ts_ + 1)
                        sp.dma_start(gw_dram, at(PG + (ts_ % 2) * P, P, 0, NB)).then_inc(s_sdr, 16)
                        sp.wait_ge(s_sdr, 32 * (layer + 1))
                        sp.dma_start(at(IXS, RING).bitcast(I32),
                                     idx_dram.rearrange("b (s c) -> (b s) c", c=RING)).then_inc(s_sld, 16)
                        sp.dma_start(at(GS, RING), gw_dram.rearrange("b (s c) -> (b s) c", c=RING)
                                     ).then_inc(s_sld, 16)
                    store(t)
                    if b + 2 < 5:
                        load(t + 2)
                for j in (3, 4):
                    sp.wait_ge(s_rst[row_slot(stage, j)], row_no(STORES, stage, j))

            def attention_sync():
                for dst, src in ((WDKV, "w_dkv"), (WDQ, "w_dq"), (WUQ, "w_uq"), (WK, "w_k"), (WV, "w_v"),
                                 (CSN, "rope_mask")):
                    n_ = a[src].shape[1]
                    sp.dma_start(at(dst, n_), a[src]).then_inc(s_mw, 16)
                sp.dma_start(at(WKT, NH * KVL, 0, NOPE), a["w_kt"]).then_inc(s_mw, 16)
                sp.dma_start(at(SUB + 1, NB).bitcast(I32), a["pages"]).then_inc(s_mw, 16)
                sp.dma_start(at(GCKV, KVL), a["g_ckv"].partition_broadcast(P)).then_inc(s_mw, 16)
                sp.dma_start(at(GCQ, QL), a["g_cq"].partition_broadcast(P)).then_inc(s_mw, 16)

                def mods(rows, first):
                    r = slice(0, 1) if rows == P else slice(1, NC9)
                    for m, c0 in ((0, 12 * D), (2, 6 * D)):
                        src = mod_dram[r, c0:c0 + 2 * D]
                        sp.dma_start(at(MMOD + m * D, 2 * D, 0, rows), src.partition_broadcast(P) if rows == P
                                     else src).then_inc(s_mm1, 16)
                    sp.dma_start(at(MHT, D, 0, rows), a["g_kv_norm"].partition_broadcast(rows)).then_inc(s_mm1, 16)
                    sp.dma_start(at(MHT + D, D, 0, rows), a["g_norm"][2:3, :].partition_broadcast(rows)
                                 ).then_inc(s_mm1, 16)

                def rows_in(j):
                    src = x2_dram[P * j:P * (j + 1)] if j < 4 else x2s_dram
                    sp.dma_start(at(MX + (j % 2) * D, D, 0, rows5(j)), src).then_inc(s_rld[j % 2], 16)

                mods(P, True)
                rows_in(0)
                rows_in(1)
                for j in range(5):
                    if j == 3:
                        sp.wait_ge(s_hin, 8)
                        sp.wait_ge(s_pr, 8)
                        mods(NB, False)
                    sp.wait_ge(s_kvr, 2 * j + 1)
                    kvr = at(KVR + (j % 2) * KVC, KVC, 0, rows5(j))
                    kd, rd = ((a["out_kv_p"][P * j:P * (j + 1)], a["out_kr_p"][P * j:P * (j + 1)]) if j < 4
                              else (a["out_kv_s"], a["out_kr_s"]))
                    sp.dma_start(kd, kvr[:, 0:KVL]).then_inc(s_kvs[j % 2], 16)
                    sp.dma_start(rd, kvr[:, KVL:KVC]).then_inc(s_kvs[j % 2], 16)
                    if j + 2 < 5:
                        sp.wait_ge(s_hin, 2 * (j + 1))
                        rows_in(j + 2)
                sp.wait_ge(s_tqh, 5)
                sp.wait_ge(s_tlc, 10)
                sp.dma_start(at(WO, KD * D), a["w_o"]).then_inc(s_mw, 16)
                sp.dma_start(at(MH, D), mod_dram[0:1, 8 * D:9 * D].partition_broadcast(P)).then_inc(s_mw, 16)
                sp.dma_start(at(MH + D, D, 0, NB), mod_dram[1:NC9, 8 * D:9 * D]).then_inc(s_mw, 16)
                for j in range(5):
                    if j == 2 or j == 3 or j == 4:
                        sp.wait_ge(s_rst[j % 2], row_no(STORES, "residual", j - 2))
                    else:
                        sp.wait_ge(s_hin, 10)
                    src = x2_dram[P * j:P * (j + 1)] if j < 4 else x2s_dram
                    sp.dma_start(at(MX + (j % 2) * D, D, 0, rows5(j)), src).then_inc(s_rld[j % 2], 16)
                    if j >= 1:
                        attention_store(j - 1)
                attention_store(4)
                for i in range(2):
                    sp.wait_ge(s_rst[i], row_no(STORES, "residual", 4 - i))
                    sp.wait_ge(s_kvs[i], 32 * (3 - i))

            def attention_store(j):
                sp.wait_ge(s_x3, j + 1)
                dst = x3_dram[P * j:P * (j + 1)] if j < 4 else x3s_dram
                sp.dma_start(dst, at(MX + (j % 2) * D, D, 0, rows5(j))).then_inc(s_rst[j % 2], 16)

            def final_sync():
                sp.dma_start(at(FMOD, 2 * D), mod_dram[0:1, 14 * D:16 * D].partition_broadcast(P)
                             ).then_inc(s_mm1, 16)
                sp.dma_start(at(FMOD + 2 * D, 2 * D, 0, NB), mod_dram[1:NC9, 14 * D:16 * D]).then_inc(s_mm1, 16)
                sp.dma_start(at(FG, D), a["g_final"].partition_broadcast(P)).then_inc(s_mm1, 16)
                for j in range(5):
                    if j >= 2:
                        sp.wait_ge(s_rst[j % 2], row_no(STORES, "final", j - 2))
                    src = x4_dram[P * j:P * (j + 1)] if j < 4 else x4s_dram
                    sp.dma_start(at(FX + (j % 2) * D, D, 0, rows5(j)), src).then_inc(s_rld[j % 2], 16)
                    if j >= 1:
                        final_store(j - 1)
                final_store(4)
                for i in range(2):
                    sp.wait_ge(s_rst[i], row_no(STORES, "final", 4 - i))

            def final_store(j):
                sp.wait_ge(s_xn, 10 + j + 1)
                dst = a["out_y_p"][P * j:P * (j + 1)] if j < 4 else a["out_y_s"]
                sp.dma_start(dst, at(FX + (j % 2) * D, D, 0, rows5(j))).then_inc(s_rst[j % 2], 16)

            peer_loads(0)
            peer_tiles(0, x1_dram, x1s_dram, x2_dram, x2s_dram)
            attention_sync()
            peer_loads(1)
            peer_tiles(1, x3_dram, x3s_dram, x4_dram, x4s_dram)
            final_sync()
            for b in range(2):
                sp.wait_ge(s_modst[b], 16 * (NMB // 2))

        @block.gpsimd
        def _(pool):
            n = [0]

            def link(ins):
                n[0] += 1
                ins.then_inc(pool_step, 1)
                pool.wait_ge(pool_step, n[0])

            pool.memset(ones, 1.0).then_inc(s_const, 1)
            pool.wait_ge(s_tabs, 1)
            shape = [P, G, GP]
            for s in range(TC):
                k = TC - 1 - s
                link(pool.tensor_tensor(bl[:, :, s, :], bbar_re, ca[:, k, :].unsqueeze(2).to_broadcast(shape),
                                        ALU.mult))
                link(pool.tensor_tensor(tmp_g, bbar_im, bb[:, k, :].unsqueeze(2).to_broadcast(shape), ALU.mult))
                ins = pool.tensor_tensor(bl[:, :, s, :], bl[:, :, s, :], tmp_g, ALU.add)
                if s < TC - 1:
                    link(ins)
                else:
                    ins.then_inc(s_blp, 1)
            for b in range(2):
                pool.wait_ge(s_modmm[b], MOD_S5 // 2)
            pool.memset(at(TOEP, G * P), 0.0).then_inc(s_tz, 1)
            pool.wait_ge(s_clr, 1)
            pool.wait_ge(s_blp, 1)
            pool.wait_ge(s_h5, 1)
            pool.memset(u2[:, :, CH:UC], 0.0).then_inc(s_tz, 1)

            def gather(layer, phase, r, ix):
                table = a["peer_" + "uv"[phase] + str(layer)]
                pool.indirect_dma_start(ring[r], None, table, bass.IndirectOffsetOnAxis(ap=ix, axis=0)).then_inc(landed[r], 16)

            def head(t, phase, base, idx, i, fresh=False):
                pool.wait_ge(s_idx, 8 * t + i + 1)
                for g in range(2):
                    used = not (fresh and g == 0)
                    ix8 = at(IX8 + g * RING, RING).bitcast(I32)
                    if used:
                        pool.wait_ge(freed[0], 2 * i + (base + g))
                    pool.tensor_copy(ix8, idx[:, bass.ds(i * TOPK + g * RING, RING)]).then_inc(s_ix8, 1)
                    for r in range(RING):
                        if r == 0:
                            pool.wait_ge(s_ix8, 2 * i + (ix8_base(t, phase) + g + 1))
                            pool.sem_inc(s_go, 1)
                        elif used:
                            pool.wait_ge(freed[r], 2 * i + (base + g))
                            pool.sem_inc(s_go, 1)
                        gather(t // 5, phase, r, ix8[:, r:r + 1])

            def peer_gathers(layer):
                for b in range(5):
                    t = 5 * layer + b
                    for phase in range(2):
                        base = group_base(t, phase)
                        if b < 4:
                            assert base % 2 == 0
                            idx = at(IDXP + (t % 2) * P, P).bitcast(I32)
                            first = t == 0 and phase == 0
                            if first:
                                head(t, phase, base, idx, 0, True)
                            with pool.Fori(1 if first else 0, PH) as i:
                                head(t, phase, base, idx, i)
                        else:
                            ixs = at(IXS, RING).bitcast(I32)
                            pool.wait_ge(s_sld, 32 * (layer + 1))
                            for r in range(RING):
                                pool.wait_ge(freed[r], base)
                                gather(layer, phase, r, ixs[:, r:r + 1])

            def attention_pool():
                pool.wait_ge(s_tqh, 5)
                pool.wait_ge(s_tlc, 10)
                pool.tensor_copy(kt_[NOPE:QKD], at(KRT, SEQ, NOPE, QKD).unsqueeze(1).to_broadcast([ROPE, NH, SEQ])
                                 ).then_inc(s_ktr, 1)
                rows = at(SUB + 1, NB).bitcast(I32)
                pool.wait_ge(s_pix, 1)
                pool.wait_ge(s_pv, NTILE * NH)
                for b in range(NB):
                    if b >= 2:
                        pool.wait_ge(s_cpv, b - 1)
                        pool.wait_ge(s_ct, 4 * (b - 1))
                    ck = CK[b % 2]
                    pool.indirect_dma_start(at(ck, ROWK), None, a["cache_kv"],
                                            bass.IndirectOffsetOnAxis(ap=rows[:, b:b + 1], axis=0)
                                            ).then_inc(s_ck[b % 2], 16)
                    pool.indirect_dma_start(at(ck + ROWK, ROWR), None, a["cache_kr"],
                                            bass.IndirectOffsetOnAxis(ap=rows[:, b:b + 1], axis=0)
                                            ).then_inc(s_ck[b % 2], 16)

            peer_gathers(0)
            attention_pool()
            peer_gathers(1)
            pool.wait_ge(s_go, 2 * 2 * NTILE * P - (RING - 1))

        @block.scalar
        def _(act):
            n = [0]

            def link(ins):
                n[0] += 1
                ins.then_inc(act_step, 1)
                act.wait_ge(act_step, n[0])

            act.wait_ge(s_in, 32)
            act.activation(at(U2 + NPAR, KD * NC9), at(SILU, KD * NC9), ACT.Exp, scale=-1.0).then_inc(s_silu, 1)
            act.wait_ge(s_par, 16)
            act.activation(small[0], log_dt, ACT.Exp).then_inc(s_dt, 1)
            act.wait_ge(s_half, 1)
            act.activation(small[5], small[4], ACT.Sin).then_inc(s_sin, 1)
            link(act.activation(small[6], small[4], ACT.Abs))
            act.activation(small[7], small[6], ACT.Sin, scale=-1.0, bias=stat[:, 60:61]).then_inc(s_sin, 1)

            def mod_evac(first, last):
                def pair(i, b, fresh=False):
                    if not fresh:
                        act.wait_ge(s_modst[b], 16 * i)
                    act.wait_ge(s_modmm[b], i + 1)
                    act.activation(at(MODO + b * MB, MB, R32, R32 + NC9), psum[0:NC9, 6 + b, :],
                                   ACT.Copy).then_inc(s_modev[b], 1)
                    act.wait_ge(s_modev[b], i + 1)
                    act.dma_start(mod_dram[:, bass.ds((2 * i + b) * MB, MB)],
                                  at(MODO + b * MB, MB, R32, R32 + NC9)).then_inc(s_modst[b], 16)

                pairs(act, first, last, pair)

            mod_evac(0, MOD_S5)
            act.wait_ge(s_x5, 48)
            act.wait_ge(s_clr, 1)
            act.wait_ge(s_blp, 1)
            for j in range(TC // 2):
                link(act.activation(at(MINB, D), x5[:, j, :], ACT.Square, accum_out=stat[:, j:j + 1]))
            act.wait_ge(s_mods5, 16 * 6)
            act.activation(at(MINB, D, 0, NB), at(TMP + D, D, 0, NB), ACT.Square,
                           accum_out=stat[0:NB, 4:5]).then_inc(s_sq, 1)
            act.wait_ge(s_ms, 1)
            act.activation(stat[:, 8:13], stat[:, 8:13], ACT.Sqrt).then_inc(s_rt, 1)

            for key in [k for k in ROUNDS if WHO[k[0]] == "A"]:
                kind, r = key
                no = round_no[key]
                act.wait_ge(s_mm, no + 1)
                ps = half(no)
                if kind == "u":
                    for s in range(2):
                        ins = act.activation(
                            u2[64 * s:64 * s + 64, RG * r:RG * (r + 1), 0:CH].rearrange(
                                "p (b g) c -> p b g c", b=4),
                            ps[0:64].rearrange("p b (g c) -> p b g c", g=4)[:, :, :, 64 * s:64 * s + 64], ACT.Copy)
                        if s == 0:
                            link(ins)
                elif kind == "k":
                    if r >= 2:
                        act.wait_ge(s_toep[r - 2], 16 * TC)
                    ins = act.activation(ksb[r % 2].rearrange("p (b g) m -> p b (g m)", b=4), ps[0:GP], ACT.Copy)
                else:
                    if r >= 2:
                        act.wait_ge(s_mm, round_no[("i", r - 2)] + 1)
                    ins = act.activation(minb[r % 2].rearrange("p (b g) m -> p b (g m)", b=4), ps, ACT.Copy)
                ins.then_inc(s_evA, 1)
            mod_evac(MOD_S5, 12)
            act.wait_ge(s_scd, 1)
            act.wait_ge(s_modmm[1], 6)
            for gp in range(2):
                act.activation(hxv[0:64, gp], hpv[64 * gp:64 * gp + 64, 0], ACT.Copy).then_inc(s_hx, 1)
            wait_copied(act, ("y", NR - 1))
            act.wait_ge(s_out, 32)
            for j in range(TC // 2):
                act.activation(z5[:, j, :].rearrange("p (g q) -> p g q", g=G), h5[:, :, j, :], ACT.Gelu_apprx_tanh).then_inc(s_gelu, 1)
            act.activation(at(MS, D, 0, NB), at(MS, D, 0, NB), ACT.Gelu_apprx_tanh).then_inc(s_gelu, 1)
            for j in range(5):
                rows = P if j < 4 else NB
                act.wait_ge(s_zt, j + 1)
                if j >= 2:
                    act.wait_ge(s_gm, 4 * (j - 1))
                act.activation(zt[j % 2][:, :, 0:rows],
                               psum[:, 2 * (j % 2):2 * (j % 2) + 2, :].rearrange(
                                   "p b (k t) -> p (b k) t", k=4)[:, :, 0:rows], ACT.Copy).then_inc(s_zc, 1)
                for q in range(4):
                    m = 4 * j + q
                    act.wait_ge(s_gm, m + 1)
                    if m >= 2:
                        act.wait_ge(s_ga, m - 1)
                    act.activation(gate[m % 2][0:rows], psum[0:rows, 4 + m % 2, 256:512],
                                   ACT.Sigmoid).then_inc(s_sg, 1)

            def peer_prep(t):
                R = rows_of(t)
                act.wait_ge(s_rld[t % 2], row_no(LOADS, f"peer{t // 5}", t % 5))
                if t % 5 == 0:
                    act.wait_ge(s_pmr, t // 5 + 1)
                act.activation(at(PTMP, D, 0, R), at(XT + (t % 2) * D, D, 0, R), ACT.Square,
                               accum_out=stat[0:R, t % 2:t % 2 + 1]).then_inc(s_sq, 1)
                act.wait_ge(s_ms, norm_no(f"peer{t // 5}", t % 5))
                act.activation(stat[0:R, 2 + t % 2:3 + t % 2], stat[0:R, 2 + t % 2:3 + t % 2], ACT.Sqrt
                               ).then_inc(s_rt, 1)
                act.wait_ge(s_pt, t + 1)
                act.activation(htr[:, :, 0:R], psum[:, 2:4, :].rearrange("p b (k t) -> p (b k) t", k=4)[:, :, 0:R],
                               ACT.Copy).then_inc(s_ptc, 1)
                for m in range(4):
                    for kind in ("qs" if m else "q") + ("s" if m == 3 else ""):
                        if kind == "q":
                            act.wait_ge(s_pq, 4 * t + m + 1)
                            act.activation(qt[:, 4 * m:4 * m + 4, 0:R],
                                           psum[:, 2 + m % 2, :].rearrange("p (h t) -> p h t", h=4)[:, :, 0:R],
                                           ACT.Copy).then_inc(s_pqc, 1)
                    for ms in ([m - 1] if m else []) + ([3] if m == 3 else []):
                        act.wait_ge(s_ps, 4 * t + ms + 1)
                        if t:
                            act.wait_ge(s_idx, 8 * (t - 1) + 2 * ms + 2)
                        act.activation(ssb[0:R, 4 * ms:4 * ms + 4, :].rearrange("p h n -> p (h n)"),
                                       psum[0:R, 4 + ms % 2, :], ACT.Copy).then_inc(s_psc, 1)

            def peer_exp(t):
                R = rows_of(t)
                act.wait_ge(s_bv, t + 1)
                act.activation(at(BV, PH * TOPK, 0, R), at(BV, PH * TOPK, 0, R), ACT.Exp).then_inc(s_ex, 1)

            def peer_gelu(t):
                act.wait_ge(s_dots, t + 1)
                n_ = P if t % 5 < 4 else RING
                act.activation(at(DOTS, n_), at(DOTS, n_), ACT.Gelu_apprx_tanh).then_inc(s_act, 1)

            def peer_diags(t):
                base = group_base(t, 1)
                act.wait_ge(s_w, t + 1)
                if t % 5 < 4:
                    with act.Fori(0, PH) as i:
                        for g in range(2):
                            for r in V_PE:
                                act.wait_ge(freed[r], 2 * i + (base + g))
                                act.activation(diag[:, r, :], ident, ACT.Copy,
                                               scale=at(DOTS + P, P)[:, bass.ds(i * TOPK + g * RING + r, 1)]
                                               ).then_inc(s_dg, 1)
                else:
                    for r in range(RING):
                        act.wait_ge(freed[r], base)
                        act.activation(diag[:, r, 0:NB], sel8, ACT.Copy,
                                       scale=at(DOTS + P + r, 1)).then_inc(s_dg, 1)

            def peer_act(layer):
                t0 = 5 * layer
                peer_prep(t0)
                peer_exp(t0)
                for b in range(5):
                    t = t0 + b
                    if b < 4:
                        peer_prep(t + 1)
                    peer_gelu(t)
                    peer_diags(t)
                    if b < 4:
                        peer_exp(t + 1)

            def attention_act():
                for j in range(5):
                    R = rows5(j)
                    x = at(MX + (j % 2) * D, D, 0, R)
                    act.wait_ge(s_rld[j % 2], row_no(LOADS, "attention", j))
                    act.wait_ge(s_mmr, 1)
                    act.activation(at(OTT, D, 0, R), x, ACT.Square, accum_out=stat[0:R, 16:17]).then_inc(s_sq, 1)
                    act.wait_ge(s_ms, norm_no("attention", j))
                    act.activation(stat[0:R, 17:18], stat[0:R, 17:18], ACT.Sqrt).then_inc(s_rt, 1)
                    for m, (ready, done) in enumerate(((s_tx, s_txc), (s_tx, s_txc))):
                        act.wait_ge(ready, 2 * j + m + 1)
                        if j == 4:
                            act.wait_ge(s_mmr, 2)
                        act.activation(mht[m][:, :, 0:R], psum[:, 2 * m:2 * m + 2, :].rearrange(
                            "p b (k t) -> p (b k) t", k=4)[:, :, 0:R], ACT.Copy).then_inc(done, 1)
                    act.wait_ge(s_pr, 2 * j + 1)
                    link(act.activation(at(OTT, KVL, 0, R), psum[0:R, 4, 0:KVL], ACT.Square,
                                        accum_out=stat[0:R, 18:19]))
                    act.wait_ge(s_pr, 2 * j + 2)
                    act.activation(at(OTT, QL, 0, R), psum[0:R, 5, 0:QL], ACT.Square,
                                   accum_out=stat[0:R, 19:20]).then_inc(s_lsq, 1)
                    act.wait_ge(s_lmn, j + 1)
                    act.activation(stat[0:R, 20:22], stat[0:R, 20:22], ACT.Sqrt).then_inc(s_lrt, 1)
                    cols = slice(P * j, P * j + R)
                    act.wait_ge(s_tl, 2 * j + 1)
                    link(act.activation(ckvt[:, :, cols], psum[:, 6, 0:2 * P].rearrange(
                        "p (c t) -> p c t", c=2)[:, :, 0:R], ACT.Copy))
                    act.activation(at(KRT + P * j, R, NOPE, QKD), psum[NOPE:QKD, 6, 2 * P:2 * P + R], ACT.Copy
                                   ).then_inc(s_tlc, 1)
                    act.wait_ge(s_tl, 2 * j + 2)
                    act.activation(at(MCQT, QL).rearrange("p (k t) -> p k t", k=4)[:, :, 0:R],
                                   psum[:, 7, :].rearrange("p (k t) -> p k t", k=4)[:, :, 0:R], ACT.Copy
                                   ).then_inc(s_tlc, 1)
                    act.wait_ge(s_q, j + 1)
                    act.activation(at(MQ, NH * QKD, 0, R), psum[0:R, 0:3, :].rearrange("p b n -> p (b n)"), ACT.Copy
                                   ).then_inc(s_qc, 1)
                    act.wait_ge(s_tqh, j + 1)
                    dst = qtm[0:QKD, :, cols] if j < 4 else qts[0:QKD]
                    act.activation(dst, psum[0:QKD, 0:4, :].rearrange("p b (h t) -> p (b h) t", h=4)[:, :, 0:R],
                                   ACT.Copy).then_inc(s_tqhc, 1)
                act.wait_ge(s_ql, 1)
                act.activation(qlt.rearrange("p c b h -> p c h b"),
                               psum[:, 5, 0:2 * NH * NB].rearrange("p (c h b) -> p c h b", c=2, h=NH), ACT.Copy
                               ).then_inc(s_qlc, 1)
                for h in range(0, NH, 2):
                    act.wait_ge(s_ktp, h + 1)
                    act.activation(kt_[0:NOPE, h, :], psum[0:NOPE, h % 4, :], ACT.Copy).then_inc(s_kta, 1)
                for n_ in range(NTILE * NH):
                    i, h = divmod(n_, NH)
                    w = P * (i + 1)
                    act.wait_ge(s_nm, n_ + 1)
                    if n_ >= 2:
                        act.wait_ge(s_T, n_ - 1)
                    act.activation(at(PP + (n_ % 2) * SEQ, w), psum[:, n_ % 2, 0:w], ACT.Exp, scale=SM_SCALE,
                                   bias=stat[:, 32 + n_ % 2:33 + n_ % 2], accum_out=at(SUMS + n_ % 16, 1)
                                   ).then_inc(s_e2, 1)
                    if h == 1 and i:
                        out_copy_act(i - 1)
                out_copy_act(3)
                for b in range(NB + 1):
                    if b < NB:
                        for q in (0, 2):
                            cache_copies(act, b, q)
                    if b >= 1:
                        c = b - 1
                        sc = at(SCS[c % 2], NKEY, 0, NH)
                        act.wait_ge(s_cnm, c + 1)
                        act.activation(sc, sc, ACT.Exp, scale=SM_SCALE, bias=stat[0:NH, 34 + c % 2:35 + c % 2],
                                       accum_out=stat[0:NH, 36 + c % 2:37 + c % 2]).then_inc(s_ce, 1)
                out_copy_act(4)

            def out_copy_act(j):
                R = rows5(j)
                act.wait_ge(s_ot, j + 1)
                act.activation(at(OTT, D).rearrange("p (k t) -> p k t", k=KD)[:, :, 0:R],
                               psum[:, 6:8, :].rearrange("p b (k t) -> p (b k) t", k=4)[:, :, 0:R], ACT.Copy
                               ).then_inc(s_otc, 1)

            def cache_copies(eng, b, q):
                cache_copy(eng, b, q, eng.activation, s_cta)

            def cache_copy(eng, b, q, copy, done):
                eng.wait_ge(s_ct, 4 * b + q + 1)
                if b:
                    eng.wait_ge(s_cs, 5 * b)
                link(copy(kts[:, :, 512 * q:512 * (q + 1)], psum[:, 2 * (q % 2):2 * (q % 2) + 2, :], ACT.Copy))
                copy(krts[NOPE:QKD, 512 * q:512 * (q + 1)], psum[0:ROPE, 4 + q % 2, :], ACT.Copy).then_inc(done, 1)

            def final_act():
                for j in range(5):
                    R = rows5(j)
                    act.wait_ge(s_rld[j % 2], row_no(LOADS, "final", j))
                    act.activation(at(FSQ, D, 0, R), at(FX + (j % 2) * D, D, 0, R), ACT.Square,
                                   accum_out=stat[0:R, 40 + j:41 + j]).then_inc(s_sq, 1)
                    act.wait_ge(s_ms, norm_no("final", j))
                    act.activation(stat[0:R, 45 + j:46 + j], stat[0:R, 45 + j:46 + j], ACT.Sqrt).then_inc(s_rt, 1)

            mod_evac(12, NMB)
            peer_act(0)
            attention_act()
            peer_act(1)
            final_act()

        @block.vector
        def _(dve):
            n = [0]

            def link(ins):
                n[0] += 1
                ins.then_inc(vec, 1)
                dve.wait_ge(vec, n[0])

            def tt(out, x, y, op):
                link(dve.tensor_tensor(out, x, y, op))

            def ts(out, x, s1, s2, op0, op1=None):
                if s2 is None:
                    link(dve.tensor_scalar(out, x, s1, None, op0))
                else:
                    link(dve.tensor_scalar(out, x, s1, s2, op0, op1))

            def stt(out, x, s, y, op0, op1):
                link(dve.scalar_tensor_tensor(out=out, in0=x, scalar=s, in1=y, op0=op0, op1=op1))

            link(dve.memset(stat, 1.0))
            dve.memset(zrow, 0.0).then_inc(s_z, 1)
            dve.wait_ge(s_z, 1)
            link(dve.memset(stat[:, 60:61], float(np.pi / 2)))
            dve.wait_ge(s_silu, 1)
            e = at(U2 + NPAR, KD * NC9)
            ts(e, e, 1.0, None, ALU.add)
            link(dve.reciprocal(e, e))
            dve.tensor_tensor(at(SILU, KD * NC9), at(SILU, KD * NC9), e, ALU.mult).then_inc(s_silu, 1)
            dt, ar, th, kk, rr, sn, _, cs, e1, tA, tB, tC, tD, tE, tF, tG = small
            dve.wait_ge(s_dt, 1)
            tt(ar, a_re, dt, ALU.mult)
            stt(th, a_im, 0.5, dt, ALU.mult, ALU.mult)
            ts(kk, th, float(1 / (2 * np.pi)), None, ALU.mult)
            ts(kk, kk, 12582912.0, None, ALU.add)
            ts(kk, kk, 12582912.0, None, ALU.subtract)
            stt(rr, kk, -6.28125, th, ALU.mult, ALU.add)
            stt(rr, kk, float(-(2 * np.pi - 6.28125)), rr, ALU.mult, ALU.add)
            dve.tensor_scalar(rr, rr, 3.1415925, -3.1415925, ALU.min, ALU.max).then_inc(s_half, 1)
            ts(ar, ar, 80.0, -80.0, ALU.min, ALU.max)
            ts(tA, ar, 1.0 / 64, None, ALU.mult)
            ts(e1, tA, 1.0 / 7, 1.0, ALU.mult, ALU.add)
            for m in (6, 5, 4, 3, 2):
                stt(e1, e1, 1.0 / m, tA, ALU.mult, ALU.mult)
                ts(e1, e1, 1.0, None, ALU.add)
            tt(e1, e1, tA, ALU.mult)
            for m in range(6):
                stt(e1, e1, 2.0, e1, ALU.add, ALU.mult)
            dve.wait_ge(s_sin, 2)
            stt(tB, sn, 2.0, cs, ALU.mult, ALU.mult)
            stt(tC, sn, -2.0, sn, ALU.mult, ALU.mult)
            ts(tD, e1, 1.0, None, ALU.add)
            tt(tE, tD, tC, ALU.mult)
            tt(tE, tE, e1, ALU.add)
            tt(tF, tD, tB, ALU.mult)
            link(dve.memset(pw_re[:, 0, :], 1.0))
            link(dve.memset(pw_im[:, 0, :], 0.0))
            ts(pw_re[:, 1, :], tE, 1.0, None, ALU.add)
            ts(pw_im[:, 1, :], tF, 1.0, None, ALU.mult)
            tt(tA, a_re, a_re, ALU.mult)
            tt(tB, a_im, a_im, ALU.mult)
            tt(tA, tA, tB, ALU.add)
            link(dve.reciprocal(tA, tA))
            tt(tB, tE, a_re, ALU.mult)
            tt(tC, tF, a_im, ALU.mult)
            tt(tB, tB, tC, ALU.add)
            tt(tB, tB, tA, ALU.mult)
            tt(tC, tF, a_re, ALU.mult)
            tt(tD, tE, a_im, ALU.mult)
            tt(tC, tC, tD, ALU.subtract)
            tt(tC, tC, tA, ALU.mult)
            shape = [P, G, GP]
            qre, qim = tB.unsqueeze(2).to_broadcast(shape), tC.unsqueeze(2).to_broadcast(shape)
            tt(bbar_re, b_re, qre, ALU.mult)
            tt(tmp_v, b_im, qim, ALU.mult)
            tt(bbar_re, bbar_re, tmp_v, ALU.subtract)
            tt(bbar_im, b_im, qre, ALU.mult)
            tt(tmp_v, b_re, qim, ALU.mult)
            tt(bbar_im, bbar_im, tmp_v, ALU.add)
            for lo in (1, 2, 4):
                sq_re = pw_re[:, lo:lo + 1, :].to_broadcast([P, lo, G])
                sq_im = pw_im[:, lo:lo + 1, :].to_broadcast([P, lo, G])
                src_re, src_im = pw_re[:, 1:1 + lo, :], pw_im[:, 1:1 + lo, :]
                dst_re, dst_im = pw_re[:, 1 + lo:1 + 2 * lo, :], pw_im[:, 1 + lo:1 + 2 * lo, :]
                t1 = at(TMP + 2 * D, lo * G).rearrange("p (m g) -> p m g", m=lo)
                tt(dst_re, src_re, sq_re, ALU.mult)
                tt(t1, src_im, sq_im, ALU.mult)
                tt(dst_re, dst_re, t1, ALU.subtract)
                tt(dst_im, src_re, sq_im, ALU.mult)
                tt(t1, src_im, sq_re, ALU.mult)
                tt(dst_im, dst_im, t1, ALU.add)
            ts(ca[0:64], pw_re[0:64], 1.0, None, ALU.mult)
            ts(cb[0:64], pw_im[0:64], -1.0, None, ALU.mult)
            ts(bb[0:64], pw_im[0:64], -1.0, None, ALU.mult)
            ts(ca[64:P], pw_im[64:P], 1.0, None, ALU.mult)
            ts(cb[64:P], pw_re[64:P], -1.0, None, ALU.mult)
            dve.tensor_scalar(bb[64:P], pw_re[64:P], 1.0, None, ALU.mult).then_inc(s_tabs, 1)
            dve.wait_ge(s_tabs, 1)
            for t in range(TC + 1):
                al = ca[:, t, :].unsqueeze(2).to_broadcast(shape)
                be = cb[:, t, :].unsqueeze(2).to_broadcast(shape)
                tt(cl[0:64, :, t, :], c_re[0:64], al[0:64], ALU.mult)
                stt(cl[64:P, :, t, :], c_re[64:P], -1.0, al[64:P], ALU.mult, ALU.mult)
                tt(tmp_v, c_im, be, ALU.mult)
                tt(cl[:, :, t, :], cl[:, :, t, :], tmp_v, ALU.add)
            for gp in range(2):
                rows = slice(64 * gp, 64 * gp + 64)
                for m, t in enumerate((TC, 1)):
                    for k, (src, sign) in enumerate(((pw_re, 1.0), (pw_re, 1.0), (pw_im, -1.0), (pw_im, 1.0))):
                        c0 = (4 * m + k) * HALF
                        ts(lamt[rows, c0:c0 + HALF], src[rows, t, gp:G:2], sign, None, ALU.mult)
            dve.tensor_scalar(stat[:, 61:62], stat[:, 60:61], 1.0, None, ALU.mult).then_inc(s_clr, 1)

            dve.wait_ge(s_clr, 1)
            dve.wait_ge(s_mods5, 16 * 6)
            g_bc, xs, sh_s, sc_s = at(TMP, D), at(TMP + D, D, 0, NB), at(TMP + 2 * D, D, 0, NB), \
                at(TMP + 3 * D, D, 0, NB)
            stt(mod_a, mod_a, 1.0, g_bc, ALU.add, ALU.mult)
            stt(sc_s, sc_s, 1.0, g_bc[0:NB], ALU.add, ALU.mult)
            dve.wait_ge(s_sq, 1)
            dve.tensor_scalar(stat[:, 8:13], stat[:, 0:5], 1.0 / D, EPS, ALU.mult, ALU.add).then_inc(s_ms, 1)
            dve.wait_ge(s_rt, 1)
            link(dve.reciprocal(stat[:, 8:13], stat[:, 8:13]))
            for j in range(TC // 2):
                stt(x5[:, j, :], x5[:, j, :], stat[:, 8 + j:9 + j], mod_a, ALU.mult, ALU.mult)
                ins = dve.tensor_tensor(h5[:, :, j, :], x5[:, j, :].rearrange("p (g q) -> p g q", g=G),
                                        mod_s.rearrange("p (g q) -> p g q", g=G), ALU.add)
                if j < 3:
                    link(ins)
                else:
                    ins.then_inc(s_h5, 1)
            stt(xs, xs, stat[0:NB, 12:13], sc_s, ALU.mult, ALU.mult)
            dve.tensor_tensor(xs, xs, sh_s, ALU.add).then_inc(s_h5, 1)
            dve.wait_ge(s_dld, 16)
            dve.wait_ge(s_hst, 16)
            dve.wait_ge(s_h5, 2)
            tt(at(MS, D, 0, NB), xs, mod_a[0:NB], ALU.mult)
            dve.wait_ge(s_mm, NR)
            for j in range(TC // 2):
                tt(h5[:, :, j, :], h5[:, :, j, :], mod_a.rearrange("p (g q) -> p g q", g=G), ALU.mult)
            for r in range(NR):
                no = round_no[("i", r)]
                dve.wait_ge(s_mm, no + 1)
                ps = half(no)[:, :, 0:4 * UC].rearrange("p b (g c) -> p b g c", g=4)
                for k in range(2):
                    for gp in range(2):
                        src = ps[64 * k:64 * k + 64, :, gp:4:2, :]
                        rows = slice(64 * gp, 64 * gp + 64)
                        g2 = slice(8 * r, 8 * r + 8)
                        link(dve.tensor_copy(sj[rows, :, k, g2].rearrange("p c (b g) -> p b g c", b=4),
                                             src[:, :, :, 0:CH]))
                        ins = dve.tensor_copy(si[rows, k, g2, :].rearrange("p (b g) c -> p b g c", b=4),
                                              src[:, :, :, CH + NB:UC])
                        if k and gp:
                            ins.then_inc(s_evV, 1)
                        else:
                            link(ins)
            link(dve.memset(hpx[:, 0, :], 0.0))
            wait_copied(dve, ("i", NR - 1))
            m4 = scan_tmp
            def scan_step(i, first=False):
                h_now = hpx[:, bass.ds(i, 1), :].rearrange("p o m -> p (o m)")
                h_next = hpx[:, bass.ds(i + 1, 1), :].rearrange("p o m -> p (o m)")
                inj = sj[:, bass.ds(i, 1), :, :].rearrange("p o k g -> p (o k g)")
                if not first:
                    dve.wait_ge(s_scan, 5 * i)
                dve.tensor_tensor(m4[:, 0:2 * HALF], lamt[:, 0:2 * HALF], h_now[:, 0:2 * HALF],
                                  ALU.mult).then_inc(s_scan, 1)
                dve.tensor_tensor(m4[:, 2 * HALF:4 * HALF], lamt[:, 2 * HALF:4 * HALF], h_now[:, HALF:3 * HALF],
                                  ALU.mult).then_inc(s_scan, 1)
                dve.wait_ge(s_scan, 5 * i + 2)
                dve.tensor_tensor(m4[:, 0:2 * HALF], m4[:, 0:2 * HALF], m4[:, 2 * HALF:4 * HALF],
                                  ALU.add).then_inc(s_scan, 1)
                dve.wait_ge(s_scan, 5 * i + 3)
                dve.tensor_tensor(h_next[:, 0:2 * HALF], m4[:, 0:2 * HALF], inj, ALU.add).then_inc(s_scan, 1)
                dve.tensor_tensor(h_next[:, 2 * HALF:3 * HALF], m4[:, 0:HALF], inj[:, 0:HALF],
                                  ALU.add).then_inc(s_scan, 1)

            scan_step(0, True)
            with dve.Fori(1, CH) as i:
                scan_step(i)
            dve.wait_ge(s_scan, 5 * CH)
            dve.tensor_copy(stat[:, 61:62], stat[:, 60:61]).then_inc(s_scd, 1)
            sh3 = [P, HALF, NB]
            lr, nli, li = (lamt[:, (4 + k) * HALF:(5 + k) * HALF].unsqueeze(2).to_broadcast(sh3) for k in (0, 2, 3))
            tx = sj_tmp
            for k, fac in ((0, nli), (1, li)):
                tt(tx, st0[:, k], lr, ALU.mult)
                tt(si[:, k], si[:, k], tx, ALU.add)
                tt(tx, st0[:, 1 - k], fac, ALU.mult)
                if k == 0:
                    tt(si[:, k], si[:, k], tx, ALU.add)
                else:
                    dve.tensor_tensor(si[:, k], si[:, k], tx, ALU.add).then_inc(s_scd, 1)
            for b in range(2):
                dve.wait_ge(s_modmm[b], 6)
            for gp in range(2):
                dve.tensor_copy(hxv[64:P, gp], hpv[64 * gp:64 * gp + 64, 1]).then_inc(s_hx, 1)
            for r in range(NR):
                no = round_no[("y", r)]
                dve.wait_ge(s_mm, no + 1)
                ps = half(no).rearrange("p b (g t q) -> p (b g) t q", g=4, t=TC)
                for s in range(2):
                    yv = h5[64 * s:64 * s + 64, RG * r:RG * (r + 1)]
                    tt(yv, yv, ps[0:64, :, 4 * s:4 * s + 4, :], ALU.add)
                ys = at(MS + RG * GP * r, RG * GP, 0, NB).rearrange("p (g q) -> p g q", g=RG)
                dve.tensor_tensor(ys, ys, ps[64:64 + NB, :, 0, :], ALU.add).then_inc(s_evV, 1)
            dve.wait_ge(s_x5, 48 + 16 * 5)
            for j in range(5):
                rows = P if j < 4 else NB
                tb = glu_t[j % 2]
                for q in range(4):
                    m = 4 * j + q
                    dve.wait_ge(s_sg, m + 1)
                    dve.tensor_tensor(tb[0:rows, 256 * q:256 * (q + 1)], psum[0:rows, 4 + m % 2, 0:256],
                                      gate[m % 2][0:rows], ALU.mult).then_inc(s_ga, 1)
                dve.wait_ge(s_ga, 4 * (j + 1))
                ga = mod_a if j < 4 else at(BL + 5 * D, D, 0, NB)
                tt(tb[0:rows], tb[0:rows], ga, ALU.mult)
                xr = at(BL + j * D, D, 0, rows)
                dve.tensor_tensor(xr, xr, tb[0:rows], ALU.add).then_inc(s_x1, 1)
                dve.wait_ge(s_x1, j + 1)

            def peer_norm(t):
                R = rows_of(t)
                st = stat[0:R, 2 + t % 2:3 + t % 2]
                x, h = at(XT + (t % 2) * D, D, 0, R), at(HT + (t % 2) * D, D, 0, R)
                sh, sc = (at(PMOD + (0 if R == P else 3 * D) + m * D, D, 0, R) for m in range(2))
                dve.wait_ge(s_sq, norm_no(f"peer{t // 5}", t % 5))
                dve.tensor_scalar(st, stat[0:R, t % 2:t % 2 + 1], 1.0 / D, EPS, ALU.mult, ALU.add
                                  ).then_inc(s_ms, 1)
                dve.wait_ge(s_rt, norm_no(f"peer{t // 5}", t % 5))
                link(dve.reciprocal(st, st))
                stt(h, x, st, sc, ALU.mult, ALU.mult)
                dve.tensor_tensor(h, h, sh, ALU.add).then_inc(s_ph, 1)

            def peer_top(t, h):
                R = rows_of(t)
                topv = at(TOPV, 2 * TOPK, 0, R).rearrange("p (s k) -> p s k", s=2)
                topi = at(TOPI, 2 * TOPK, 0, R).bitcast(U32).rearrange("p (s k) -> p s k", s=2)
                topf = at(TOPI + 32, 2 * TOPK, 0, R).rearrange("p (s k) -> p s k", s=2)
                cand = at(CAND, TOPK * TOPK, 0, R)
                bv = at(BV + h * TOPK, TOPK, 0, R)
                bp = at(BP, TOPK, 0, R).bitcast(U32)
                ab = at(AB, 2 * TOPK, 0, R)
                onehot = at(ONEH, 512, 0, R)

                def best16(vals, v16, i16):
                    link(dve.max(v16[:, 0:8], vals))
                    link(dve.max_index(i16[:, 0:8], v16[:, 0:8], vals))
                    link(dve.match_replace(vals, v16[:, 0:8], vals, -3.0e38))
                    link(dve.max(v16[:, 8:16], vals))
                    link(dve.max_index(i16[:, 8:16], v16[:, 8:16], vals))

                dve.wait_ge(s_psc, 4 * t + h // 2 + 1)
                for s in range(2):
                    best16(ssb[0:R, 2 * h + s, :], topv[:, s], topi[:, s])
                link(dve.tensor_copy(topf, topi))
                tt(cand.rearrange("p (a b) -> p a b", a=TOPK),
                   topv[:, 0].unsqueeze(2).to_broadcast([R, TOPK, TOPK]),
                   topv[:, 1].unsqueeze(1).to_broadcast([R, TOPK, TOPK]), ALU.add)
                best16(cand, bv, bp)
                abi = at(AB + 32, 2 * TOPK, 0, R).bitcast(U32)
                link(dve.tensor_scalar(abi[:, 0:TOPK], bp, 4, None, ALU.logical_shift_right))
                link(dve.tensor_scalar(abi[:, TOPK:2 * TOPK], bp, TOPK - 1, None, ALU.bitwise_and))
                link(dve.tensor_copy(ab, abi))
                oh = onehot.rearrange("p (k m) -> p k m", m=TOPK)
                tt(oh, ab.unsqueeze(2).to_broadcast([R, 2 * TOPK, TOPK]),
                   iota16[0:R].unsqueeze(1).to_broadcast([R, 2 * TOPK, TOPK]), ALU.is_equal)
                for s in range(2):
                    o3 = oh[:, s * TOPK:(s + 1) * TOPK]
                    tt(o3, o3, topf[:, s].unsqueeze(1).to_broadcast([R, TOPK, TOPK]), ALU.mult)
                link(dve.tensor_reduce(ab, oh, AX.X, ALU.add))
                idx = at(IDXP + (t % 2) * P + h * TOPK, TOPK, 0, R).bitcast(I32)
                dve.scalar_tensor_tensor(out=idx, in0=ab[:, 0:TOPK], scalar=float(N_KEYS), in1=ab[:, TOPK:2 * TOPK],
                                         op0=ALU.mult, op1=ALU.add).then_inc(s_idx, 1)
                dve.wait_ge(s_idx, 8 * t + h + 1)

            def peer_shift(t):
                R = rows_of(t)
                bv = at(BV, PH * TOPK, 0, R).rearrange("p (h k) -> p h k", h=PH)
                mx = at(CAND, PH, 0, R)
                link(dve.tensor_copy(mx, bv[:, :, 0]))
                dve.tensor_tensor(bv, bv, mx.unsqueeze(2).to_broadcast([R, PH, TOPK]), ALU.subtract
                                  ).then_inc(s_bv, 1)

            def peer_gates(t):
                R = rows_of(t)
                bv = at(BV, PH * TOPK, 0, R).rearrange("p (h k) -> p h k", h=PH)
                g = at(PG + (t % 2) * P, PH * TOPK, 0, R).rearrange("p (h k) -> p h k", h=PH)
                dve.wait_ge(s_ex, t + 1)
                sums = at(CAND, PH, 0, R)
                link(dve.tensor_reduce(sums, bv, AX.X, ALU.add))
                link(dve.reciprocal(sums, sums))
                dve.tensor_tensor(g, bv, sums.unsqueeze(2).to_broadcast([R, PH, TOPK]), ALU.mult).then_inc(s_g, 1)

            def dot(t, r, g, col):
                h = at(HT + (t % 2) * D, D) if t % 5 < 4 else at(HT + ((t + 1) % 2) * D, D)
                dve.scalar_tensor_tensor(out=ring[r], in0=ring[r], scalar=1.0, in1=h, op0=ALU.mult, op1=ALU.mult,
                                         accum_out=col).then_inc(freed[r], 1)

            def peer_dots(t):
                base = group_base(t, 0)
                if t % 5 < 4:
                    with dve.Fori(0, PH) as i:
                        for g in range(2):
                            for r in range(RING):
                                dve.wait_ge(landed[r], 32 * i + 16 * (base + g + 1))
                                dot(t, r, g, at(DOTS, P)[:, bass.ds(i * TOPK + g * RING + r, 1)])
                else:
                    dve.wait_ge(s_shb, 16 * NB * (t // 5 + 1))
                    for r in range(RING):
                        dve.wait_ge(landed[r], 16 * (base + 1))
                        dot(t, r, 0, at(DOTS + r, 1))
                last = group_base(t, 1)
                dve.wait_ge(freed[RING - 1], last)
                dve.tensor_copy(stat[:, 61:62], stat[:, 60:61]).then_inc(s_dots, 1)

            def peer_weights(t):
                dve.wait_ge(s_act, t + 1)
                if t % 5 < 4:
                    g, n_ = at(PG + (t % 2) * P, P), P
                    dve.wait_ge(s_g, t + 1)
                else:
                    g, n_ = at(GS, RING), RING
                    dve.wait_ge(s_sld, 32 * (t // 5 + 1))
                dve.tensor_tensor(at(DOTS + P, n_), at(DOTS, n_), g, ALU.mult).then_inc(s_w, 1)
                dve.wait_ge(s_w, t + 1)

            def peer_values(t, h):
                for g in range(2):
                    base = group_base(t, 1) + 2 * h + g
                    for r in V_DVE:
                        dve.wait_ge(landed[r], 16 * (base + 1))
                        dve.scalar_tensor_tensor(out=at(YACC, D), in0=ring[r],
                                                 scalar=at(DOTS + P + h * TOPK + g * RING + r, 1),
                                                 in1=at(YACC, D), op0=ALU.mult, op1=ALU.add).then_inc(freed[r], 1)
                        dve.wait_ge(freed[r], base + 1)

            def peer_out(t):
                R = rows_of(t)
                y = at(YACC, D, 0, R)
                x = at(XT + (t % 2) * D, D, 0, R)
                ga = at(PMOD + (2 if R == P else 5) * D, D, 0, R)
                ps = psum[0:R, 0:2, :].rearrange("p b n -> p (b n)")
                dve.wait_ge(s_yp, t + 1)
                if R == P:
                    dve.tensor_tensor(y, y, ps, ALU.add).then_inc(s_yr, 1)
                else:
                    dve.tensor_copy(y, ps).then_inc(s_yr, 1)
                dve.wait_ge(s_yr, t + 1)
                tt(y, y, ga, ALU.mult)
                dve.tensor_tensor(x, x, y, ALU.add).then_inc(s_xn, 1)

            def peer_dve(layer):
                t0 = 5 * layer
                dve.wait_ge(s_pmod, 48 * (layer + 1))
                for m in (1, 4):
                    R = P if m == 1 else NB
                    sc = at(PMOD + m * D, D, 0, R)
                    ins = dve.scalar_tensor_tensor(out=sc, in0=sc, scalar=1.0, in1=at(PTMP, D, 0, R), op0=ALU.add,
                                                   op1=ALU.mult)
                    if m == 1:
                        link(ins)
                    else:
                        ins.then_inc(s_pmr, 1)
                dve.wait_ge(s_pmr, layer + 1)
                peer_norm(t0)
                for h in range(PH):
                    peer_top(t0, h)
                peer_shift(t0)
                peer_gates(t0)
                for b in range(5):
                    t = t0 + b
                    if b < 4:
                        peer_norm(t + 1)
                    peer_dots(t)
                    peer_weights(t)
                    if b < 4:
                        link(dve.memset(at(YACC, D), 0.0))
                        for h in range(PH):
                            peer_top(t + 1, h)
                            peer_values(t, h)
                        peer_shift(t + 1)
                    peer_out(t)
                    if b < 4:
                        peer_gates(t + 1)

            def rotate(x1, x2, cos, sin, shape):
                n_ = shape[1] * shape[2] if len(shape) == 3 else shape[1]
                t = [at(PP + i * 256, n_, 0, shape[0]) for i in range(4)]
                if len(shape) == 3:
                    t = [v_.rearrange("p (h m) -> p h m", h=shape[1]) for v_ in t]
                tt(t[0], x1, cos, ALU.mult)
                tt(t[1], x2, sin, ALU.mult)
                tt(t[2], x1, sin, ALU.mult)
                tt(t[3], x2, cos, ALU.mult)
                return t

            def attention_mods(R, n_):
                dve.wait_ge(s_mm1, 64 * n_)
                kv_sc, q_sc = at(MMOD + D, D, 0, R), at(MMOD + 3 * D, D, 0, R)
                stt(kv_sc, kv_sc, 1.0, at(MHT, D, 0, R), ALU.add, ALU.mult)
                dve.scalar_tensor_tensor(out=q_sc, in0=q_sc, scalar=1.0, in1=at(MHT + D, D, 0, R), op0=ALU.add,
                                         op1=ALU.mult).then_inc(s_mmr, 1)
                dve.wait_ge(s_mmr, n_)

            def attention_dve():
                dve.wait_ge(s_mw, 160)
                pages = at(SUB + 1, NB)
                link(dve.tensor_copy(at(OL, NB), pages.bitcast(I32)))
                dve.tensor_scalar(pages.bitcast(I32), at(OL, NB), 8.0, at(SUB, 1), ALU.mult, ALU.add
                                  ).then_inc(s_pix, 1)
                attention_mods(P, 1)
                for j in range(5):
                    R = rows5(j)
                    if j == 4:
                        attention_mods(NB, 2)
                    x = at(MX + (j % 2) * D, D, 0, R)
                    dve.wait_ge(s_sq, norm_no("attention", j))
                    st = stat[0:R, 17:18]
                    dve.tensor_scalar(st, stat[0:R, 16:17], 1.0 / D, EPS, ALU.mult, ALU.add).then_inc(s_ms, 1)
                    dve.wait_ge(s_rt, norm_no("attention", j))
                    link(dve.reciprocal(st, st))
                    for m, (used, made) in enumerate(((s_tx, s_hin), (s_tx, s_hin))):
                        h = at(MH + m * D, D, 0, R)
                        if j:
                            dve.wait_ge(used, 2 * (j - 1) + m + 1)
                        stt(h, x, st, at(MMOD + (2 * m + 1) * D, D, 0, R), ALU.mult, ALU.mult)
                        dve.tensor_tensor(h, h, at(MMOD + 2 * m * D, D, 0, R), ALU.add).then_inc(made, 1)
                    dve.wait_ge(s_lsq, j + 1)
                    link(dve.tensor_scalar(stat[0:R, 20:21], stat[0:R, 18:19], 1.0 / KVL, EPS, ALU.mult, ALU.add))
                    dve.tensor_scalar(stat[0:R, 21:22], stat[0:R, 19:20], 1.0 / QL, EPS, ALU.mult, ALU.add
                                      ).then_inc(s_lmn, 1)
                    dve.wait_ge(s_lrt, j + 1)
                    link(dve.reciprocal(stat[0:R, 20:22], stat[0:R, 20:22]))
                    kvr = at(KVR + (j % 2) * KVC, KVC, 0, R)
                    if j >= 2:
                        dve.wait_ge(s_kvs[j % 2], 32 * (j // 2))
                        dve.wait_ge(s_tl, 2 * (j - 2) + 1)
                    stt(kvr[:, 0:KVL], psum[0:R, 4, 0:KVL], stat[0:R, 20:21], at(GCKV, KVL, 0, R), ALU.mult, ALU.mult)
                    m_ = ROPE // 2
                    t = rotate(psum[0:R, 4, KVL:KVL + m_], psum[0:R, 4, KVL + m_:KVC], csn[0:R, j, 0], csn[0:R, j, 1],
                               [R, m_])
                    tt(kvr[:, KVL:KVL + m_], t[0], t[1], ALU.subtract)
                    dve.tensor_tensor(kvr[:, KVL + m_:KVC], t[2], t[3], ALU.add).then_inc(s_kvr, 1)
                    dve.scalar_tensor_tensor(out=at(MCQ, QL, 0, R), in0=psum[0:R, 5, 0:QL], scalar=stat[0:R, 21:22],
                                             in1=at(GCQ, QL, 0, R), op0=ALU.mult, op1=ALU.mult).then_inc(s_kvr, 1)
                    dve.wait_ge(s_qc, j + 1)
                    q3 = at(MQ, NH * QKD, 0, R).rearrange("p (h n) -> p h n", h=NH)
                    x1, x2 = q3[:, :, NOPE:NOPE + m_], q3[:, :, NOPE + m_:QKD]
                    shape = [R, NH, m_]
                    cos, sin = (csn[0:R, j, i].unsqueeze(1).to_broadcast(shape) for i in range(2))
                    dve.wait_ge(s_kvr, 2 * j + 2)
                    t = rotate(x1, x2, cos, sin, shape)
                    tt(x1, t[0], t[1], ALU.subtract)
                    dve.tensor_tensor(x2, t[2], t[3], ALU.add).then_inc(s_qr, 1)
                for h in range(1, NH, 2):
                    dve.wait_ge(s_ktp, h + 1)
                    dve.tensor_copy(kt_[0:NOPE, h, :], psum[0:NOPE, h % 4, :]).then_inc(s_ktv, 1)
                dve.wait_ge(s_ql, 1)
                for i in range(NTILE):
                    dve.wait_ge(s_vp, i + 1)
                    dve.tensor_copy(vv[:, i, :], psum[:, 4 + 2 * (i % 2):6 + 2 * (i % 2), :].rearrange(
                        "p b n -> p (b n)")).then_inc(s_vc, 1)
                for n_ in range(NTILE * NH + 1):
                    if n_ < NTILE * NH:
                        i, h = divmod(n_, NH)
                        w = P * (i + 1)
                        dve.wait_ge(s_S, n_ + 1)
                        nm = stat[:, 32 + n_ % 2:33 + n_ % 2]
                        if n_ >= 2:
                            dve.wait_ge(s_e2, n_ - 1)
                        link(dve.tensor_reduce(nm, psum[:, n_ % 2, 0:w], AX.X, ALU.max))
                        dve.tensor_scalar(nm, nm, -SM_SCALE, None, ALU.mult).then_inc(s_nm, 1)
                    if n_ >= 1:
                        m = n_ - 1
                        i, h = divmod(m, NH)
                        w = P * (i + 1)
                        dve.wait_ge(s_T, m + 1)
                        if m >= 2:
                            dve.wait_ge(s_pv, m - 1)
                        dve.tensor_copy(at(PTT + (m % 2) * SEQ, w), psum[:, 2 + m % 2, 0:w]).then_inc(s_Tc, 1)
                        if h % 8 == 1 and m > 8:
                            head_scale(m // 8 - 1)
                        if h == 2 and i:
                            attention_out(i - 1)
                head_scale(7)
                attention_out(3)
                for b in range(NB + 1):
                    if b < NB:
                        for q in range(4):
                            if q % 2:
                                cache_copy(b, q)
                            if q:
                                sample_scores(b, q - 1)
                        sample_scores(b, 3)
                        sample_scores(b, 4)
                        sc = at(SCS[b % 2], NKEY, 0, NH)
                        nm = stat[0:NH, 34 + b % 2:35 + b % 2]
                        dve.wait_ge(s_csc, 5 * (b + 1))
                        link(dve.tensor_reduce(nm, sc, AX.X, ALU.max))
                        dve.tensor_scalar(nm, nm, -SM_SCALE, None, ALU.mult).then_inc(s_cnm, 1)
                    if b >= 1:
                        c = b - 1
                        dve.wait_ge(s_cT, c + 1)
                        ps = psum[:, 6, 0:17 * NH].rearrange("p (r h) -> p r h", r=17)
                        link(dve.tensor_copy(pts[:, 0:16], ps[:, 0:16]))
                        dve.tensor_copy(pts[0:NB, 16], ps[0:NB, 16]).then_inc(s_cTc, 1)
                        sm = stat[0:NH, 36 + c % 2:37 + c % 2]
                        dve.wait_ge(s_ce, c + 1)
                        link(dve.reciprocal(sm, sm))
                        dve.wait_ge(s_cpv, c + 1)
                        dve.tensor_scalar(at(OL, KVL, 0, NH), psum[0:NH, 7, 0:KVL], sm, None, ALU.mult
                                          ).then_inc(s_col, 1)
                        dve.wait_ge(s_cot, c + 1)
                        dve.tensor_copy(olt[:, :, :, c], psum[:, 7, KVL:KVL + 2 * NH].rearrange(
                            "p (c h) -> p c h", c=2)).then_inc(s_coc, 1)
                dve.wait_ge(s_os, 1)
                dve.wait_ge(s_ot, 4)
                dve.tensor_copy(at(OO, D, 0, NB), psum[0:NB, 0:2, :].rearrange("p b n -> p (b n)")).then_inc(s_on, 1)
                attention_out(4)

            def cache_copy(b, q):
                dve.wait_ge(s_ct, 4 * b + q + 1)
                if b:
                    dve.wait_ge(s_cs, 5 * b)
                link(dve.tensor_copy(kts[:, :, 512 * q:512 * (q + 1)], psum[:, 2 * (q % 2):2 * (q % 2) + 2, :]))
                dve.tensor_copy(krts[NOPE:QKD, 512 * q:512 * (q + 1)], psum[0:ROPE, 4 + q % 2, :]).then_inc(s_ctv, 1)

            def sample_scores(b, q):
                m = 5 * b + q
                dve.wait_ge(s_cs, m + 1)
                if b >= 2 and q == 0:
                    dve.wait_ge(s_cT, b - 1)
                sc = at(SCS[b % 2], NKEY, 0, NH)
                if q < 4:
                    dve.tensor_copy(sc[:, 512 * q:512 * (q + 1)], psum[0:NH, 6 + m % 2, :]).then_inc(s_csc, 1)
                else:
                    dve.tensor_tensor(sc[:, PAST:NKEY], psum[0:NH, 6 + m % 2, 0:NB],
                                      at(SMASK + NB * b, NB, 0, NH), ALU.add).then_inc(s_csc, 1)

            def head_scale(u):
                sm = at(SUMS + 8 * (u % 2), 8)
                dve.wait_ge(s_pv, 8 * (u + 1))
                dve.wait_ge(s_e2, 8 * (u + 1))
                link(dve.reciprocal(sm, sm))
                if u >= 2 and u % 2 == 0:
                    dve.wait_ge(s_ot, u // 2)
                dve.tensor_tensor(at(OO + 512 * (u % 2), 512).rearrange("p (h n) -> p h n", h=8),
                                  psum[:, 4 + u % 2, :].rearrange("p (h n) -> p h n", h=8),
                                  sm.unsqueeze(2).to_broadcast([P, 8, VH]), ALU.mult).then_inc(s_on, 1)

            def attention_out(j):
                R = rows5(j)
                x = at(MX + (j % 2) * D, D, 0, R)
                ga = at(MH + (0 if j < 4 else D), D, 0, R)
                dve.wait_ge(s_mw, 160 + 48)
                dve.wait_ge(s_rld[j % 2], row_no(LOADS, "residual", j))
                dve.wait_ge(s_yy, j + 1)
                y = at(MHT, D, 0, R)
                tt(y, psum[0:R, 6:8, :].rearrange("p b n -> p (b n)"), ga, ALU.mult)
                dve.tensor_tensor(x, x, y, ALU.add).then_inc(s_x3, 1)

            def final_dve():
                dve.wait_ge(s_mm1, 64 * 2 + 48)
                for m in (1, 3):
                    R = P if m == 1 else NB
                    sc = at(FMOD + m * D, D, 0, R)
                    stt(sc, sc, 1.0, at(FG, D, 0, R), ALU.add, ALU.mult)
                for j in range(5):
                    R = rows5(j)
                    x = at(FX + (j % 2) * D, D, 0, R)
                    m = 0 if j < 4 else 2
                    st = stat[0:R, 45 + j:46 + j]
                    dve.wait_ge(s_sq, norm_no("final", j))
                    dve.tensor_scalar(st, stat[0:R, 40 + j:41 + j], 1.0 / D, EPS, ALU.mult, ALU.add).then_inc(s_ms, 1)
                    dve.wait_ge(s_rt, norm_no("final", j))
                    link(dve.reciprocal(st, st))
                    stt(x, x, st, at(FMOD + (m + 1) * D, D, 0, R), ALU.mult, ALU.mult)
                    dve.tensor_tensor(x, x, at(FMOD + m * D, D, 0, R), ALU.add).then_inc(s_xn, 1)

            peer_dve(0)
            attention_dve()
            peer_dve(1)
            final_dve()

        @block.tensor
        def _(pe):
            def mod_products(first, last, slots):
                def pair(i, b, fresh=False):
                    pe.wait_ge(s_modw[b], 32 * i + 32)
                    if not fresh:
                        pe.wait_ge(s_modev[b], i)
                    w = at(slots[b], KD * MB).rearrange("p (k n) -> p k n", k=KD)
                    for k in range(KD):
                        pe.matmul(psum[0:NC9, 6 + b, :], silu[:, k, :], w[:, k, :], start=(k == 0), stop=False)
                    pe.matmul(psum[0:NC9, 6 + b, :], ones[0:1, 0:NC9], at(MODB + b * MB, MB, 0, 1),
                              start=False, stop=True).then_inc(s_modmm[b], 1)

                pairs(pe, first, last, pair)

            pe.wait_ge(s_silu, 2)
            pe.wait_ge(s_const, 1)
            mod_products(0, MOD_S5, (MODW0, MODW1))
            for b in range(2):
                pe.wait_ge(s_modev[b], MOD_S5 // 2)
            pe.wait_ge(s_h5, 1)
            for no, (kind, r) in enumerate(ROUNDS):
                if no >= 2:
                    wait_copied(pe, ROUNDS[no - 2])
                ps = half(no)
                if kind == "u" and r == 0:
                    pe.wait_ge(s_in, 32)
                if kind == "k" and r == 0:
                    pe.wait_ge(s_clr, 1)
                    pe.wait_ge(s_blp, 1)
                if kind == "i":
                    wait_copied(pe, ("m", r))
                    if r == 0:
                        pe.wait_ge(s_us, 16 * 2 * NB)
                        wait_copied(pe, ("u", NR - 1))
                if kind == "y" and r == 0:
                    mod_products(MOD_S5, 12, (MODW2, MODW3))
                    for b in range(2):
                        pe.wait_ge(s_modev[b], 6)
                    pe.wait_ge(s_hx, 4)
                    pe.wait_ge(s_st0, 16)
                    for q in range(NR):
                        pe.wait_ge(s_toep[q], 16 * TC)
                for gl in range(RG):
                    g = RG * r + gl
                    bank, slot = gl // 4, gl % 4
                    last = slot == 3
                    if kind == "u":
                        ins = pe.transpose(ps[0:64, bank, P * slot:P * (slot + 1)],
                                           h5[:, g].rearrange("p j q -> p (j q)"), ident)
                    elif kind == "k":
                        ins = pe.matmul(ps[0:GP, bank, P * slot:P * (slot + 1)], bl[:, g, TC - 1, :],
                                        cl[:, g, 0:TC, :], start=True, stop=True)
                    elif kind == "m":
                        ins = pe.transpose(ps[:, bank, P * slot:P * (slot + 1)],
                                           bl[:, g].rearrange("p s q -> p (s q)"), ident)
                    elif kind == "i":
                        ins = pe.matmul(ps[:, bank, UC * slot:UC * (slot + 1)], minb[r % 2][:, gl, :], u2[:, g, :],
                                        start=True, stop=True)
                    else:
                        out = ps[0:CH + NB, bank, P * slot:P * (slot + 1)]
                        pe.matmul(out, u2[:, g, 0:CH + NB], toep[:, g, :], start=True, stop=False)
                        ins = pe.matmul(out, hx[:, g, :], cl[:, g, 1:TC + 1, :], start=False, stop=True)
                ins.then_inc(s_mm, 1)
            wglu = at(CL, KD * 2 * D).rearrange("p (k n) -> p k n", k=KD)
            wait_copied(pe, ROUNDS[-1])
            for j in range(5):
                rows = P if j < 4 else NB
                z = z5[:, j, :] if j < 4 else at(MS, D, 0, NB)
                pe.wait_ge(s_gelu, j + 1)
                if j >= 2:
                    pe.wait_ge(s_zc, j - 1)
                for k in range(KD):
                    ins = pe.transpose(psum[:, 2 * (j % 2) + k // 4, P * (k % 4):P * (k % 4) + rows],
                                       z[:, P * k:P * (k + 1)], ident[0:rows, 0:rows])
                ins.then_inc(s_zt, 1)
                pe.wait_ge(s_zc, j + 1)
                if j == 0:
                    pe.wait_ge(s_wglu, 16)
                for q in range(4):
                    m = 4 * j + q
                    if m >= 2:
                        pe.wait_ge(s_ga, m - 1)
                    for k in range(KD):
                        ins = pe.matmul(psum[0:rows, 4 + m % 2, :], zt[j % 2][:, k, 0:rows],
                                        wglu[:, k, MB * q:MB * (q + 1)], start=(k == 0), stop=(k == KD - 1))
                    ins.then_inc(s_gm, 1)

            def peer_prep(t):
                R = rows_of(t)
                h = at(HT + (t % 2) * D, D, 0, R)
                pe.wait_ge(s_ph, t + 1)
                if t:
                    pe.wait_ge(s_pqc, 4 * t)
                for k in range(KD):
                    ins = pe.transpose(psum[:, 2 + k // 4, P * (k % 4):P * (k % 4) + R], h[:, P * k:P * (k + 1)],
                                       ident[0:R, 0:R])
                ins.then_inc(s_pt, 1)

                def queries(m):
                    if m < 2:
                        pe.wait_ge(s_ptc, t + 1)
                    else:
                        pe.wait_ge(s_pqc, 4 * t + m - 1)
                    if m == 0 and t % 5 == 0:
                        pe.wait_ge(s_pw, 32 * (t // 5 + 1))
                    for q in range(4):
                        for k in range(KD):
                            ins = pe.matmul(psum[:, 2 + m % 2, P * q:P * q + R],
                                            wq[:, k, P * (4 * m + q):P * (4 * m + q + 1)], htr[:, k, 0:R],
                                            start=(k == 0), stop=(k == KD - 1))
                    ins.then_inc(s_pq, 1)

                def scores(m):
                    n_ = 4 * t + m
                    pe.wait_ge(s_pqc, n_ + 1)
                    if n_ >= 2:
                        pe.wait_ge(s_psc, n_ - 1)
                    for q in range(4):
                        ins = pe.matmul(psum[0:R, 4 + m % 2, P * q:P * (q + 1)], qt[:, 4 * m + q, 0:R],
                                        keys[:, 4 * m + q, :], start=True, stop=True)
                    ins.then_inc(s_ps, 1)

                queries(0)
                for m in range(1, 4):
                    queries(m)
                    scores(m - 1)
                scores(3)

            def peer_values(t):
                R = rows_of(t)
                base = group_base(t, 1)
                acc = [psum[0:R, c, :] for c in range(2)]
                if t:
                    pe.wait_ge(s_yr, t)
                for c in range(2):
                    pe.matmul(acc[c], ident[64:65, 0:R], zrow, start=True, stop=False, skip_group_check=True)

                def product(r):
                    for c in range(2):
                        ins = pe.matmul(acc[c], diag[:, r, 0:R], ring[r][:, 512 * c:512 * (c + 1)], start=False,
                                        stop=False, skip_group_check=True)
                    ins.then_inc(freed[r], 1)

                if t % 5 < 4:
                    with pe.Fori(0, PH) as i:
                        for g in range(2):
                            for m, r in enumerate(V_PE):
                                pe.wait_ge(landed[r], 32 * i + 16 * (base + g + 1))
                                pe.wait_ge(s_dg, 2 * len(V_PE) * i + (diag_base(t) + len(V_PE) * g + m + 1))
                                product(r)
                else:
                    for r in range(RING):
                        pe.wait_ge(landed[r], 16 * (base + 1))
                        pe.wait_ge(s_dg, diag_base(t) + r + 1)
                        product(r)
                for c in range(2):
                    ins = pe.matmul(acc[c], ident[64:65, 0:R], zrow, start=False, stop=True, skip_group_check=True)
                ins.then_inc(s_yp, 1)

            def peer_pe(layer):
                t0 = 5 * layer
                peer_prep(t0)
                for b in range(5):
                    if b < 4:
                        peer_prep(t0 + b + 1)
                    peer_values(t0 + b)

            def attention_pe():
                pe.wait_ge(s_mw, 160)
                for j in range(5):
                    R = rows5(j)
                    if j:
                        pe.wait_ge(s_tqhc, j)
                    for m, (made, done) in enumerate(((s_hin, s_tx), (s_hin, s_tx))):
                        pe.wait_ge(made, 2 * j + m + 1)
                        h = at(MH + m * D, D, 0, R)
                        for k in range(KD):
                            ins = pe.transpose(psum[:, 2 * m + k // 4, P * (k % 4):P * (k % 4) + R],
                                               h[:, P * k:P * (k + 1)], ident[0:R, 0:R])
                        ins.then_inc(done, 1)
                    if j:
                        pe.wait_ge(s_kvr, 2 * j)
                    for m, (copied_, w, n_, done) in enumerate(((s_txc, wdkv, KVC, s_pr), (s_txc, wdq, QL, s_pr))):
                        pe.wait_ge(copied_, 2 * j + m + 1)
                        for k in range(KD):
                            ins = pe.matmul(psum[0:R, 4 + m, 0:n_], mht[m][:, k, 0:R], w[:, k, :], start=(k == 0),
                                            stop=(k == KD - 1))
                        ins.then_inc(done, 1)
                    kvr = at(KVR + (j % 2) * KVC, KVC, 0, R)
                    pe.wait_ge(s_kvr, 2 * j + 1)
                    if j:
                        pe.wait_ge(s_tlc, 2 * j)
                    for c in range(2):
                        pe.transpose(psum[:, 6, P * c:P * c + R], kvr[:, P * c:P * (c + 1)], ident[0:R, 0:R])
                    pe.transpose(psum[0:QKD, 6, 2 * P:2 * P + R], kvr[:, KVC - QKD:KVC], ident[0:R, 0:R]
                                 ).then_inc(s_tl, 1)
                    pe.wait_ge(s_kvr, 2 * j + 2)
                    for k in range(QL // P):
                        ins = pe.transpose(psum[:, 7, P * k:P * k + R], at(MCQ + P * k, P, 0, R), ident[0:R, 0:R])
                    ins.then_inc(s_tl, 1)
                    pe.wait_ge(s_tlc, 2 * j + 2)
                    cqt = at(MCQT, QL).rearrange("p (k t) -> p k t", k=4)
                    for c in range(3):
                        for k in range(QL // P):
                            ins = pe.matmul(psum[0:R, c, :], cqt[:, k, 0:R], wuq[:, k, 512 * c:512 * (c + 1)],
                                            start=(k == 0), stop=(k == QL // P - 1))
                    ins.then_inc(s_q, 1)
                    pe.wait_ge(s_qr, j + 1)
                    for h in range(NH):
                        ins = pe.transpose(psum[0:QKD, h // 4, P * (h % 4):P * (h % 4) + R],
                                           at(MQ + QKD * h, QKD, 0, R), ident[0:R, 0:R])
                    ins.then_inc(s_tqh, 1)
                pe.wait_ge(s_tqhc, 5)
                for c in range(2):
                    for h in range(NH):
                        ins = pe.matmul(psum[:, 5, (c * NH + h) * NB:(c * NH + h + 1) * NB],
                                        wkt[:, h, P * c:P * (c + 1)], qts[0:NOPE, h, :], start=True, stop=True)
                ins.then_inc(s_ql, 1)
                pe.wait_ge(s_tlc, 10)
                for h in range(NH):
                    if h >= 4:
                        pe.wait_ge(s_ktv if h % 2 else s_kta, (h - 4) // 2 + 1)
                    for c in range(2):
                        ins = pe.matmul(psum[0:NOPE, h % 4, :], wk[:, c, h, :], ckvt[:, c, 0:SEQ], start=(c == 0),
                                        stop=(c == 1))
                    ins.then_inc(s_ktp, 1)
                pe.wait_ge(s_qlc, 1)
                for i in range(NTILE):
                    if i >= 2:
                        pe.wait_ge(s_vc, i - 1)
                    for n_ in range(2):
                        for c in range(2):
                            ins = pe.matmul(psum[:, 4 + 2 * (i % 2) + n_, :], ckvt[:, c, P * i:P * (i + 1)],
                                            wv[:, c, 512 * n_:512 * (n_ + 1)], start=(c == 0), stop=(c == 1))
                    ins.then_inc(s_vp, 1)
                pe.wait_ge(s_kta, NH // 2)
                pe.wait_ge(s_ktv, NH // 2)
                pe.wait_ge(s_ktr, 1)
                pe.wait_ge(s_vc, NTILE)
                for n_ in range(NTILE * NH + 2):
                    if n_ < NTILE * NH:
                        i, h = divmod(n_, NH)
                        w = P * (i + 1)
                        if n_ >= 2:
                            pe.wait_ge(s_e2, n_ - 1)
                        pe.matmul(psum[:, n_ % 2, 0:w], qtm[0:QKD, h, P * i:w], kt_[0:QKD, h, 0:w], start=True,
                                  stop=False, skip_group_check=True)
                        pe.matmul(psum[:, n_ % 2, P * i:w], ident, at(MASK, P), start=False, stop=True,
                                  skip_group_check=True).then_inc(s_S, 1)
                    if 1 <= n_ <= NTILE * NH:
                        m = n_ - 1
                        pe.wait_ge(s_e2, m + 1)
                        if m >= 2:
                            pe.wait_ge(s_Tc, m - 1)
                        for k in range(m // NH + 1):
                            ins = pe.transpose(psum[:, 2 + m % 2, P * k:P * (k + 1)],
                                               at(PP + (m % 2) * SEQ + P * k, P), ident)
                        ins.then_inc(s_T, 1)
                    if n_ >= 2:
                        m = n_ - 2
                        i, h = divmod(m, NH)
                        u = m // 8
                        pe.wait_ge(s_Tc, m + 1)
                        if u >= 2 and m % 8 == 0:
                            pe.wait_ge(s_on, u - 1)
                        for k in range(i + 1):
                            ins = pe.matmul(psum[:, 4 + u % 2, VH * (m % 8):VH * (m % 8 + 1)],
                                            at(PTT + (m % 2) * SEQ + P * k, P), vv[:, k, VH * h:VH * (h + 1)],
                                            start=(k == 0), stop=(k == i))
                        ins.then_inc(s_pv, 1)
                        if h == 0 and i:
                            project(i - 1)
                project(3)
                for b in range(NB + 1):
                    if b < NB:
                        ck = CK[b % 2]
                        pe.wait_ge(s_ck[b % 2], 32 * (b // 2 + 1))
                        for q in range(5):
                            if q < 4:
                                pe.wait_ge(s_ctv if q % 2 else s_cta, 2 * b + q // 2) if 2 * b + q // 2 else None
                                for c in range(2):
                                    for r in range(4):
                                        pe.transpose(psum[:, 2 * (q % 2) + c, P * r:P * (r + 1)],
                                                     at(ck + (4 * q + r) * KVL + P * c, P), ident)
                                for r in range(4):
                                    ins = pe.transpose(psum[0:ROPE, 4 + q % 2, P * r:P * (r + 1)],
                                                       at(ck + ROWK + (4 * q + r) * ROPE, ROPE), ident)
                                ins.then_inc(s_ct, 1)
                            if q:
                                cache_scores(b, q - 1)
                        cache_scores(b, 4)
                    if b >= 1:
                        c_ = b - 1
                        sc = at(SCS[c_ % 2], NKEY, 0, NH)
                        pe.wait_ge(s_ce, c_ + 1)
                        pe.wait_ge(s_csc, 5 * min(b + 1, NB))
                        for r in range(17):
                            n_ = P if r < 16 else NB
                            ins = pe.transpose(psum[0:n_, 6, NH * r:NH * (r + 1)], sc[:, P * r:P * r + n_],
                                               ident[0:NH, 0:NH])
                        ins.then_inc(s_cT, 1)
                        pe.wait_ge(s_cTc, c_ + 1)
                        if c_:
                            pe.wait_ge(s_coc, c_)
                        ck = CK[c_ % 2]
                        for r in range(16):
                            pe.matmul(psum[0:NH, 7, 0:KVL], pts[:, r, :], at(ck + r * KVL, KVL), start=(r == 0),
                                      stop=False)
                        pe.matmul(psum[0:NH, 7, 0:KVL], pts[0:NB, 16, :], at(KVR, KVL, 0, NB), start=False,
                                  stop=True).then_inc(s_cpv, 1)
                        pe.wait_ge(s_col, c_ + 1)
                        for c in range(2):
                            ins = pe.transpose(psum[:, 7, KVL + NH * c:KVL + NH * (c + 1)],
                                               at(OL + P * c, P, 0, NH), ident[0:NH, 0:NH])
                        ins.then_inc(s_cot, 1)
                pe.wait_ge(s_coc, NB)
                for h in range(NH):
                    for c in range(2):
                        ins = pe.matmul(psum[0:NB, h // 8, VH * (h % 8):VH * (h % 8 + 1)], olt[:, c, h, :],
                                        wv[:, c, VH * h:VH * (h + 1)], start=(c == 0), stop=(c == 1))
                ins.then_inc(s_os, 1)
                project(4)

            def cache_scores(b, q):
                m = 5 * b + q
                if m >= 2:
                    pe.wait_ge(s_csc, m - 1)
                if m == 0:
                    pe.wait_ge(s_x3, 4)
                if q == 0 and b >= 2:
                    pe.wait_ge(s_coc, b - 1)
                if q < 4:
                    pe.wait_ge(s_ctv if q % 2 else s_cta, 2 * b + q // 2 + 1)
                    keys_, rot = (kts[:, :, 512 * q:512 * (q + 1)], krts[NOPE:QKD, 512 * q:512 * (q + 1)])
                    out = psum[0:NH, 6 + m % 2, :]
                else:
                    keys_, rot = ckvt[:, :, SEQ:SEQ + NB], at(KRT + SEQ, NB, NOPE, QKD)
                    out = psum[0:NH, 6 + m % 2, 0:NB]
                for c in range(2):
                    pe.matmul(out, qlt[:, c, b, :], keys_[:, c], start=(c == 0), stop=False)
                pe.matmul(out, qts[NOPE:QKD, :, b], rot, start=False, stop=True).then_inc(s_cs, 1)

            def project(j):
                R = rows5(j)
                pe.wait_ge(s_on, 2 * (j + 1) if j < 4 else 9)
                if j:
                    pe.wait_ge(s_x3, j)
                for k in range(KD):
                    ins = pe.transpose(psum[:, 6 + k // 4, P * (k % 4):P * (k % 4) + R], at(OO + P * k, P, 0, R),
                                       ident[0:R, 0:R])
                ins.then_inc(s_ot, 1)
                pe.wait_ge(s_otc, j + 1)
                pe.wait_ge(s_mw, 160 + 48)
                ot = at(OTT, D).rearrange("p (k t) -> p k t", k=KD)
                for n_ in range(2):
                    for k in range(KD):
                        ins = pe.matmul(psum[0:R, 6 + n_, :], ot[:, k, 0:R], wo[:, k, 512 * n_:512 * (n_ + 1)],
                                        start=(k == 0), stop=(k == KD - 1))
                ins.then_inc(s_yy, 1)

            mod_products(12, NMB, (MODW2, MODW3))
            for b in range(2):
                pe.wait_ge(s_modev[b], NMB // 2)
            peer_pe(0)
            attention_pe()
            peer_pe(1)


def host_inputs(i):
    f = lambda x: np.ascontiguousarray(x)
    i = {k: np.asarray(v) for k, v in i.items()}
    arr = {}
    c9 = np.concatenate([i["c_prompt"], i["c_sample"]], 0)
    arr["c_t"] = f(c9.T.reshape(KD, P, NC9).transpose(1, 0, 2)).reshape(P, KD * NC9)
    arr["consts"] = np.concatenate([np.eye(P), np.tile(np.arange(TOPK), (P, 1)),
                                    np.arange(P)[:, None] // 16 == np.arange(NB)[None]], 1).astype(np.float32)
    w = np.concatenate([i["w_mod"][0], i["w_mod"][1], i["w_mod_kv"], i["w_mod_final"]], 1)
    arr["w_mod"] = f(w.reshape(KD, P, NMB, MB).transpose(2, 1, 0, 3)).reshape(NMB, P, KD * MB)
    arr["b_mod"] = np.concatenate([i["b_mod"][0], i["b_mod"][1], i["b_mod_kv"], i["b_mod_final"]]).reshape(NMB, MB)
    twice = lambda x: np.concatenate([x, x], 0)
    cols = [twice(i["ssm_a_re"][0].T), twice(i["ssm_a_im"][0].T), np.broadcast_to(i["ssm_log_dt"][0][None], (P, G))]
    for n in ("ssm_b_re", "ssm_b_im"):
        cols.append(twice(i[n][0].transpose(1, 0, 2).reshape(N, G * GP)))
    for n in ("ssm_c_re", "ssm_c_im"):
        cols.append(twice(i[n][0].transpose(2, 0, 1).reshape(N, G * GP)))
    arr["s5_par"] = f(np.concatenate(cols, 1))
    arr["x_prompt"] = i["x_prompt"][0]
    arr["x_sample"] = i["x_sample"][:, 0]
    arr["g_norm"] = i["g_norm"].reshape(4, D)
    arr["ssm_d"] = i["ssm_d"].reshape(1, D)
    st = np.stack([i["state_ssm_re"][0], i["state_ssm_im"][0]])
    arr["state_x"] = f(st.transpose(0, 3, 2, 1)).reshape(P, G, NB)
    arr["state_g"] = f(st.reshape(2, NB, G // 2, 2, N).transpose(3, 4, 0, 2, 1)).reshape(P, G * NB)
    wg = i["ssm_w_glu"][0].reshape(KD, P, 2, 4, 256)
    arr["w_glu"] = f(wg.transpose(1, 0, 3, 2, 4)).reshape(P, KD * 2 * D)
    arr["peer_wq"] = f(i["peer_w_q"].reshape(2, KD, P, HQ).transpose(0, 2, 1, 3)).reshape(2, P, KD * HQ)
    arr["peer_keys"] = f(i["peer_keys"].transpose(0, 4, 1, 2, 3)).reshape(2, P, 2 * PH * P)
    for l in range(2):
        arr[f"peer_u{l}"], arr[f"peer_v{l}"] = i["peer_u"][l], i["peer_v"][l]
    arr["w_dkv"] = f(np.concatenate([i["w_dkv"], i["w_kr"]], 1).reshape(KD, P, KVL + ROPE).transpose(1, 0, 2)
                     ).reshape(P, -1)
    arr["w_dq"] = f(i["w_dq"][0].reshape(KD, P, QL).transpose(1, 0, 2)).reshape(P, -1)
    arr["w_uq"] = f(i["w_uq"][0].reshape(QL // P, P, NH * QKD).transpose(1, 0, 2)).reshape(P, -1)
    ukv = i["w_ukv"].reshape(2, P, NH, NOPE + VH)
    arr["w_k"] = f(ukv[..., :NOPE].transpose(1, 0, 2, 3)).reshape(P, -1)
    arr["w_v"] = f(ukv[..., NOPE:].transpose(1, 0, 2, 3)).reshape(P, -1)
    arr["w_kt"] = f(i["w_ukv"][..., :NOPE].transpose(2, 1, 0)).reshape(NOPE, -1)
    arr["w_o"] = f(i["w_o"][0].reshape(KD, P, D).transpose(1, 0, 2)).reshape(P, -1)
    inv = (np.float32(10000.0) ** (-np.arange(0, ROPE, 2, dtype=np.float32) / np.float32(ROPE))).astype(np.float32)
    pos = np.concatenate([np.arange(SEQ), np.full(P, PAST)]).astype(np.float32)
    ang = pos[:, None] * inv
    cs = np.stack([np.cos(ang), np.sin(ang)], 1).astype(np.float32).reshape(5, P, ROPE).transpose(1, 0, 2)
    mask = np.where(np.arange(P)[None] <= np.arange(P)[:, None], 0, -1e30)
    smask = np.tile(np.where(np.eye(NB) > 0, 0, -1e30).reshape(1, -1), (P, 1))
    arr["rope_mask"] = np.concatenate([cs.reshape(P, -1), mask, smask, np.arange(P)[:, None] % 8], 1
                                      ).astype(np.float32)
    arr["pages"] = f(np.repeat(i["page_table"], 8, 1).T).astype(np.int32)
    arr["g_ckv"], arr["g_cq"] = i["g_ckv"].reshape(1, KVL), i["g_cq"].reshape(1, QL)
    arr["g_kv_norm"], arr["g_final"] = i["g_kv_norm"].reshape(1, D), i["g_final"].reshape(1, D)
    arr["cache_kv"] = i["cache_kv_latent"].reshape(-1, 16 * KVL)
    arr["cache_kr"] = i["cache_k_rope"].reshape(-1, 16 * ROPE)
    return arr


def kernel(**inputs):
    from concourse import bacc
    from concourse.bass_utils import run_bass_kernel_spmd

    arrays = host_inputs(inputs)
    nc = bacc.Bacc("TRN2", target_bir_lowering=False, num_devices=1)
    a = {n: nc.dram_tensor(n, x.shape, mybir.dt.from_np(x.dtype), kind="ExternalInput").ap()
         for n, x in arrays.items()}
    outs = {"out_ssm_p": (P, G), "out_ssm_s": (P, G * NB), "out_kv_p": (SEQ, KVL), "out_kr_p": (SEQ, ROPE),
            "out_kv_s": (NB, KVL), "out_kr_s": (NB, ROPE), "out_y_p": (SEQ, D), "out_y_s": (NB, D)}
    for n, shape in outs.items():
        a[n] = nc.dram_tensor(n, shape, F32, kind="ExternalOutput").ap()
    program(nc, a)
    r = run_bass_kernel_spmd(nc, [arrays], core_ids=[0]).results[0]
    p = r["out_ssm_p"].reshape(2, N, 2, G // 2).transpose(2, 3, 0, 1).reshape(2, 1, 1, G, N)
    s = r["out_ssm_s"].reshape(2, N, 2, G // 2, NB).transpose(2, 4, 3, 0, 1).reshape(2, 1, NB, G, N)
    return (r["out_y_p"].reshape(1, SEQ, D), r["out_y_s"].reshape(NB, 1, D), p[0], p[1],
            r["out_kv_p"].reshape(1, SEQ, KVL), r["out_kr_p"].reshape(1, SEQ, ROPE), s[0], s[1],
            r["out_kv_s"].reshape(NB, 1, KVL), r["out_kr_s"].reshape(NB, 1, ROPE))
```

```python
from contextlib import ExitStack

import numpy as np

import concourse.bass as bass
from concourse import mybir

F32 = mybir.dt.float32
I32 = mybir.dt.int32
U32 = mybir.dt.uint32
ALU = mybir.AluOpType
ACT = mybir.ActivationFunctionType
AX = mybir.AxisListType

P = 128
D = 1024
KD = D // P
SEQ = 512
NTILE = SEQ // P
NB = 8
NC9 = 1 + NB
EPS = 1e-6
G = 64
GP = 16
N = 64
TC = 8
CH = SEQ // TC
UC = CH + 2 * NB
RG = 16
PH = 8
N_KEYS = 128
TOPK = 16
HQ = PH * 2 * P
N_EXP = N_KEYS * N_KEYS
RING = 8
NH = 16
NOPE = 64
ROPE = 32
QKD = NOPE + ROPE
VH = 64
QL = 512
KVL = 256
PAST = 2048
SM_SCALE = QKD ** -0.5
NR = G // RG
MB = 512
NMB = 32
MOD_S5 = 4
MOD_ONE = 10
MOD_TWO = 28
HALF_MOD = KD * MB // 2


def program(nc, a):
    with ExitStack() as ctx:
        sem_names = {}

        def sem(name):
            sem_names[name] = ctx.enter_context(nc.semaphore(name))
            return sem_names[name]

        ARENA = 53200
        arena = ctx.enter_context(nc.sbuf_tensor("arena", [P, ARENA], F32))
        psum = ctx.enter_context(nc.psum_tensor("psum", [P, 8, 512], F32))

        def at(off, n, p0=0, p1=P):
            assert off + n <= ARENA, (off, n)
            return arena[p0:p1, off:off + n]

        def scratch(name, shape):
            return nc.dram_tensor(name, shape, F32, kind="Internal").ap()

        mod_dram = scratch("mod_rows", (NC9, NMB * MB))
        hs_dram = scratch("s5_sample_in", (NB, D))
        x1_dram = scratch("x_after_mixer", (SEQ, D))
        x1s_dram = scratch("xs_after_mixer", (NB, D))
        x3_dram = scratch("x_after_attention", (SEQ, D))
        x3s_dram = scratch("xs_after_attention", (NB, D))
        x2_dram = scratch("x_after_layer0", (SEQ, D))
        x2s_dram = scratch("xs_after_layer0", (NB, D))

        o = 0
        IDENT = o; o += P
        IOTA = o; o += TOPK
        SEL = o; o += NB
        SILU = o; o += KD * NC9
        ONES = o; o += 16
        STAT = o; o += 64
        MODB = o; o += 2 * MB
        LAMT = o; o += 8 * (G // 2)
        ST0 = o; o += 2 * (G // 2) * NB
        MODO = MODB
        R32 = 32
        FIXED_END = o
        CL = o; o += G * (TC + 1) * GP
        TOEP = o; o += G * P
        BL = o; o += G * P
        MINB = o; o += 2 * RG * P
        U2 = o; o += G * UC
        HX = o; o += G * (CH + NB)
        SJ = o; o += CH * 2 * (G // 2) + NB * 2 * (G // 2)
        H5 = o; o += (TC // 2) * D
        MA = o; o += D
        MS = o; o += D
        assert o <= ARENA, o
        HPX = BL
        PARAM = U2
        NPAR = 3 * G + 4 * G * GP
        assert NPAR <= G * UC
        KSB = HX
        TAB = MINB
        TMP = SJ
        MODW0, MODW1 = TOEP, TOEP + 4096
        MODW2, MODW3 = MINB, HX
        MOD_PLACES = [[(w, w + HALF_MOD) for w in pair] for pair in ((MODW0, MODW1), (MODW2, MODW3))]

        ident = at(IDENT, P)
        silu = at(SILU, KD * NC9).rearrange("p (k r) -> p k r", k=KD)
        ones = at(ONES, 16)
        cl = at(CL, G * (TC + 1) * GP).rearrange("p (g t q) -> p g t q", g=G, t=TC + 1)
        bl = at(BL, G * P).rearrange("p (g s q) -> p g s q", g=G, s=TC)
        toep = at(TOEP, G * P).rearrange("p (g m) -> p g m", g=G)
        u2 = at(U2, G * UC).rearrange("p (g c) -> p g c", g=G)
        hx = at(HX, G * (CH + NB)).rearrange("p (g c) -> p g c", g=G)
        minb = [at(MINB + i * RG * P, RG * P).rearrange("p (g m) -> p g m", g=RG) for i in range(2)]
        ksb = [at(KSB + i * RG * P, RG * P, 0, GP).rearrange("p (g m) -> p g m", g=RG) for i in range(2)]
        sj = at(SJ, CH * G).rearrange("p (c k g) -> p c k g", c=CH, k=2)
        si = at(SJ + CH * G, NB * G).rearrange("p (k g b) -> p k g b", k=2, g=G // 2)
        hpx = at(HPX, (CH + 1) * 3 * (G // 2)).rearrange("p (c m) -> p c m", c=CH + 1)
        h5 = at(H5, (TC // 2) * D).rearrange("p (g j q) -> p g j q", g=G, j=TC // 2)
        x5 = at(U2, (TC // 2) * D).rearrange("p (j d) -> p j d", j=TC // 2)
        z5 = at(SJ, (TC // 2) * D).rearrange("p (j d) -> p j d", j=TC // 2)
        mod_a, mod_s = at(MA, D), at(MS, D)

        par = at(PARAM, NPAR)
        a_re, a_im, log_dt = par[:, 0:G], par[:, G:2 * G], par[:, 2 * G:3 * G]
        b_re, b_im, c_re, c_im = (par[:, 3 * G + i * D:3 * G + (i + 1) * D].rearrange("p (g q) -> p g q", g=G)
                                  for i in range(4))

        t9 = (TC + 1) * G
        pw_re = at(TAB, t9).rearrange("p (t g) -> p t g", t=TC + 1)
        pw_im = at(TAB + t9, t9).rearrange("p (t g) -> p t g", t=TC + 1)
        ca = at(TAB + 2 * t9, t9).rearrange("p (t g) -> p t g", t=TC + 1)
        cb = at(TAB + 3 * t9, t9).rearrange("p (t g) -> p t g", t=TC + 1)
        bb = at(TAB + 4 * t9, t9).rearrange("p (t g) -> p t g", t=TC + 1)
        small = [at(TAB + 5 * t9 + i * G, G) for i in range(16)]
        assert 5 * t9 + 16 * G <= 2 * RG * P
        bbar_re = at(TMP, D).rearrange("p (g q) -> p g q", g=G)
        bbar_im = at(TMP + D, D).rearrange("p (g q) -> p g q", g=G)
        tmp_v = at(TMP + 2 * D, D).rearrange("p (g q) -> p g q", g=G)
        tmp_g = at(TMP + 3 * D, D).rearrange("p (g q) -> p g q", g=G)
        HALF = G // 2
        lamt = at(LAMT, 8 * HALF)
        st0 = at(ST0, 2 * HALF * NB).rearrange("p (k g b) -> p k g b", k=2, g=HALF)
        stat = at(STAT, 64)

        s_in = sem("inputs_loaded")
        s_par = sem("s5_params_loaded")
        s_silu = sem("silu_ready")
        s_const = sem("constants_ready")
        s_modw = [sem(f"mod_weights_loaded{i}") for i in range(2)]
        s_modmm = [sem(f"mod_products_done{i}") for i in range(2)]
        s_modev = [sem(f"mod_rows_copied{i}") for i in range(2)]
        s_dt = sem("dt_ready")
        s_half = sem("half_angle_ready")
        s_sin = sem("half_angle_sines_ready")
        s_modst = [sem(f"mod_rows_stored{i}") for i in range(2)]
        vec = sem("vector_step")
        act_step = sem("scalar_step")
        pool_step = sem("pool_step")
        s_tabs = sem("b_factors_ready")
        s_blp = sem("bl_ready")
        s_clr = sem("cl_ready")
        s_x5 = sem("chunk_rows_loaded")
        s_mods5 = sem("s5_mods_loaded")
        s_sq = sem("row_squares_summed")
        s_ms = sem("row_means_ready")
        s_rt = sem("row_roots_ready")
        s_rld = [sem(f"rows_loaded{i}") for i in range(2)]
        s_rst = [sem(f"rows_stored{i}") for i in range(2)]
        s_h5 = sem("s5_input_ready")
        s_hst = sem("s5_sample_in_stored")
        s_us = sem("sample_columns_loaded")
        s_tz = sem("response_and_chunk_pad_cleared")
        s_toep = [sem(f"response_loaded{r}") for r in range(NR)]
        s_mm = sem("s5_round_products")
        s_evA = sem("s5_round_copied_by_scalar")
        s_evV = sem("s5_round_copied_by_vector")
        s_scan = sem("scan_step")
        s_scd = sem("scan_done")
        s_dld = sem("skip_loaded")
        s_st0 = sem("sample_state_loaded")
        s_hx = sem("states_placed")
        s_gelu = sem("gelu_ready")
        s_wglu = sem("glu_weights_loaded")
        s_lw = sem("late_weights_loaded")
        s_zt = sem("glu_transposes")
        s_zc = sem("glu_transposes_copied")
        s_gm = sem("glu_products")
        s_sg = sem("glu_gate_ready")
        s_ga = sem("glu_block_ready")
        s_x1 = sem("mixer_out_ready")
        s_out = sem("outputs_stored")

        NORMS = [("s5", 0)] + [("peer0", j) for j in range(5)] + [("attention", j) for j in range(5)] + [("peer1", 0)]
        for j in range(5):
            NORMS += ([("peer1", j + 1)] if j < 4 else []) + [("final", j)]

        def norm_no(stage, j):
            return NORMS.index((stage, j)) + 1

        LATE_GLU, LATE_Q, LATE_HEADS = 16, (48, 128), 96

        LOADS = ("peer0", "attention", "residual", "peer1")
        STORES = ("peer0", "residual", "peer1")

        def row_slot(stage, j):
            return (j + (stage == "peer1")) % 2

        def row_no(passes, stage, j):
            slot = row_slot(stage, j)
            before = sum(row_slot(q, m) == slot for q in passes[:passes.index(stage)] for m in range(5))
            return 16 * (before + sum(row_slot(stage, m) == slot for m in range(j + 1)))

        ROUNDS = ([("u", r) for r in range(NR)] + [("k", r) for r in range(NR)]
                  + [("m", 0), ("m", 1), ("i", 0), ("m", 2), ("i", 1), ("m", 3), ("i", 2), ("i", 3)]
                  + [("y", r) for r in range(NR)])
        WHO = {"u": "A", "k": "A", "m": "A", "i": "V", "y": "V"}
        round_no = {key: n for n, key in enumerate(ROUNDS)}
        copied = {}
        for who in "AV":
            mine = [key for key in ROUNDS if WHO[key[0]] == who]
            for n, key in enumerate(mine):
                copied[key] = (who, n + 1)

        def wait_copied(eng, key):
            who, n = copied[key]
            eng.wait_ge(s_evA if who == "A" else s_evV, n)

        def half(n):
            return psum[:, 4 * (n % 2):4 * (n % 2) + 4, :]

        def pairs(eng, first, last, pair):
            if first == 0:
                for b in range(2):
                    pair(0, b, True)
            with eng.Fori(first // 2 + (first == 0), last // 2) as i:
                for b in range(2):
                    pair(i, b)

        hpv = hpx[:, 0:CH, :].rearrange("p c (k g) -> p k g c", k=3)
        hxv = hx[:, :, 0:CH].rearrange("p (g two) c -> p two g c", two=2)
        zt = [at(U2 + i * D, D).rearrange("p (k t) -> p k t", k=KD) for i in range(2)]
        gate = [at(U2 + 2 * D + i * 256, 256) for i in range(2)]
        glu_t = [at(U2 + 2 * D + 512 + i * D, D) for i in range(2)]
        QW = KD * MB
        wglu_at = [at(MINB, QW)] + [at(CL + q * QW, QW) for q in range(3)]
        scan_tmp = at(MA, 4 * HALF)
        sj_tmp = at(MA + 4 * HALF, HALF * NB).rearrange("p (g b) -> p g b", g=HALF)

        o = FIXED_END
        WQ = o; o += KD * HQ
        KEYS = o; o += 2 * PH * P
        RINGP = o; o += RING * D
        XT = o; o += 2 * D
        HT = o; o += 2 * D
        HTR = o; o += D
        QT = o; o += 2 * PH * P
        PMOD = o; o += 6 * D
        SSB = o; o += 2 * PH * P
        TOPV = o; o += 64
        TOPI = o; o += 64
        CAND = o; o += 256
        ONEH = o; o += 512
        BV = o; o += PH * TOPK
        BP = o; o += 32
        AB = o; o += 64
        IDXP = o; o += 2 * P
        PG = o; o += 2 * P
        DOTS = o; o += 2 * P
        DIAG = o; o += RING * P
        YACC = o; o += D
        PTMP = o; o += 2 * D
        IX8 = o; o += 2 * RING
        IXS = o; o += RING
        GS = o; o += RING
        assert o <= ARENA, o
        PEER_END = o

        def rows_of(t):
            return P if t % 5 < 4 else NB

        wq = at(WQ, KD * HQ).rearrange("p (m k n) -> p m k n", m=4, k=KD)
        keys = at(KEYS, 2 * PH * P).rearrange("p (h n) -> p h n", h=2 * PH)
        ring = [at(RINGP + r * D, D) for r in range(RING)]
        qt = at(QT, 2 * PH * P).rearrange("p (h t) -> p h t", h=2 * PH)
        htr = at(HTR, D).rearrange("p (k t) -> p k t", k=KD)
        ssb = at(SSB, 2 * PH * P).rearrange("p (h n) -> p h n", h=2 * PH)
        diag = at(DIAG, RING * P).rearrange("p (r n) -> p r n", r=RING)
        iota16, sel8 = at(IOTA, TOPK), at(SEL, NB)
        zrow = at(MODB, 512, 64, 65)
        idx_dram = nc.dram_tensor("sample_idx", (NB, P), I32, kind="Internal").ap()
        gw_dram = scratch("sample_gates", (NB, P))
        ph_dram = scratch("peer_sample_in", (NB, D))

        s_pw = sem("peer_weights_loaded")
        s_pmod = sem("peer_mods_loaded")
        s_pmr = sem("peer_mods_ready")
        s_ph = sem("peer_input_ready")
        s_pt = sem("peer_input_transposed")
        s_ptc = sem("peer_transposes_copied")
        s_pq = sem("query_products")
        s_pqc = sem("queries_copied")
        s_ps = sem("key_scores")
        s_psc = sem("key_scores_copied")
        s_idx = sem("head_experts_ready")
        s_bv = sem("expert_scores_shifted")
        s_ex = sem("expert_exps_ready")
        s_g = sem("gates_ready")
        s_dots = sem("expert_dots_ready")
        s_act = sem("expert_acts_ready")
        s_w = sem("expert_weights_ready")
        s_go = sem("gather_slot_found_free")
        s_ix8 = sem("group_indices_copied")
        landed = [sem(f"expert_row_landed{r}") for r in range(RING)]
        freed = [sem(f"expert_row_used{r}") for r in range(RING)]
        s_dg = sem("weight_diagonals_ready")
        s_yp = sem("peer_sum_closed")
        s_yr = sem("peer_sum_read")
        s_xn = sem("peer_out_ready")
        s_sdr = sem("sample_rows_stored")
        s_sld = sem("sample_experts_spread")
        s_gs = sem("sample_gates_spread")
        s_shs = sem("sample_input_stored")
        s_shb = sem("sample_input_spread")
        s_z = sem("zero_row_ready")

        def group_base(t, phase):
            layer, b = divmod(t, 5)
            per = 2 * NTILE * P // RING + 2
            return layer * per + (b * 2 + phase) * (P // RING) if b < 4 else \
                layer * per + 2 * NTILE * P // RING + phase

        V_DVE = (1, 4, 7)
        V_PE = tuple(r for r in range(RING) if r not in V_DVE)

        def diag_base(t):
            layer, b = divmod(t, 5)
            return (layer * 4 + b) * (P // RING) * len(V_PE) + layer * RING

        def ix8_base(t, phase):
            layer, b = divmod(t, 5)
            return ((layer * 4 + b) * 2 + phase) * (P // RING)

        KVC = KVL + ROPE
        o = FIXED_END
        WDKV = o; o += KD * KVC
        WDQ = o; o += KD * QL
        WUQ = o; o += (QL // P) * NH * QKD
        MMOD = o; o += 4 * D
        CSN = o; o += 5 * ROPE
        MASK = o; o += P
        SMASK = o; o += NB * NB
        SUB = o; o += 1 + NB
        GCKV = o; o += KVL
        GCQ = o; o += QL
        assert o <= KEYS + 2 * PH * P
        KT = WDKV
        WO = KT + NH * SEQ
        assert WO + KD * D <= o
        QTM = o; o += NH * SEQ
        VV = o; o += NTILE * NH * VH
        WKT = VV
        WK = o; o += 2 * NH * NOPE
        WV = o; o += 2 * NH * VH
        CKVT = o; o += 2 * (SEQ + NB)
        KRT = o; o += SEQ + NB
        KVR = o; o += 2 * KVC
        MX = o; o += 2 * D
        MH = o; o += 2 * D
        MHT = o; o += 2 * D
        MCQ = o; o += QL
        MCQT = o; o += QL
        MQ = o; o += NH * QKD
        SC1 = MCQ
        PP = o; o += 2 * SEQ
        PTT = o; o += 2 * SEQ
        OO = o; o += D
        OTT = o; o += D
        QTS = o; o += NH * NB
        QLT = o; o += 2 * NB * NH
        SUMS = o; o += 32
        PTS = o; o += 17 * NH
        OL = o; o += KVL
        OLT = o; o += 2 * NH * NB
        RT = o; o += 1
        assert o <= ARENA, o
        ROWK = KVL * 16
        ROWR = ROPE * 16
        CK = [QTM, QTM + ROWK + ROWR]
        SC0 = QTM + 2 * (ROWK + ROWR)
        NKEY = PAST + NB
        assert SC0 + NKEY <= WK and NKEY <= 2 * QL + NH * QKD
        SCS = [SC0, SC1]
        KTS = KT
        KRTS = KT + 2 * PAST
        assert KRTS + PAST <= WO
        wdkv = at(WDKV, KD * KVC).rearrange("p (k n) -> p k n", k=KD)
        wdq = at(WDQ, KD * QL).rearrange("p (k n) -> p k n", k=KD)
        wuq = at(WUQ, (QL // P) * NH * QKD).rearrange("p (k n) -> p k n", k=QL // P)
        kt_ = at(KT, NH * SEQ).rearrange("p (h t) -> p h t", h=NH)
        wo = at(WO, KD * D).rearrange("p (k n) -> p k n", k=KD)
        qtm = at(QTM, NH * SEQ).rearrange("p (h t) -> p h t", h=NH)
        qts = at(QTS, NH * NB).rearrange("p (h b) -> p h b", h=NH)
        qlt = at(QLT, 2 * NB * NH).rearrange("p (c b h) -> p c b h", c=2, b=NB)
        vv = at(VV, NTILE * NH * VH).rearrange("p (i n) -> p i n", i=NTILE)
        wkt = at(WKT, NH * KVL, 0, NOPE).rearrange("p (h c) -> p h c", h=NH)
        wk = at(WK, 2 * NH * NOPE).rearrange("p (c n) -> p c n", c=2)
        wv = at(WV, 2 * NH * VH).rearrange("p (c n) -> p c n", c=2)
        ckvt = at(CKVT, 2 * (SEQ + NB)).rearrange("p (c t) -> p c t", c=2)
        csn = at(CSN, 5 * ROPE).rearrange("p (i k m) -> p i k m", i=5, k=2)
        kts = at(KTS, 2 * PAST).rearrange("p (c t) -> p c t", c=2)
        krts = at(KRTS, PAST)
        pts = at(PTS, 17 * NH).rearrange("p (r h) -> p r h", r=17)
        olt = at(OLT, 2 * NH * NB).rearrange("p (c h b) -> p c h b", c=2, h=NH)
        mht = [at(MHT + i * D, D).rearrange("p (k t) -> p k t", k=KD) for i in range(2)]

        s_mw = sem("attention_weights_loaded")
        s_mm1 = sem("attention_mods_loaded")
        s_mmr = sem("attention_mods_ready")
        s_hin = sem("attention_inputs_ready")
        s_tx = sem("attention_inputs_transposed")
        s_txc = sem("attention_input_transposes_copied")
        s_pr = sem("latent_products")
        s_tl = sem("latents_transposed")
        s_tlc = sem("latent_transposes_copied")
        s_lsq = sem("latent_squares_ready")
        s_lmn = sem("latent_means_ready")
        s_lrt = sem("latent_roots_ready")
        s_kvr = sem("latents_ready")
        s_kvs = [sem(f"latents_stored{i}") for i in range(2)]
        s_q = sem("head_query_products")
        s_qc = sem("head_queries_copied")
        s_qr = sem("head_queries_rotated")
        s_tqh = sem("head_queries_transposed")
        s_tqhc = sem("head_transposes_copied")
        s_ql = sem("sample_latent_queries")
        s_qlc = sem("sample_latent_queries_copied")
        s_ktp = sem("head_key_products")
        s_kta = sem("head_keys_copied_by_scalar")
        s_ktv = sem("head_keys_copied_by_vector")
        s_ktr = sem("rotary_keys_spread")
        s_vp = sem("value_products")
        s_vc = sem("values_copied")
        s_S = sem("scores_ready")
        s_nm = sem("score_maximum_ready")
        s_e2 = sem("probabilities_ready")
        s_T = sem("probabilities_transposed")
        s_Tc = sem("probability_transposes_copied")
        s_pv = sem("head_outputs")
        s_on = sem("head_outputs_scaled")
        s_ot = sem("outputs_transposed")
        s_otc = sem("output_transposes_copied")
        s_yy = sem("output_products")
        s_x3 = sem("attention_out_ready")
        s_pix = sem("page_rows_ready")
        s_ck = [sem(f"cache_rows_landed{i}") for i in range(2)]
        s_ct = sem("cache_rows_transposed")
        s_cta = sem("cache_transposes_copied_by_scalar")
        s_ctv = sem("cache_transposes_copied_by_vector")
        s_cs = sem("sample_scores")
        s_csc = sem("sample_scores_copied")
        s_cnm = sem("sample_maximum_ready")
        s_ce = sem("sample_probabilities_ready")
        s_cT = sem("sample_probabilities_transposed")
        s_cTc = sem("sample_transposes_copied")
        s_cpv = sem("sample_latent_outputs")
        s_col = sem("sample_latent_outputs_scaled")
        s_cot = sem("sample_outputs_transposed")
        s_coc = sem("sample_output_transposes_copied")
        s_os = sem("sample_head_outputs")

        def rows5(j):
            return P if j < 4 else NB

        FMOD = PEER_END
        FG = FMOD + 2 * D
        FMODS = PMOD
        FSQ = PTMP + D
        assert FG + D <= ARENA
        MOD_PLACES.append([(DIAG, FMOD)] * 2)
        assert YACC == DIAG + RING * P and HALF_MOD <= YACC + D - DIAG and FMOD + HALF_MOD <= ARENA

        def out_no(t):
            return t + 1 if t < 5 else 5 + 2 * (t - 5) + 1

        block = ctx.enter_context(nc.Block())

        @block.sync
        def _(sp):
            sp.dma_start(at(SILU, KD * NC9), a["c_t"]).then_inc(s_in, 16)
            sp.dma_start(at(IDENT, P + TOPK + NB), a["consts"]).then_inc(s_in, 16)
            sp.dma_start(par, a["s5_par"]).then_inc(s_par, 16)

            def mod_loads(first, last, places, shared=False):
                def pair(i, b, fresh=False):
                    w = a["w_mod"][bass.ds(2 * i + b, 1), :, :].rearrange("o p n -> (o p) n")
                    for k in range(2):
                        if shared:
                            sp.wait_ge(s_modmm[1 - b], 2 * i + (2 * b - 1 + k))
                        elif not fresh:
                            sp.wait_ge(s_modmm[b], 2 * i - 1 + k)
                        sp.dma_start(at(places[b][k], HALF_MOD), w[:, k * HALF_MOD:(k + 1) * HALF_MOD]
                                     ).then_inc(s_modw[b], 16)
                    sp.dma_start(at(MODB + b * MB, MB, 0, 1), a["b_mod"][bass.ds(2 * i + b, 1), :]
                                 ).then_inc(s_modw[b], 16)

                pairs(sp, first, last, pair)

            mod_loads(0, MOD_S5, MOD_PLACES[0])
            x5v = a["x_prompt"].rearrange("(c s j) d -> s c (j d)", s=2, j=TC // 2)
            sp.dma_start(at(ST0, 2 * HALF * NB), a["state_g"]).then_inc(s_x5, 16)
            for b in range(2):
                sp.wait_ge(s_modst[b], 16 * (MOD_S5 // 2))
            sp.dma_start(mod_s, mod_dram[0:1, 0:D].partition_broadcast(P)).then_inc(s_mods5, 16)
            sp.dma_start(mod_a, mod_dram[0:1, D:2 * D].partition_broadcast(P)).then_inc(s_mods5, 16)
            mod_loads(MOD_S5, MOD_ONE, MOD_PLACES[0])
            sp.wait_ge(s_clr, 1)
            sp.wait_ge(s_blp, 1)
            for s in range(2):
                sp.dma_start(at(U2, 4 * D, 64 * s, 64 * s + 64), x5v[s]).then_inc(s_x5, 16)
            sp.dma_start(at(TMP, D), a["g_norm"][0:1, :].partition_broadcast(P)).then_inc(s_mods5, 16)
            sp.dma_start(at(TMP + D, D, 0, NB), a["x_sample"]).then_inc(s_mods5, 16)
            sp.dma_start(at(TMP + 2 * D, D, 0, NB), mod_dram[1:NC9, 0:D]).then_inc(s_mods5, 16)
            sp.dma_start(at(TMP + 3 * D, D, 0, NB), mod_dram[1:NC9, D:2 * D]).then_inc(s_mods5, 16)
            sp.wait_ge(s_h5, 2)
            sp.dma_start(hs_dram, at(TMP + D, D, 0, NB)).then_inc(s_hst, 16)
            sp.dma_start(mod_a, a["ssm_d"].partition_broadcast(P)).then_inc(s_dld, 16)
            sp.wait_ge(s_hst, 16)
            sp.wait_ge(s_tz, 2)
            hsv = hs_dram.rearrange("b (g p) -> p g b", p=GP)
            for b in range(NB):
                for k, rows in enumerate((slice(0, GP), slice(P - GP, P))):
                    sp.dma_start(u2[rows, :, CH + k * NB + b], hsv[:, :, b],
                                 allow_slow_non_contiguous=True).then_inc(s_us, 16)
            sp.wait_ge(s_tz, 1)
            for r in range(NR):
                wait_copied(sp, ("k", r))
                for s in range(TC):
                    sp.dma_start(toep[GP * s:GP * (s + 1), RG * r:RG * (r + 1), GP * s:P],
                                 ksb[r % 2][:, :, 0:P - GP * s]).then_inc(s_toep[r], 16)
            wait_copied(sp, ("i", NR - 1))
            for r in range(NR):
                sp.wait_ge(s_toep[r], 16 * TC)
            mod_loads(MOD_ONE, MOD_TWO, MOD_PLACES[1])
            for b in range(2):
                sp.wait_ge(s_modmm[b], MOD_TWO)
            sp.dma_start(hx[:, :, CH:CH + NB], a["state_x"]).then_inc(s_st0, 16)
            sp.dma_start(wglu_at[0], a["w_glu"][:, 0:QW]).then_inc(s_wglu, 16)
            sp.wait_ge(s_scd, 1)
            sp.dma_start(a["out_ssm_p"], hpx[:, CH, 0:2 * HALF]).then_inc(s_out, 16)
            sp.wait_ge(s_scd, 2)
            sp.dma_start(a["out_ssm_s"], at(SJ + CH * G, NB * G)).then_inc(s_out, 16)
            wait_copied(sp, ("y", NR - 1))
            sp.wait_ge(s_wglu, 16)
            for q in range(1, 4):
                sp.dma_start(wglu_at[q], a["w_glu"][:, QW * q:QW * (q + 1)]).then_inc(s_lw if q == 1 else s_wglu, 16)
            sp.wait_ge(s_out, 32)
            for s in range(2):
                sp.dma_start(at(BL, 4 * D, 64 * s, 64 * s + 64), x5v[s]).then_inc(s_x5, 16)
            sp.dma_start(at(BL + 4 * D, D, 0, NB), a["x_sample"]).then_inc(s_x5, 16)
            sp.dma_start(at(BL + 5 * D, D, 0, NB), mod_dram[1:NC9, 2 * D:3 * D]).then_inc(s_x5, 16)
            sp.dma_start(mod_a, mod_dram[0:1, 2 * D:3 * D].partition_broadcast(P)).then_inc(s_x5, 16)
            x1v = x1_dram.rearrange("(c s j) d -> s j c d", s=2, j=TC // 2)
            for j in range(TC // 2):
                sp.wait_ge(s_x1, j + 1)
                for s in range(2):
                    sp.dma_start(x1v[s, j], at(BL + j * D, D, 64 * s, 64 * s + 64)).then_inc(s_out, 16)
            sp.wait_ge(s_x1, 5)
            sp.dma_start(x1s_dram, at(BL + 4 * D, D, 0, NB)).then_inc(s_out, 16)
            sp.wait_ge(s_out, 32 + 16 * 9)
            for b in range(2):
                sp.wait_ge(s_modst[b], 16 * (MOD_TWO // 2))

            def peer_loads(layer):
                c0 = (layer * 6 + 3) * D
                sp.dma_start(at(PMOD, 3 * D), mod_dram[0:1, c0:c0 + 3 * D].partition_broadcast(P)
                             ).then_inc(s_pmod, 16)
                sp.dma_start(at(PMOD + 3 * D, 3 * D, 0, NB), mod_dram[1:NC9, c0:c0 + 3 * D]).then_inc(s_pmod, 16)
                sp.dma_start(at(PTMP, D), a["g_norm"][2 * layer + 1:2 * layer + 2, :].partition_broadcast(P)
                             ).then_inc(s_pmod, 16)

            def final_loads():
                sp.dma_start(at(FMOD, 2 * D), mod_dram[0:1, 14 * D:16 * D].partition_broadcast(P)
                             ).then_inc(s_mm1, 16)
                sp.dma_start(at(FG, D), a["g_final"].partition_broadcast(P)).then_inc(s_mm1, 16)

            def peer_weights(layer, m):
                n_ = KD * HQ // 4
                sp.dma_start(at(WQ + m * n_, n_), a["peer_wq"][layer][:, m * n_:(m + 1) * n_]
                             ).then_inc(s_pw if m < 2 else s_lw, 16)

            def peer_keys(layer):
                sp.dma_start(at(KEYS, 2 * PH * P), a["peer_keys"][layer]).then_inc(s_pw, 16)

            def peer_tiles(layer, x_in, xs_in, x_out, xs_out, meanwhile=None):
                stage = f"peer{layer}"

                def load(t):
                    b = t % 5
                    if t % 5 >= 2:
                        sp.wait_ge(s_rst[t % 2], row_no(STORES, stage, b - 2))
                    src = x_in[P * b:P * (b + 1)] if b < 4 else xs_in
                    sp.dma_start(at(XT + (t % 2) * D, D, 0, rows_of(t)), src).then_inc(s_rld[t % 2], 16)

                def store(t):
                    b = t % 5
                    sp.wait_ge(s_xn, out_no(t) + layer)
                    dst = x_out[P * b:P * (b + 1)] if b < 4 else xs_out
                    sp.dma_start(dst, at(XT + (t % 2) * D, D, 0, rows_of(t))).then_inc(s_rst[t % 2], 16)

                t0 = 5 * layer
                load(t0)
                load(t0 + 1)
                if layer == 0:
                    for m in range(4):
                        peer_weights(0, m)
                        if m == 0:
                            peer_keys(0)
                    mod_loads(MOD_TWO, NMB, MOD_PLACES[2], True)
                else:
                    peer_weights(1, 2)
                    peer_weights(1, 3)
                    final_loads()
                for b in range(5):
                    t = t0 + b
                    if b == 3 and layer:
                        sp.wait_ge(s_ph, t + 1)
                        sp.dma_start(at(FMODS, 2 * D, 0, NB), mod_dram[1:NC9, 14 * D:16 * D]).then_inc(s_mm1, 16)
                    if b == 3 and meanwhile:
                        meanwhile()
                    if b == 3:
                        ts_ = t0 + 4
                        sp.wait_ge(s_ph, ts_ + 1)
                        sp.dma_start(ph_dram, at(HT + (ts_ % 2) * D, D, 0, NB)).then_inc(s_shs, 16)
                        sp.wait_ge(s_shs, 16 * (layer + 1))
                        sp.wait_ge(s_dots, t0 + 4)
                        for q in range(NB):
                            sp.dma_start(at(HT + ((ts_ + 1) % 2) * D, D, 16 * q, 16 * q + 16),
                                         ph_dram[q:q + 1, :].partition_broadcast(16)).then_inc(s_shb, 16)
                        sp.wait_ge(s_idx, 8 * (ts_ + 1))
                        sp.dma_start(idx_dram, at(IDXP + (ts_ % 2) * P, P, 0, NB).bitcast(I32)).then_inc(s_sdr, 16)
                        sp.wait_ge(s_sdr, 32 * layer + 16)
                        sp.dma_start(at(IXS, RING).bitcast(I32),
                                     idx_dram.rearrange("b (s c) -> (b s) c", c=RING)).then_inc(s_sld, 16)
                    store(t)
                    if b == 3:
                        sp.wait_ge(s_g, ts_ + 1)
                        sp.dma_start(gw_dram, at(PG + (ts_ % 2) * P, P, 0, NB)).then_inc(s_sdr, 16)
                        sp.wait_ge(s_sdr, 32 * (layer + 1))
                        sp.dma_start(at(GS, RING), gw_dram.rearrange("b (s c) -> (b s) c", c=RING)
                                     ).then_inc(s_gs, 16)
                    if b + 2 < 5:
                        load(t + 2)
                if layer:
                    for j in (3, 4):
                        sp.wait_ge(s_rst[row_slot(stage, j)], row_no(STORES, stage, j))

            def mod_rows(rows, done):
                r = slice(0, 1) if rows == P else slice(1, NC9)
                for m, c0 in ((0, 12 * D), (2, 6 * D)):
                    src = mod_dram[r, c0:c0 + 2 * D]
                    sp.dma_start(at(MMOD + m * D, 2 * D, 0, rows), src.partition_broadcast(P) if rows == P
                                 else src).then_inc(done, 16)

            def attention_weights():
                sp.wait_ge(s_pq, 20)
                sp.wait_ge(s_ps, 20)
                for dst, src in ((WDKV, "w_dkv"), (WDQ, "w_dq"), (WUQ, "w_uq"), (CSN, "rope_mask")):
                    n_ = a[src].shape[1]
                    sp.dma_start(at(dst, n_), a[src]).then_inc(s_mw, 16)
                sp.dma_start(at(SUB + 1, NB).bitcast(I32), a["pages"]).then_inc(s_mw, 16)
                sp.dma_start(at(GCKV, KVL), a["g_ckv"].partition_broadcast(P)).then_inc(s_mw, 16)
                sp.dma_start(at(GCQ, QL), a["g_cq"].partition_broadcast(P)).then_inc(s_mw, 16)
                for b in range(2):
                    sp.wait_ge(s_modst[b], 16 * (NMB // 2))
                mod_rows(P, s_mw)

            def attention_sync():
                def gains(rows):
                    sp.dma_start(at(MHT, D, 0, rows), a["g_kv_norm"].partition_broadcast(rows)).then_inc(s_mm1, 16)
                    sp.dma_start(at(MHT + D, D, 0, rows), a["g_norm"][2:3, :].partition_broadcast(rows)
                                 ).then_inc(s_mm1, 16)

                def rows_in(j):
                    src = x2_dram[P * j:P * (j + 1)] if j < 4 else x2s_dram
                    sp.dma_start(at(MX + (j % 2) * D, D, 0, rows5(j)), src).then_inc(s_rld[j % 2], 16)

                gains(P)
                rows_in(0)
                rows_in(1)
                for j in (3, 4):
                    sp.wait_ge(s_rst[j % 2], row_no(STORES, "peer0", j))
                for dst, src, rows in ((WK, "w_k", P), (WV, "w_v", P), (WKT, "w_kt", NOPE)):
                    n_ = a[src].shape[1]
                    sp.dma_start(at(dst, n_, 0, rows), a[src]).then_inc(s_lw, 16)
                for j in range(5):
                    if j == 3:
                        sp.wait_ge(s_hin, 8)
                        sp.wait_ge(s_pr, 8)
                        mod_rows(NB, s_mm1)
                        gains(NB)
                    sp.wait_ge(s_kvr, 2 * j + 1)
                    kvr = at(KVR + (j % 2) * KVC, KVC, 0, rows5(j))
                    kd, rd = ((a["out_kv_p"][P * j:P * (j + 1)], a["out_kr_p"][P * j:P * (j + 1)]) if j < 4
                              else (a["out_kv_s"], a["out_kr_s"]))
                    sp.dma_start(kd, kvr[:, 0:KVL]).then_inc(s_kvs[j % 2], 16)
                    sp.dma_start(rd, kvr[:, KVL:KVC]).then_inc(s_kvs[j % 2], 16)
                    if j + 2 < 5:
                        sp.wait_ge(s_hin, 2 * (j + 1))
                        rows_in(j + 2)
                sp.wait_ge(s_tqh, 5)
                sp.wait_ge(s_tlc, 10)
                sp.dma_start(at(WO, KD * D), a["w_o"]).then_inc(s_mw, 16)
                sp.dma_start(at(MH, D), mod_dram[0:1, 8 * D:9 * D].partition_broadcast(P)).then_inc(s_mw, 16)
                sp.dma_start(at(MH + D, D, 0, NB), mod_dram[1:NC9, 8 * D:9 * D]).then_inc(s_mw, 16)
                for j in range(5):
                    if j == 2 or j == 3 or j == 4:
                        sp.wait_ge(s_rst[j % 2], row_no(STORES, "residual", j - 2))
                    else:
                        sp.wait_ge(s_hin, 10)
                    src = x2_dram[P * j:P * (j + 1)] if j < 4 else x2s_dram
                    sp.dma_start(at(MX + (j % 2) * D, D, 0, rows5(j)), src).then_inc(s_rld[j % 2], 16)
                    if j >= 1:
                        attention_store(j - 1)
                sp.wait_ge(s_csc, 5 * NB)
                peer_weights(1, 0)
                peer_weights(1, 1)
                sp.wait_ge(s_cpv, NB)
                peer_keys(1)
                sp.wait_ge(s_yy, 5)
                attention_store(4)
                for i in range(2):
                    sp.wait_ge(s_rst[i], row_no(STORES, "residual", 4 - i))
                    sp.wait_ge(s_kvs[i], 32 * (3 - i))

            def attention_store(j):
                sp.wait_ge(s_x3, j + 1)
                dst = x3_dram[P * j:P * (j + 1)] if j < 4 else x3s_dram
                sp.dma_start(dst, at(MX + (j % 2) * D, D, 0, rows5(j))).then_inc(s_rst[j % 2], 16)

            peer_loads(0)
            peer_tiles(0, x1_dram, x1s_dram, x2_dram, x2s_dram, attention_weights)
            attention_sync()
            peer_loads(1)
            peer_tiles(1, x3_dram, x3s_dram, a["out_y_p"], a["out_y_s"])

        @block.gpsimd
        def _(pool):
            n = [0]

            def link(ins):
                n[0] += 1
                ins.then_inc(pool_step, 1)
                pool.wait_ge(pool_step, n[0])

            pool.memset(ones, 1.0).then_inc(s_const, 1)
            pool.wait_ge(s_tabs, 1)
            shape = [P, G, GP]
            for s in range(TC):
                k = TC - 1 - s
                link(pool.tensor_tensor(bl[:, :, s, :], bbar_re, ca[:, k, :].unsqueeze(2).to_broadcast(shape),
                                        ALU.mult))
                link(pool.tensor_tensor(tmp_g, bbar_im, bb[:, k, :].unsqueeze(2).to_broadcast(shape), ALU.mult))
                ins = pool.tensor_tensor(bl[:, :, s, :], bl[:, :, s, :], tmp_g, ALU.add)
                if s < TC - 1:
                    link(ins)
                else:
                    ins.then_inc(s_blp, 1)
            for b in range(2):
                pool.wait_ge(s_modmm[b], MOD_ONE)
            pool.memset(at(TOEP, G * P), 0.0).then_inc(s_tz, 1)
            pool.wait_ge(s_clr, 1)
            pool.wait_ge(s_blp, 1)
            pool.wait_ge(s_h5, 1)
            pool.memset(u2[:, :, CH:UC], 0.0).then_inc(s_tz, 1)

            def gather(layer, phase, r, ix):
                table = a["peer_" + "uv"[phase] + str(layer)]
                pool.indirect_dma_start(ring[r], None, table, bass.IndirectOffsetOnAxis(ap=ix, axis=0)).then_inc(landed[r], 16)

            def head(t, phase, base, idx, i, fresh=False):
                pool.wait_ge(s_idx, 8 * t + i + 1)
                for g in range(2):
                    used = not (fresh and g == 0)
                    ix8 = at(IX8 + g * RING, RING).bitcast(I32)
                    if used:
                        pool.wait_ge(freed[0], 2 * i + (base + g))
                    pool.tensor_copy(ix8, idx[:, bass.ds(i * TOPK + g * RING, RING)]).then_inc(s_ix8, 1)
                    for r in range(RING):
                        if r == 0:
                            pool.wait_ge(s_ix8, 2 * i + (ix8_base(t, phase) + g + 1))
                            pool.sem_inc(s_go, 1)
                        elif used:
                            pool.wait_ge(freed[r], 2 * i + (base + g))
                            pool.sem_inc(s_go, 1)
                        gather(t // 5, phase, r, ix8[:, r:r + 1])

            def peer_gathers(layer):
                for b in range(5):
                    t = 5 * layer + b
                    for phase in range(2):
                        base = group_base(t, phase)
                        if b < 4:
                            assert base % 2 == 0
                            idx = at(IDXP + (t % 2) * P, P).bitcast(I32)
                            first = t == 0 and phase == 0
                            if first:
                                head(t, phase, base, idx, 0, True)
                            with pool.Fori(1 if first else 0, PH) as i:
                                head(t, phase, base, idx, i)
                        else:
                            ixs = at(IXS, RING).bitcast(I32)
                            pool.wait_ge(s_sld, 16 * (layer + 1))
                            for r in range(RING):
                                pool.wait_ge(freed[r], base)
                                gather(layer, phase, r, ixs[:, r:r + 1])

            def attention_pool():
                pool.wait_ge(s_tqh, 5)
                pool.wait_ge(s_tlc, 10)
                pool.tensor_copy(kt_[NOPE:QKD], at(KRT, SEQ, NOPE, QKD).unsqueeze(1).to_broadcast([ROPE, NH, SEQ])
                                 ).then_inc(s_ktr, 1)
                rows = at(SUB + 1, NB).bitcast(I32)
                pool.wait_ge(s_pix, 1)
                pool.wait_ge(s_pv, NTILE * NH)
                for b in range(NB):
                    if b >= 2:
                        pool.wait_ge(s_cpv, b - 1)
                        pool.wait_ge(s_ct, 4 * (b - 1))
                    ck = CK[b % 2]
                    pool.indirect_dma_start(at(ck, ROWK), None, a["cache_kv"],
                                            bass.IndirectOffsetOnAxis(ap=rows[:, b:b + 1], axis=0)
                                            ).then_inc(s_ck[b % 2], 16)
                    pool.indirect_dma_start(at(ck + ROWK, ROWR), None, a["cache_kr"],
                                            bass.IndirectOffsetOnAxis(ap=rows[:, b:b + 1], axis=0)
                                            ).then_inc(s_ck[b % 2], 16)

            peer_gathers(0)
            attention_pool()
            peer_gathers(1)
            pool.wait_ge(s_go, 2 * 2 * NTILE * P - (RING - 1))

        @block.scalar
        def _(act):
            n = [0]

            def link(ins):
                n[0] += 1
                ins.then_inc(act_step, 1)
                act.wait_ge(act_step, n[0])

            act.wait_ge(s_in, 32)
            act.activation(at(U2 + NPAR, KD * NC9), at(SILU, KD * NC9), ACT.Exp, scale=-1.0).then_inc(s_silu, 1)
            act.wait_ge(s_par, 16)
            act.activation(small[0], log_dt, ACT.Exp).then_inc(s_dt, 1)
            act.wait_ge(s_half, 1)
            act.activation(small[5], small[4], ACT.Sin).then_inc(s_sin, 1)
            link(act.activation(small[6], small[4], ACT.Abs))
            act.activation(small[7], small[6], ACT.Sin, scale=-1.0, bias=stat[:, 60:61]).then_inc(s_sin, 1)

            def mod_evac(first, last):
                def pair(i, b, fresh=False):
                    if not fresh:
                        act.wait_ge(s_modst[b], 16 * i)
                    act.wait_ge(s_modmm[b], 2 * i + 2)
                    act.activation(at(MODO + b * MB, MB, R32, R32 + NC9), psum[0:NC9, 6 + b, :],
                                   ACT.Copy).then_inc(s_modev[b], 1)
                    act.wait_ge(s_modev[b], i + 1)
                    act.dma_start(mod_dram[:, bass.ds((2 * i + b) * MB, MB)],
                                  at(MODO + b * MB, MB, R32, R32 + NC9)).then_inc(s_modst[b], 16)

                pairs(act, first, last, pair)

            mod_evac(0, MOD_ONE)
            act.wait_ge(s_x5, 48)
            act.wait_ge(s_clr, 1)
            act.wait_ge(s_blp, 1)
            for j in range(TC // 2):
                link(act.activation(at(MINB, D), x5[:, j, :], ACT.Square, accum_out=stat[:, j:j + 1]))
            act.wait_ge(s_mods5, 16 * 6)
            act.activation(at(MINB, D, 0, NB), at(TMP + D, D, 0, NB), ACT.Square,
                           accum_out=stat[0:NB, 4:5]).then_inc(s_sq, 1)
            act.wait_ge(s_ms, 1)
            act.activation(stat[:, 8:13], stat[:, 8:13], ACT.Sqrt).then_inc(s_rt, 1)

            for key in [k for k in ROUNDS if WHO[k[0]] == "A"]:
                kind, r = key
                no = round_no[key]
                act.wait_ge(s_mm, no + 1)
                ps = half(no)
                if kind == "u":
                    for s in range(2):
                        ins = act.activation(
                            u2[64 * s:64 * s + 64, RG * r:RG * (r + 1), 0:CH].rearrange(
                                "p (b g) c -> p b g c", b=4),
                            ps[0:64].rearrange("p b (g c) -> p b g c", g=4)[:, :, :, 64 * s:64 * s + 64], ACT.Copy)
                        if s == 0:
                            link(ins)
                elif kind == "k":
                    if r >= 2:
                        act.wait_ge(s_toep[r - 2], 16 * TC)
                    ins = act.activation(ksb[r % 2].rearrange("p (b g) m -> p b (g m)", b=4), ps[0:GP], ACT.Copy)
                else:
                    if r >= 2:
                        act.wait_ge(s_mm, round_no[("i", r - 2)] + 1)
                    ins = act.activation(minb[r % 2].rearrange("p (b g) m -> p b (g m)", b=4), ps, ACT.Copy)
                ins.then_inc(s_evA, 1)
            mod_evac(MOD_ONE, MOD_TWO)
            act.wait_ge(s_scd, 1)
            act.wait_ge(s_modmm[1], MOD_TWO)
            for gp in range(2):
                act.activation(hxv[0:64, gp], hpv[64 * gp:64 * gp + 64, 0], ACT.Copy).then_inc(s_hx, 1)
            wait_copied(act, ("y", NR - 1))
            act.wait_ge(s_out, 32)
            for j in range(TC // 2):
                act.activation(z5[:, j, :].rearrange("p (g q) -> p g q", g=G), h5[:, :, j, :], ACT.Gelu_apprx_tanh).then_inc(s_gelu, 1)
            act.activation(at(MS, D, 0, NB), at(MS, D, 0, NB), ACT.Gelu_apprx_tanh).then_inc(s_gelu, 1)
            for j in range(5):
                rows = P if j < 4 else NB
                act.wait_ge(s_zt, j + 1)
                if j >= 2:
                    act.wait_ge(s_gm, 4 * (j - 1))
                act.activation(zt[j % 2][:, :, 0:rows],
                               psum[:, 2 * (j % 2):2 * (j % 2) + 2, :].rearrange(
                                   "p b (k t) -> p (b k) t", k=4)[:, :, 0:rows], ACT.Copy).then_inc(s_zc, 1)
                for q in range(4):
                    m = 4 * j + q
                    act.wait_ge(s_gm, m + 1)
                    if m >= 2:
                        act.wait_ge(s_ga, m - 1)
                    act.activation(gate[m % 2][0:rows], psum[0:rows, 4 + m % 2, 256:512],
                                   ACT.Sigmoid).then_inc(s_sg, 1)

            def peer_prep(t):
                R = rows_of(t)
                act.wait_ge(s_rld[t % 2], row_no(LOADS, f"peer{t // 5}", t % 5))
                if t % 5 == 0:
                    act.wait_ge(s_pmr, t // 5 + 1)
                act.activation(at(PTMP, D, 0, R), at(XT + (t % 2) * D, D, 0, R), ACT.Square,
                               accum_out=stat[0:R, t % 2:t % 2 + 1]).then_inc(s_sq, 1)
                act.wait_ge(s_ms, norm_no(f"peer{t // 5}", t % 5))
                act.activation(stat[0:R, 2 + t % 2:3 + t % 2], stat[0:R, 2 + t % 2:3 + t % 2], ACT.Sqrt
                               ).then_inc(s_rt, 1)
                act.wait_ge(s_pt, t + 1)
                act.activation(htr[:, :, 0:R], psum[:, 2:4, :].rearrange("p b (k t) -> p (b k) t", k=4)[:, :, 0:R],
                               ACT.Copy).then_inc(s_ptc, 1)
                def queries(m):
                    act.wait_ge(s_pq, 4 * t + m + 1)
                    act.activation(qt[:, 4 * m:4 * m + 4, 0:R],
                                   psum[:, 2 + m % 2, :].rearrange("p (h t) -> p h t", h=4)[:, :, 0:R],
                                   ACT.Copy).then_inc(s_pqc, 1)

                def scores(m):
                    act.wait_ge(s_ps, 4 * t + m + 1)
                    if t:
                        act.wait_ge(s_idx, 8 * (t - 1) + 2 * m + 2)
                    act.activation(ssb[0:R, 4 * m:4 * m + 4, :].rearrange("p h n -> p (h n)"),
                                   psum[0:R, 4 + m % 2, :], ACT.Copy).then_inc(s_psc, 1)

                if t % 5 == 0:
                    for m in range(4):
                        queries(m)
                        scores(m)
                else:
                    queries(0)
                    for m in range(1, 4):
                        queries(m)
                        scores(m - 1)
                    scores(3)

            def peer_exp(t):
                R = rows_of(t)
                act.wait_ge(s_bv, t + 1)
                act.activation(at(BV, PH * TOPK, 0, R), at(BV, PH * TOPK, 0, R), ACT.Exp).then_inc(s_ex, 1)

            def peer_gelu(t):
                act.wait_ge(s_dots, t + 1)
                n_ = P if t % 5 < 4 else RING
                act.activation(at(DOTS, n_), at(DOTS, n_), ACT.Gelu_apprx_tanh).then_inc(s_act, 1)

            def peer_diags(t):
                base = group_base(t, 1)
                act.wait_ge(s_w, t + 1)
                if t % 5 < 4:
                    with act.Fori(0, PH) as i:
                        for g in range(2):
                            for r in V_PE:
                                act.wait_ge(freed[r], 2 * i + (base + g))
                                act.activation(diag[:, r, :], ident, ACT.Copy,
                                               scale=at(DOTS + P, P)[:, bass.ds(i * TOPK + g * RING + r, 1)]
                                               ).then_inc(s_dg, 1)
                else:
                    for r in range(RING):
                        act.wait_ge(freed[r], base)
                        act.activation(diag[:, r, 0:NB], sel8, ACT.Copy,
                                       scale=at(DOTS + P + r, 1)).then_inc(s_dg, 1)

            def final_squares(t):
                j, R = t - 5, rows_of(t)
                act.wait_ge(s_xn, out_no(t))
                act.activation(at(FSQ, D, 0, R), at(XT + (t % 2) * D, D, 0, R), ACT.Square,
                               accum_out=stat[0:R, 40 + j:41 + j]).then_inc(s_sq, 1)
                act.wait_ge(s_ms, norm_no("final", j))
                act.activation(stat[0:R, 45 + j:46 + j], stat[0:R, 45 + j:46 + j], ACT.Sqrt).then_inc(s_rt, 1)

            def peer_act(layer):
                t0 = 5 * layer
                peer_prep(t0)
                if t0 == 0:
                    mod_evac(MOD_TWO, NMB)
                peer_prep(t0 + 1)
                peer_exp(t0)
                for b in range(5):
                    t = t0 + b
                    if 1 <= b < 4:
                        peer_prep(t + 1)
                    peer_gelu(t)
                    peer_diags(t)
                    if b < 4:
                        peer_exp(t + 1)
                    if layer:
                        final_squares(t)

            def input_squares(j):
                R = rows5(j)
                x = at(MX + (j % 2) * D, D, 0, R)
                act.wait_ge(s_rld[j % 2], row_no(LOADS, "attention", j))
                act.wait_ge(s_mmr, 1)
                act.activation(at(OTT, D, 0, R), x, ACT.Square, accum_out=stat[0:R, 16:17]).then_inc(s_sq, 1)
                act.wait_ge(s_ms, norm_no("attention", j))
                act.activation(stat[0:R, 17:18], stat[0:R, 17:18], ACT.Sqrt).then_inc(s_rt, 1)

            def input_copies(j):
                R = rows5(j)
                for m, (ready, done) in enumerate(((s_tx, s_txc),) * 2):
                    act.wait_ge(ready, 2 * j + m + 1)
                    if j == 4:
                        act.wait_ge(s_mmr, 2)
                    act.activation(mht[m][:, :, 0:R], psum[:, 2 * m:2 * m + 2, :].rearrange(
                        "p b (k t) -> p (b k) t", k=4)[:, :, 0:R], ACT.Copy).then_inc(done, 1)

            def latent_squares(j):
                R = rows5(j)
                act.wait_ge(s_pr, 2 * j + 1)
                link(act.activation(at(OTT, KVL, 0, R), psum[0:R, 4, 0:KVL], ACT.Square,
                                    accum_out=stat[0:R, 18:19]))
                act.wait_ge(s_pr, 2 * j + 2)
                act.activation(at(OTT, QL, 0, R), psum[0:R, 5, 0:QL], ACT.Square,
                               accum_out=stat[0:R, 19:20]).then_inc(s_lsq, 1)
                act.wait_ge(s_lmn, j + 1)
                act.activation(stat[0:R, 20:22], stat[0:R, 20:22], ACT.Sqrt).then_inc(s_lrt, 1)

            def latent_copies(j):
                R = rows5(j)
                cols = slice(P * j, P * j + R)
                act.wait_ge(s_tl, 2 * j + 1)
                link(act.activation(ckvt[:, :, cols], psum[:, 6, 0:2 * P].rearrange(
                    "p (c t) -> p c t", c=2)[:, :, 0:R], ACT.Copy))
                act.activation(at(KRT + P * j, R, NOPE, QKD), psum[NOPE:QKD, 6, 2 * P:2 * P + R], ACT.Copy
                               ).then_inc(s_tlc, 1)
                act.wait_ge(s_tl, 2 * j + 2)
                act.activation(at(MCQT, QL).rearrange("p (k t) -> p k t", k=4)[:, :, 0:R],
                               psum[:, 7, :].rearrange("p (k t) -> p k t", k=4)[:, :, 0:R], ACT.Copy
                               ).then_inc(s_tlc, 1)
                act.wait_ge(s_q, j + 1)
                act.activation(at(MQ, NH * QKD, 0, R), psum[0:R, 0:3, :].rearrange("p b n -> p (b n)"), ACT.Copy
                               ).then_inc(s_qc, 1)
                act.wait_ge(s_tqh, j + 1)
                dst = qtm[0:QKD, :, cols] if j < 4 else qts[0:QKD]
                act.activation(dst, psum[0:QKD, 0:4, :].rearrange("p b (h t) -> p (b h) t", h=4)[:, :, 0:R],
                               ACT.Copy).then_inc(s_tqhc, 1)

            def attention_act():
                input_squares(0)
                input_copies(0)
                for j in range(5):
                    if j < 4:
                        input_squares(j + 1)
                    latent_squares(j)
                    if j < 4:
                        input_copies(j + 1)
                    latent_copies(j)
                act.wait_ge(s_ql, 1)
                act.activation(qlt.rearrange("p c b h -> p c h b"),
                               psum[:, 5, 0:2 * NH * NB].rearrange("p (c h b) -> p c h b", c=2, h=NH), ACT.Copy
                               ).then_inc(s_qlc, 1)
                for h in range(0, NH, 2):
                    act.wait_ge(s_ktp, h // 2 + 1)
                    act.activation(kt_[0:NOPE, h, :], psum[0:NOPE, h // 2 % 4, :], ACT.Copy).then_inc(s_kta, 1)
                for n_ in range(NTILE * NH):
                    i, h = divmod(n_, NH)
                    w = P * (i + 1)
                    act.wait_ge(s_nm, n_ + 1)
                    if n_ >= 2:
                        act.wait_ge(s_T, n_ - 1)
                    act.activation(at(PP + (n_ % 2) * SEQ, w), psum[:, n_ % 2, 0:w], ACT.Exp, scale=SM_SCALE,
                                   bias=stat[:, 32 + n_ % 2:33 + n_ % 2], accum_out=at(SUMS + n_ % 16, 1)
                                   ).then_inc(s_e2, 1)
                    if h == 1 and i:
                        out_copy_act(i - 1)
                out_copy_act(3)
                for b in range(NB + 1):
                    if b < NB:
                        for q in (0, 2):
                            cache_copies(act, b, q)
                    if b >= 1:
                        c = b - 1
                        sc = at(SCS[c % 2], NKEY, 0, NH)
                        act.wait_ge(s_cnm, c + 1)
                        act.activation(sc, sc, ACT.Exp, scale=SM_SCALE, bias=stat[0:NH, 34 + c % 2:35 + c % 2],
                                       accum_out=stat[0:NH, 36 + c % 2:37 + c % 2]).then_inc(s_ce, 1)
                out_copy_act(4)

            def out_copy_act(j):
                R = rows5(j)
                act.wait_ge(s_ot, j + 1)
                act.activation(at(OTT, D).rearrange("p (k t) -> p k t", k=KD)[:, :, 0:R],
                               psum[:, 6:8, :].rearrange("p b (k t) -> p (b k) t", k=4)[:, :, 0:R], ACT.Copy
                               ).then_inc(s_otc, 1)

            def cache_copies(eng, b, q):
                cache_copy(eng, b, q, eng.activation, s_cta)

            def cache_copy(eng, b, q, copy, done):
                eng.wait_ge(s_ct, 4 * b + q + 1)
                if b:
                    eng.wait_ge(s_cs, 5 * b)
                link(copy(kts[:, :, 512 * q:512 * (q + 1)], psum[:, 2 * (q % 2):2 * (q % 2) + 2, :], ACT.Copy))
                copy(krts[NOPE:QKD, 512 * q:512 * (q + 1)], psum[0:ROPE, 4 + q % 2, :], ACT.Copy).then_inc(done, 1)

            peer_act(0)
            attention_act()
            peer_act(1)

        @block.vector
        def _(dve):
            n = [0]

            def link(ins):
                n[0] += 1
                ins.then_inc(vec, 1)
                dve.wait_ge(vec, n[0])

            def tt(out, x, y, op):
                link(dve.tensor_tensor(out, x, y, op))

            def ts(out, x, s1, s2, op0, op1=None):
                if s2 is None:
                    link(dve.tensor_scalar(out, x, s1, None, op0))
                else:
                    link(dve.tensor_scalar(out, x, s1, s2, op0, op1))

            def stt(out, x, s, y, op0, op1):
                link(dve.scalar_tensor_tensor(out=out, in0=x, scalar=s, in1=y, op0=op0, op1=op1))

            link(dve.memset(stat, 1.0))
            dve.memset(zrow, 0.0).then_inc(s_z, 1)
            dve.wait_ge(s_z, 1)
            link(dve.memset(stat[:, 60:61], float(np.pi / 2)))
            dve.wait_ge(s_silu, 1)
            e = at(U2 + NPAR, KD * NC9)
            ts(e, e, 1.0, None, ALU.add)
            link(dve.reciprocal(e, e))
            dve.tensor_tensor(at(SILU, KD * NC9), at(SILU, KD * NC9), e, ALU.mult).then_inc(s_silu, 1)
            dt, ar, th, kk, rr, sn, _, cs, e1, tA, tB, tC, tD, tE, tF, tG = small
            dve.wait_ge(s_dt, 1)
            tt(ar, a_re, dt, ALU.mult)
            stt(th, a_im, 0.5, dt, ALU.mult, ALU.mult)
            ts(kk, th, float(1 / (2 * np.pi)), None, ALU.mult)
            ts(kk, kk, 12582912.0, None, ALU.add)
            ts(kk, kk, 12582912.0, None, ALU.subtract)
            stt(rr, kk, -6.28125, th, ALU.mult, ALU.add)
            stt(rr, kk, float(-(2 * np.pi - 6.28125)), rr, ALU.mult, ALU.add)
            dve.tensor_scalar(rr, rr, 3.1415925, -3.1415925, ALU.min, ALU.max).then_inc(s_half, 1)
            ts(ar, ar, 80.0, -80.0, ALU.min, ALU.max)
            ts(tA, ar, 1.0 / 64, None, ALU.mult)
            ts(e1, tA, 1.0 / 7, 1.0, ALU.mult, ALU.add)
            for m in (6, 5, 4, 3, 2):
                stt(e1, e1, 1.0 / m, tA, ALU.mult, ALU.mult)
                ts(e1, e1, 1.0, None, ALU.add)
            tt(e1, e1, tA, ALU.mult)
            for m in range(6):
                stt(e1, e1, 2.0, e1, ALU.add, ALU.mult)
            dve.wait_ge(s_sin, 2)
            stt(tB, sn, 2.0, cs, ALU.mult, ALU.mult)
            stt(tC, sn, -2.0, sn, ALU.mult, ALU.mult)
            ts(tD, e1, 1.0, None, ALU.add)
            tt(tE, tD, tC, ALU.mult)
            tt(tE, tE, e1, ALU.add)
            tt(tF, tD, tB, ALU.mult)
            link(dve.memset(pw_re[:, 0, :], 1.0))
            link(dve.memset(pw_im[:, 0, :], 0.0))
            ts(pw_re[:, 1, :], tE, 1.0, None, ALU.add)
            ts(pw_im[:, 1, :], tF, 1.0, None, ALU.mult)
            tt(tA, a_re, a_re, ALU.mult)
            tt(tB, a_im, a_im, ALU.mult)
            tt(tA, tA, tB, ALU.add)
            link(dve.reciprocal(tA, tA))
            tt(tB, tE, a_re, ALU.mult)
            tt(tC, tF, a_im, ALU.mult)
            tt(tB, tB, tC, ALU.add)
            tt(tB, tB, tA, ALU.mult)
            tt(tC, tF, a_re, ALU.mult)
            tt(tD, tE, a_im, ALU.mult)
            tt(tC, tC, tD, ALU.subtract)
            tt(tC, tC, tA, ALU.mult)
            shape = [P, G, GP]
            qre, qim = tB.unsqueeze(2).to_broadcast(shape), tC.unsqueeze(2).to_broadcast(shape)
            tt(bbar_re, b_re, qre, ALU.mult)
            tt(tmp_v, b_im, qim, ALU.mult)
            tt(bbar_re, bbar_re, tmp_v, ALU.subtract)
            tt(bbar_im, b_im, qre, ALU.mult)
            tt(tmp_v, b_re, qim, ALU.mult)
            tt(bbar_im, bbar_im, tmp_v, ALU.add)
            for lo in (1, 2, 4):
                sq_re = pw_re[:, lo:lo + 1, :].to_broadcast([P, lo, G])
                sq_im = pw_im[:, lo:lo + 1, :].to_broadcast([P, lo, G])
                src_re, src_im = pw_re[:, 1:1 + lo, :], pw_im[:, 1:1 + lo, :]
                dst_re, dst_im = pw_re[:, 1 + lo:1 + 2 * lo, :], pw_im[:, 1 + lo:1 + 2 * lo, :]
                t1 = at(TMP + 2 * D, lo * G).rearrange("p (m g) -> p m g", m=lo)
                tt(dst_re, src_re, sq_re, ALU.mult)
                tt(t1, src_im, sq_im, ALU.mult)
                tt(dst_re, dst_re, t1, ALU.subtract)
                tt(dst_im, src_re, sq_im, ALU.mult)
                tt(t1, src_im, sq_re, ALU.mult)
                tt(dst_im, dst_im, t1, ALU.add)
            ts(ca[0:64], pw_re[0:64], 1.0, None, ALU.mult)
            ts(cb[0:64], pw_im[0:64], -1.0, None, ALU.mult)
            ts(bb[0:64], pw_im[0:64], -1.0, None, ALU.mult)
            ts(ca[64:P], pw_im[64:P], 1.0, None, ALU.mult)
            ts(cb[64:P], pw_re[64:P], -1.0, None, ALU.mult)
            dve.tensor_scalar(bb[64:P], pw_re[64:P], 1.0, None, ALU.mult).then_inc(s_tabs, 1)
            dve.wait_ge(s_tabs, 1)
            for t in range(TC + 1):
                al = ca[:, t, :].unsqueeze(2).to_broadcast(shape)
                be = cb[:, t, :].unsqueeze(2).to_broadcast(shape)
                tt(cl[0:64, :, t, :], c_re[0:64], al[0:64], ALU.mult)
                stt(cl[64:P, :, t, :], c_re[64:P], -1.0, al[64:P], ALU.mult, ALU.mult)
                tt(tmp_v, c_im, be, ALU.mult)
                tt(cl[:, :, t, :], cl[:, :, t, :], tmp_v, ALU.add)
            for gp in range(2):
                rows = slice(64 * gp, 64 * gp + 64)
                for m, t in enumerate((TC, 1)):
                    for k, (src, sign) in enumerate(((pw_re, 1.0), (pw_re, 1.0), (pw_im, -1.0), (pw_im, 1.0))):
                        c0 = (4 * m + k) * HALF
                        ts(lamt[rows, c0:c0 + HALF], src[rows, t, gp:G:2], sign, None, ALU.mult)
            dve.tensor_scalar(stat[:, 61:62], stat[:, 60:61], 1.0, None, ALU.mult).then_inc(s_clr, 1)

            dve.wait_ge(s_clr, 1)
            dve.wait_ge(s_mods5, 16 * 6)
            g_bc, xs, sh_s, sc_s = at(TMP, D), at(TMP + D, D, 0, NB), at(TMP + 2 * D, D, 0, NB), \
                at(TMP + 3 * D, D, 0, NB)
            stt(mod_a, mod_a, 1.0, g_bc, ALU.add, ALU.mult)
            stt(sc_s, sc_s, 1.0, g_bc[0:NB], ALU.add, ALU.mult)
            dve.wait_ge(s_sq, 1)
            dve.tensor_scalar(stat[:, 8:13], stat[:, 0:5], 1.0 / D, EPS, ALU.mult, ALU.add).then_inc(s_ms, 1)
            dve.wait_ge(s_rt, 1)
            link(dve.reciprocal(stat[:, 8:13], stat[:, 8:13]))
            for j in range(TC // 2):
                stt(x5[:, j, :], x5[:, j, :], stat[:, 8 + j:9 + j], mod_a, ALU.mult, ALU.mult)
                ins = dve.tensor_tensor(h5[:, :, j, :], x5[:, j, :].rearrange("p (g q) -> p g q", g=G),
                                        mod_s.rearrange("p (g q) -> p g q", g=G), ALU.add)
                if j < 3:
                    link(ins)
                else:
                    ins.then_inc(s_h5, 1)
            stt(xs, xs, stat[0:NB, 12:13], sc_s, ALU.mult, ALU.mult)
            dve.tensor_tensor(xs, xs, sh_s, ALU.add).then_inc(s_h5, 1)
            dve.wait_ge(s_dld, 16)
            dve.wait_ge(s_hst, 16)
            dve.wait_ge(s_h5, 2)
            tt(at(MS, D, 0, NB), xs, mod_a[0:NB], ALU.mult)
            dve.wait_ge(s_mm, NR)
            for j in range(TC // 2):
                tt(h5[:, :, j, :], h5[:, :, j, :], mod_a.rearrange("p (g q) -> p g q", g=G), ALU.mult)
            for r in range(NR):
                no = round_no[("i", r)]
                dve.wait_ge(s_mm, no + 1)
                ps = half(no)[:, :, 0:4 * UC].rearrange("p b (g c) -> p b g c", g=4)
                for k in range(2):
                    for gp in range(2):
                        src = ps[64 * k:64 * k + 64, :, gp:4:2, :]
                        rows = slice(64 * gp, 64 * gp + 64)
                        g2 = slice(8 * r, 8 * r + 8)
                        link(dve.tensor_copy(sj[rows, :, k, g2].rearrange("p c (b g) -> p b g c", b=4),
                                             src[:, :, :, 0:CH]))
                        ins = dve.tensor_copy(si[rows, k, g2, :].rearrange("p (b g) c -> p b g c", b=4),
                                              src[:, :, :, CH + NB:UC])
                        if k and gp:
                            ins.then_inc(s_evV, 1)
                        else:
                            link(ins)
            link(dve.memset(hpx[:, 0, :], 0.0))
            wait_copied(dve, ("i", NR - 1))
            m4 = scan_tmp
            def scan_step(i, first=False):
                h_now = hpx[:, bass.ds(i, 1), :].rearrange("p o m -> p (o m)")
                h_next = hpx[:, bass.ds(i + 1, 1), :].rearrange("p o m -> p (o m)")
                inj = sj[:, bass.ds(i, 1), :, :].rearrange("p o k g -> p (o k g)")
                if not first:
                    dve.wait_ge(s_scan, 5 * i)
                dve.tensor_tensor(m4[:, 0:2 * HALF], lamt[:, 0:2 * HALF], h_now[:, 0:2 * HALF],
                                  ALU.mult).then_inc(s_scan, 1)
                dve.tensor_tensor(m4[:, 2 * HALF:4 * HALF], lamt[:, 2 * HALF:4 * HALF], h_now[:, HALF:3 * HALF],
                                  ALU.mult).then_inc(s_scan, 1)
                dve.wait_ge(s_scan, 5 * i + 2)
                dve.tensor_tensor(m4[:, 0:2 * HALF], m4[:, 0:2 * HALF], m4[:, 2 * HALF:4 * HALF],
                                  ALU.add).then_inc(s_scan, 1)
                dve.wait_ge(s_scan, 5 * i + 3)
                dve.tensor_tensor(h_next[:, 0:2 * HALF], m4[:, 0:2 * HALF], inj, ALU.add).then_inc(s_scan, 1)
                dve.tensor_tensor(h_next[:, 2 * HALF:3 * HALF], m4[:, 0:HALF], inj[:, 0:HALF],
                                  ALU.add).then_inc(s_scan, 1)

            scan_step(0, True)
            with dve.Fori(1, CH) as i:
                scan_step(i)
            dve.wait_ge(s_scan, 5 * CH)
            dve.tensor_copy(stat[:, 61:62], stat[:, 60:61]).then_inc(s_scd, 1)
            sh3 = [P, HALF, NB]
            lr, nli, li = (lamt[:, (4 + k) * HALF:(5 + k) * HALF].unsqueeze(2).to_broadcast(sh3) for k in (0, 2, 3))
            tx = sj_tmp
            for k, fac in ((0, nli), (1, li)):
                tt(tx, st0[:, k], lr, ALU.mult)
                tt(si[:, k], si[:, k], tx, ALU.add)
                tt(tx, st0[:, 1 - k], fac, ALU.mult)
                if k == 0:
                    tt(si[:, k], si[:, k], tx, ALU.add)
                else:
                    dve.tensor_tensor(si[:, k], si[:, k], tx, ALU.add).then_inc(s_scd, 1)
            for b in range(2):
                dve.wait_ge(s_modmm[b], MOD_TWO)
            for gp in range(2):
                dve.tensor_copy(hxv[64:P, gp], hpv[64 * gp:64 * gp + 64, 1]).then_inc(s_hx, 1)
            for r in range(NR):
                no = round_no[("y", r)]
                dve.wait_ge(s_mm, no + 1)
                ps = half(no).rearrange("p b (g t q) -> p (b g) t q", g=4, t=TC)
                for s in range(2):
                    yv = h5[64 * s:64 * s + 64, RG * r:RG * (r + 1)]
                    tt(yv, yv, ps[0:64, :, 4 * s:4 * s + 4, :], ALU.add)
                ys = at(MS + RG * GP * r, RG * GP, 0, NB).rearrange("p (g q) -> p g q", g=RG)
                dve.tensor_tensor(ys, ys, ps[64:64 + NB, :, 0, :], ALU.add).then_inc(s_evV, 1)
            dve.wait_ge(s_x5, 48 + 16 * 5)
            for j in range(5):
                rows = P if j < 4 else NB
                tb = glu_t[j % 2]
                for q in range(4):
                    m = 4 * j + q
                    dve.wait_ge(s_sg, m + 1)
                    dve.tensor_tensor(tb[0:rows, 256 * q:256 * (q + 1)], psum[0:rows, 4 + m % 2, 0:256],
                                      gate[m % 2][0:rows], ALU.mult).then_inc(s_ga, 1)
                dve.wait_ge(s_ga, 4 * (j + 1))
                ga = mod_a if j < 4 else at(BL + 5 * D, D, 0, NB)
                tt(tb[0:rows], tb[0:rows], ga, ALU.mult)
                xr = at(BL + j * D, D, 0, rows)
                dve.tensor_tensor(xr, xr, tb[0:rows], ALU.add).then_inc(s_x1, 1)
                dve.wait_ge(s_x1, j + 1)

            def peer_norm(t):
                R = rows_of(t)
                st = stat[0:R, 2 + t % 2:3 + t % 2]
                x, h = at(XT + (t % 2) * D, D, 0, R), at(HT + (t % 2) * D, D, 0, R)
                sh, sc = (at(PMOD + (0 if R == P else 3 * D) + m * D, D, 0, R) for m in range(2))
                dve.wait_ge(s_sq, norm_no(f"peer{t // 5}", t % 5))
                dve.tensor_scalar(st, stat[0:R, t % 2:t % 2 + 1], 1.0 / D, EPS, ALU.mult, ALU.add
                                  ).then_inc(s_ms, 1)
                dve.wait_ge(s_rt, norm_no(f"peer{t // 5}", t % 5))
                link(dve.reciprocal(st, st))
                stt(h, x, st, sc, ALU.mult, ALU.mult)
                dve.tensor_tensor(h, h, sh, ALU.add).then_inc(s_ph, 1)

            def best16(chains):
                steps = (lambda x, v, i: dve.max(v[:, 0:8], x), lambda x, v, i: dve.max_index(i[:, 0:8], v[:, 0:8], x),
                         lambda x, v, i: dve.match_replace(x, v[:, 0:8], x, -3.0e38),
                         lambda x, v, i: dve.max(v[:, 8:16], x), lambda x, v, i: dve.max_index(i[:, 8:16], v[:, 8:16], x))
                for m, step in enumerate(steps):
                    for c in chains:
                        if m:
                            dve.wait_ge(vec, n[0] - len(chains) + 1)
                        n[0] += 1
                        step(*c).then_inc(vec, 1)
                dve.wait_ge(vec, n[0])

            def both(*instructions):
                for ins in instructions:
                    n[0] += 1
                    ins.then_inc(vec, 1)
                dve.wait_ge(vec, n[0])

            def peer_top(t, h, part):
                R = rows_of(t)
                topv = at(TOPV, 2 * TOPK, 0, R).rearrange("p (s k) -> p s k", s=2)
                topi = at(TOPI, 2 * TOPK, 0, R).bitcast(U32).rearrange("p (s k) -> p s k", s=2)
                topf = at(TOPI + 32, 2 * TOPK, 0, R).rearrange("p (s k) -> p s k", s=2)
                cand = at(CAND, TOPK * TOPK, 0, R)
                bp = at(BP, TOPK, 0, R).bitcast(U32)
                pairs3 = [R, TOPK, TOPK]
                if part == 0:
                    dve.wait_ge(s_psc, 4 * t + h // 2 + 1)
                    best16([(ssb[0:R, 2 * h + s, :], topv[:, s], topi[:, s]) for s in range(2)])
                elif part == 1:
                    both(dve.tensor_copy(topf, topi),
                         dve.tensor_tensor(cand.rearrange("p (a b) -> p a b", a=TOPK),
                                           topv[:, 0].unsqueeze(2).to_broadcast(pairs3),
                                           topv[:, 1].unsqueeze(1).to_broadcast(pairs3), ALU.add))
                    best16([(cand, at(BV + h * TOPK, TOPK, 0, R), bp)])
                else:
                    ab = at(AB, 2 * TOPK, 0, R)
                    abi = at(AB + 32, 2 * TOPK, 0, R).bitcast(U32)
                    oh = at(ONEH, 512, 0, R).rearrange("p (k m) -> p k m", m=TOPK)
                    both(dve.tensor_scalar(abi[:, 0:TOPK], bp, 4, None, ALU.logical_shift_right),
                         dve.tensor_scalar(abi[:, TOPK:2 * TOPK], bp, TOPK - 1, None, ALU.bitwise_and))
                    link(dve.tensor_copy(ab, abi))
                    tt(oh, ab.unsqueeze(2).to_broadcast([R, 2 * TOPK, TOPK]),
                       iota16[0:R].unsqueeze(1).to_broadcast([R, 2 * TOPK, TOPK]), ALU.is_equal)
                    halves = [oh[:, s * TOPK:(s + 1) * TOPK] for s in range(2)]
                    both(*[dve.tensor_tensor(halves[s], halves[s], topf[:, s].unsqueeze(1).to_broadcast(pairs3),
                                             ALU.mult) for s in range(2)])
                    link(dve.tensor_reduce(ab, oh, AX.X, ALU.add))
                    idx = at(IDXP + (t % 2) * P + h * TOPK, TOPK, 0, R).bitcast(I32)
                    dve.scalar_tensor_tensor(out=idx, in0=ab[:, 0:TOPK], scalar=float(N_KEYS),
                                             in1=ab[:, TOPK:2 * TOPK], op0=ALU.mult, op1=ALU.add).then_inc(s_idx, 1)
                    dve.wait_ge(s_idx, 8 * t + h + 1)

            def peer_shift(t):
                R = rows_of(t)
                bv = at(BV, PH * TOPK, 0, R).rearrange("p (h k) -> p h k", h=PH)
                mx = at(CAND, PH, 0, R)
                link(dve.tensor_copy(mx, bv[:, :, 0]))
                dve.tensor_tensor(bv, bv, mx.unsqueeze(2).to_broadcast([R, PH, TOPK]), ALU.subtract
                                  ).then_inc(s_bv, 1)

            def peer_gates(t):
                R = rows_of(t)
                bv = at(BV, PH * TOPK, 0, R).rearrange("p (h k) -> p h k", h=PH)
                g = at(PG + (t % 2) * P, PH * TOPK, 0, R).rearrange("p (h k) -> p h k", h=PH)
                dve.wait_ge(s_ex, t + 1)
                sums = at(CAND, PH, 0, R)
                link(dve.tensor_reduce(sums, bv, AX.X, ALU.add))
                link(dve.reciprocal(sums, sums))
                dve.tensor_tensor(g, bv, sums.unsqueeze(2).to_broadcast([R, PH, TOPK]), ALU.mult).then_inc(s_g, 1)

            def dot(t, r, g, col):
                h = at(HT + (t % 2) * D, D) if t % 5 < 4 else at(HT + ((t + 1) % 2) * D, D)
                dve.scalar_tensor_tensor(out=ring[r], in0=ring[r], scalar=1.0, in1=h, op0=ALU.mult, op1=ALU.mult,
                                         accum_out=col).then_inc(freed[r], 1)

            def head_dots(t, h):
                for g in range(2):
                    for r in range(RING):
                        dve.wait_ge(landed[r], 16 * (group_base(t, 0) + 2 * h + g + 1))
                        dot(t, r, g, at(DOTS + h * TOPK + g * RING + r, 1))

            def peer_dots(t):
                base = group_base(t, 0)
                if t % 5 < 4:
                    for heads in ((0, 2), (2, PH)):
                        if heads[0]:
                            peer_norm(t + 1)
                        with dve.Fori(*heads) as i:
                            for g in range(2):
                                for r in range(RING):
                                    dve.wait_ge(landed[r], 32 * i + 16 * (base + g + 1))
                                    dot(t, r, g, at(DOTS, P)[:, bass.ds(i * TOPK + g * RING + r, 1)])
                else:
                    dve.wait_ge(s_shb, 16 * NB * (t // 5 + 1))
                    for r in range(RING):
                        dve.wait_ge(landed[r], 16 * (base + 1))
                        dot(t, r, 0, at(DOTS + r, 1))
                all_dots(t)

            def all_dots(t):
                last = group_base(t, 1)
                dve.wait_ge(freed[RING - 1], last)
                dve.tensor_copy(stat[:, 61:62], stat[:, 60:61]).then_inc(s_dots, 1)

            def peer_weights(t):
                dve.wait_ge(s_act, t + 1)
                if t % 5 < 4:
                    g, n_ = at(PG + (t % 2) * P, P), P
                    dve.wait_ge(s_g, t + 1)
                else:
                    g, n_ = at(GS, RING), RING
                    dve.wait_ge(s_gs, 16 * (t // 5 + 1))
                dve.tensor_tensor(at(DOTS + P, n_), at(DOTS, n_), g, ALU.mult).then_inc(s_w, 1)
                dve.wait_ge(s_w, t + 1)

            def peer_values(t, h, first, last):
                for g, r in [(g, r) for g in range(2) for r in V_DVE][first:last]:
                    base = group_base(t, 1) + 2 * h + g
                    dve.wait_ge(landed[r], 16 * (base + 1))
                    dve.scalar_tensor_tensor(out=at(YACC, D), in0=ring[r],
                                             scalar=at(DOTS + P + h * TOPK + g * RING + r, 1),
                                             in1=at(YACC, D), op0=ALU.mult, op1=ALU.add).then_inc(freed[r], 1)
                    dve.wait_ge(freed[r], base + 1)

            def peer_out(t):
                R = rows_of(t)
                y = at(YACC, D, 0, R)
                x = at(XT + (t % 2) * D, D, 0, R)
                ga = at(PMOD + (2 if R == P else 5) * D, D, 0, R)
                ps = psum[0:R, 0:2, :].rearrange("p b n -> p (b n)")
                dve.wait_ge(s_yp, t + 1)
                if R == P:
                    dve.tensor_tensor(y, y, ps, ALU.add).then_inc(s_yr, 1)
                else:
                    dve.tensor_copy(y, ps).then_inc(s_yr, 1)
                dve.wait_ge(s_yr, t + 1)
                tt(y, y, ga, ALU.mult)
                dve.tensor_tensor(x, x, y, ALU.add).then_inc(s_xn, 1)
                if t >= 5:
                    dve.wait_ge(s_xn, out_no(t))
                    final_norm(t - 5, x)

            def final_norm(j, x):
                R = rows5(j)
                mods = FMOD if j < 4 else FMODS
                if j == 0:
                    dve.wait_ge(s_mm1, 96 + 32)
                    stt(at(FMOD + D, D), at(FMOD + D, D), 1.0, at(FG, D), ALU.add, ALU.mult)
                if j == 4:
                    dve.wait_ge(s_mm1, 96 + 48)
                    sc = at(mods + D, D, 0, R)
                    stt(sc, sc, 1.0, at(FG, D, 0, R), ALU.add, ALU.mult)
                st = stat[0:R, 45 + j:46 + j]
                dve.wait_ge(s_sq, norm_no("final", j))
                dve.tensor_scalar(st, stat[0:R, 40 + j:41 + j], 1.0 / D, EPS, ALU.mult, ALU.add).then_inc(s_ms, 1)
                dve.wait_ge(s_rt, norm_no("final", j))
                link(dve.reciprocal(st, st))
                stt(x, x, st, at(mods + D, D, 0, R), ALU.mult, ALU.mult)
                dve.tensor_tensor(x, x, at(mods, D, 0, R), ALU.add).then_inc(s_xn, 1)

            def peer_dve(layer):
                t0 = 5 * layer
                dve.wait_ge(s_pmod, 48 * (layer + 1))
                for m in (1, 4):
                    R = P if m == 1 else NB
                    sc = at(PMOD + m * D, D, 0, R)
                    ins = dve.scalar_tensor_tensor(out=sc, in0=sc, scalar=1.0, in1=at(PTMP, D, 0, R), op0=ALU.add,
                                                   op1=ALU.mult)
                    if m == 1:
                        link(ins)
                    else:
                        ins.then_inc(s_pmr, 1)
                dve.wait_ge(s_pmr, layer + 1)
                peer_norm(t0)
                for h in range(PH + 1):
                    if h < PH:
                        for part in range(3):
                            peer_top(t0, h, part)
                    if h == PH - 1:
                        peer_shift(t0)
                    if h == 4:
                        peer_norm(t0 + 1)
                    if h:
                        head_dots(t0, h - 1)
                all_dots(t0)
                peer_gates(t0)
                for b in range(5):
                    t = t0 + b
                    if b:
                        peer_dots(t)
                    peer_weights(t)
                    if b < 4:
                        if t == 0:
                            dve.wait_ge(s_modmm[1], NMB)
                        link(dve.memset(at(YACC, D), 0.0))
                        for h in range(PH):
                            per = 3 if b < 3 else 4
                            parts = range(per * h, min(per * (h + 1), 3 * PH))
                            for m in range(per):
                                if m < len(parts):
                                    peer_top(t + 1, *divmod(parts[m], 3))
                                n_ = 2 * len(V_DVE)
                                peer_values(t, h, m * n_ // per, (m + 1) * n_ // per)
                        peer_shift(t + 1)
                    peer_out(t)
                    if b < 4:
                        peer_gates(t + 1)

            def rotate(x1, x2, cos, sin, shape):
                n_ = shape[1] * shape[2] if len(shape) == 3 else shape[1]
                t = [at(PP + i * 256, n_, 0, shape[0]) for i in range(4)]
                if len(shape) == 3:
                    t = [v_.rearrange("p (h m) -> p h m", h=shape[1]) for v_ in t]
                tt(t[0], x1, cos, ALU.mult)
                tt(t[1], x2, sin, ALU.mult)
                tt(t[2], x1, sin, ALU.mult)
                tt(t[3], x2, cos, ALU.mult)
                return t

            def attention_mods(R, n_):
                dve.wait_ge(s_mm1, 32 if n_ == 1 else 96)
                kv_sc, q_sc = at(MMOD + D, D, 0, R), at(MMOD + 3 * D, D, 0, R)
                stt(kv_sc, kv_sc, 1.0, at(MHT, D, 0, R), ALU.add, ALU.mult)
                dve.scalar_tensor_tensor(out=q_sc, in0=q_sc, scalar=1.0, in1=at(MHT + D, D, 0, R), op0=ALU.add,
                                         op1=ALU.mult).then_inc(s_mmr, 1)
                dve.wait_ge(s_mmr, n_)

            def attention_inputs(j):
                R = rows5(j)
                if j == 4:
                    attention_mods(NB, 2)
                x = at(MX + (j % 2) * D, D, 0, R)
                dve.wait_ge(s_sq, norm_no("attention", j))
                st = stat[0:R, 17:18]
                dve.tensor_scalar(st, stat[0:R, 16:17], 1.0 / D, EPS, ALU.mult, ALU.add).then_inc(s_ms, 1)
                dve.wait_ge(s_rt, norm_no("attention", j))
                link(dve.reciprocal(st, st))
                for m, (used, made) in enumerate(((s_tx, s_hin),) * 2):
                    h = at(MH + m * D, D, 0, R)
                    if j:
                        dve.wait_ge(used, 2 * (j - 1) + m + 1)
                    stt(h, x, st, at(MMOD + (2 * m + 1) * D, D, 0, R), ALU.mult, ALU.mult)
                    dve.tensor_tensor(h, h, at(MMOD + 2 * m * D, D, 0, R), ALU.add).then_inc(made, 1)

            def latents_and_rotations(j):
                R = rows5(j)
                dve.wait_ge(s_lsq, j + 1)
                link(dve.tensor_scalar(stat[0:R, 20:21], stat[0:R, 18:19], 1.0 / KVL, EPS, ALU.mult, ALU.add))
                dve.tensor_scalar(stat[0:R, 21:22], stat[0:R, 19:20], 1.0 / QL, EPS, ALU.mult, ALU.add
                                  ).then_inc(s_lmn, 1)
                dve.wait_ge(s_lrt, j + 1)
                link(dve.reciprocal(stat[0:R, 20:22], stat[0:R, 20:22]))
                kvr = at(KVR + (j % 2) * KVC, KVC, 0, R)
                if j >= 2:
                    dve.wait_ge(s_kvs[j % 2], 32 * (j // 2))
                    dve.wait_ge(s_tl, 2 * (j - 2) + 1)
                stt(kvr[:, 0:KVL], psum[0:R, 4, 0:KVL], stat[0:R, 20:21], at(GCKV, KVL, 0, R), ALU.mult, ALU.mult)
                m_ = ROPE // 2
                t = rotate(psum[0:R, 4, KVL:KVL + m_], psum[0:R, 4, KVL + m_:KVC], csn[0:R, j, 0], csn[0:R, j, 1],
                           [R, m_])
                tt(kvr[:, KVL:KVL + m_], t[0], t[1], ALU.subtract)
                dve.tensor_tensor(kvr[:, KVL + m_:KVC], t[2], t[3], ALU.add).then_inc(s_kvr, 1)
                dve.scalar_tensor_tensor(out=at(MCQ, QL, 0, R), in0=psum[0:R, 5, 0:QL], scalar=stat[0:R, 21:22],
                                         in1=at(GCQ, QL, 0, R), op0=ALU.mult, op1=ALU.mult).then_inc(s_kvr, 1)
                dve.wait_ge(s_qc, j + 1)
                q3 = at(MQ, NH * QKD, 0, R).rearrange("p (h n) -> p h n", h=NH)
                x1, x2 = q3[:, :, NOPE:NOPE + m_], q3[:, :, NOPE + m_:QKD]
                shape = [R, NH, m_]
                cos, sin = (csn[0:R, j, i].unsqueeze(1).to_broadcast(shape) for i in range(2))
                dve.wait_ge(s_kvr, 2 * j + 2)
                t = rotate(x1, x2, cos, sin, shape)
                tt(x1, t[0], t[1], ALU.subtract)
                dve.tensor_tensor(x2, t[2], t[3], ALU.add).then_inc(s_qr, 1)

            def attention_dve():
                dve.wait_ge(s_mw, 144)
                pages = at(SUB + 1, NB)
                link(dve.tensor_copy(at(OL, NB), pages.bitcast(I32)))
                dve.tensor_scalar(pages.bitcast(I32), at(OL, NB), 8.0, at(SUB, 1), ALU.mult, ALU.add
                                  ).then_inc(s_pix, 1)
                attention_mods(P, 1)
                attention_inputs(0)
                for j in range(5):
                    if j < 4:
                        attention_inputs(j + 1)
                    latents_and_rotations(j)
                for h in range(1, NH, 2):
                    dve.wait_ge(s_ktp, h // 2 + 1)
                    dve.tensor_copy(kt_[0:NOPE, h, :], psum[NOPE:P, h // 2 % 4, :]).then_inc(s_ktv, 1)
                dve.wait_ge(s_ql, 1)
                for i in range(NTILE):
                    dve.wait_ge(s_vp, i + 1)
                    dve.tensor_copy(vv[:, i, :], psum[:, 4 + 2 * (i % 2):6 + 2 * (i % 2), :].rearrange(
                        "p b n -> p (b n)")).then_inc(s_vc, 1)
                for n_ in range(NTILE * NH + 1):
                    if n_ < NTILE * NH:
                        i, h = divmod(n_, NH)
                        w = P * (i + 1)
                        dve.wait_ge(s_S, n_ + 1)
                        nm = stat[:, 32 + n_ % 2:33 + n_ % 2]
                        if n_ >= 2:
                            dve.wait_ge(s_e2, n_ - 1)
                        link(dve.tensor_reduce(nm, psum[:, n_ % 2, 0:w], AX.X, ALU.max))
                        dve.tensor_scalar(nm, nm, -SM_SCALE, None, ALU.mult).then_inc(s_nm, 1)
                    if n_ >= 1:
                        m = n_ - 1
                        i, h = divmod(m, NH)
                        w = P * (i + 1)
                        dve.wait_ge(s_T, m + 1)
                        if m >= 2:
                            dve.wait_ge(s_pv, m - 1)
                        dve.tensor_copy(at(PTT + (m % 2) * SEQ, w), psum[:, 2 + m % 2, 0:w]).then_inc(s_Tc, 1)
                        if h % 8 == 1 and m > 8:
                            head_scale(m // 8 - 1)
                        if h == 2 and i:
                            attention_out(i - 1)
                head_scale(7)
                attention_out(3)
                for b in range(NB + 1):
                    if b < NB:
                        for q in range(4):
                            if q % 2:
                                cache_copy(b, q)
                            if q:
                                sample_scores(b, q - 1)
                        sample_scores(b, 3)
                        sample_scores(b, 4)
                        sc = at(SCS[b % 2], NKEY, 0, NH)
                        nm = stat[0:NH, 34 + b % 2:35 + b % 2]
                        dve.wait_ge(s_csc, 5 * (b + 1))
                        link(dve.tensor_reduce(nm, sc, AX.X, ALU.max))
                        dve.tensor_scalar(nm, nm, -SM_SCALE, None, ALU.mult).then_inc(s_cnm, 1)
                    if b >= 1:
                        c = b - 1
                        dve.wait_ge(s_cT, c + 1)
                        ps = psum[:, 6, 0:17 * NH].rearrange("p (r h) -> p r h", r=17)
                        link(dve.tensor_copy(pts[:, 0:16], ps[:, 0:16]))
                        dve.tensor_copy(pts[0:NB, 16], ps[0:NB, 16]).then_inc(s_cTc, 1)
                        sm = stat[0:NH, 36 + c % 2:37 + c % 2]
                        dve.wait_ge(s_ce, c + 1)
                        link(dve.reciprocal(sm, sm))
                        dve.wait_ge(s_cpv, c + 1)
                        dve.tensor_scalar(at(OL, KVL, 0, NH), psum[0:NH, 7, 0:KVL], sm, None, ALU.mult
                                          ).then_inc(s_col, 1)
                        dve.wait_ge(s_cot, c + 1)
                        dve.tensor_copy(olt[:, :, :, c], psum[:, 7, KVL:KVL + 2 * NH].rearrange(
                            "p (c h) -> p c h", c=2)).then_inc(s_coc, 1)
                dve.wait_ge(s_os, 1)
                dve.wait_ge(s_ot, 4)
                dve.tensor_copy(at(OO, D, 0, NB), psum[0:NB, 0:2, :].rearrange("p b n -> p (b n)")).then_inc(s_on, 1)
                attention_out(4)

            def cache_copy(b, q):
                dve.wait_ge(s_ct, 4 * b + q + 1)
                if b:
                    dve.wait_ge(s_cs, 5 * b)
                link(dve.tensor_copy(kts[:, :, 512 * q:512 * (q + 1)], psum[:, 2 * (q % 2):2 * (q % 2) + 2, :]))
                dve.tensor_copy(krts[NOPE:QKD, 512 * q:512 * (q + 1)], psum[0:ROPE, 4 + q % 2, :]).then_inc(s_ctv, 1)

            def sample_scores(b, q):
                m = 5 * b + q
                dve.wait_ge(s_cs, m + 1)
                if b >= 2 and q == 0:
                    dve.wait_ge(s_cT, b - 1)
                sc = at(SCS[b % 2], NKEY, 0, NH)
                if q < 4:
                    dve.tensor_copy(sc[:, 512 * q:512 * (q + 1)], psum[0:NH, 6 + m % 2, :]).then_inc(s_csc, 1)
                else:
                    dve.tensor_tensor(sc[:, PAST:NKEY], psum[0:NH, 6 + m % 2, 0:NB],
                                      at(SMASK + NB * b, NB, 0, NH), ALU.add).then_inc(s_csc, 1)

            def head_scale(u):
                sm = at(SUMS + 8 * (u % 2), 8)
                dve.wait_ge(s_pv, 8 * (u + 1))
                dve.wait_ge(s_e2, 8 * (u + 1))
                link(dve.reciprocal(sm, sm))
                if u >= 2 and u % 2 == 0:
                    dve.wait_ge(s_ot, u // 2)
                dve.tensor_tensor(at(OO + 512 * (u % 2), 512).rearrange("p (h n) -> p h n", h=8),
                                  psum[:, 4 + u % 2, :].rearrange("p (h n) -> p h n", h=8),
                                  sm.unsqueeze(2).to_broadcast([P, 8, VH]), ALU.mult).then_inc(s_on, 1)

            def attention_out(j):
                R = rows5(j)
                x = at(MX + (j % 2) * D, D, 0, R)
                ga = at(MH + (0 if j < 4 else D), D, 0, R)
                dve.wait_ge(s_mw, 144 + 48)
                dve.wait_ge(s_rld[j % 2], row_no(LOADS, "residual", j))
                dve.wait_ge(s_yy, j + 1)
                y = at(MHT, D, 0, R)
                tt(y, psum[0:R, 6:8, :].rearrange("p b n -> p (b n)"), ga, ALU.mult)
                dve.tensor_tensor(x, x, y, ALU.add).then_inc(s_x3, 1)

            peer_dve(0)
            attention_dve()
            peer_dve(1)

        @block.tensor
        def _(pe):
            def mod_products(first, last, places):
                def pair(i, b, fresh=False):
                    pe.wait_ge(s_modw[b], 48 * i + 48)
                    if not fresh:
                        pe.wait_ge(s_modev[b], i)
                    w = [at(place, HALF_MOD).rearrange("p (k n) -> p k n", k=KD // 2) for place in places[b]]
                    for k in range(KD):
                        ins = pe.matmul(psum[0:NC9, 6 + b, :], silu[:, k, :], w[k // 4][:, k % 4, :],
                                        start=(k == 0), stop=False)
                        if k == KD // 2 - 1:
                            ins.then_inc(s_modmm[b], 1)
                    pe.matmul(psum[0:NC9, 6 + b, :], ones[0:1, 0:NC9], at(MODB + b * MB, MB, 0, 1),
                              start=False, stop=True).then_inc(s_modmm[b], 1)

                pairs(pe, first, last, pair)

            pe.wait_ge(s_silu, 2)
            pe.wait_ge(s_const, 1)
            mod_products(0, MOD_ONE, MOD_PLACES[0])
            for b in range(2):
                pe.wait_ge(s_modev[b], MOD_ONE // 2)
            pe.wait_ge(s_h5, 1)
            for no, (kind, r) in enumerate(ROUNDS):
                if no >= 2:
                    wait_copied(pe, ROUNDS[no - 2])
                ps = half(no)
                if kind == "u" and r == 0:
                    pe.wait_ge(s_in, 32)
                if kind == "k" and r == 0:
                    pe.wait_ge(s_clr, 1)
                    pe.wait_ge(s_blp, 1)
                if kind == "i":
                    wait_copied(pe, ("m", r))
                    if r == 0:
                        pe.wait_ge(s_us, 16 * 2 * NB)
                        wait_copied(pe, ("u", NR - 1))
                if kind == "y" and r == 0:
                    mod_products(MOD_ONE, MOD_TWO, MOD_PLACES[1])
                    for b in range(2):
                        pe.wait_ge(s_modev[b], MOD_TWO // 2)
                    pe.wait_ge(s_hx, 4)
                    pe.wait_ge(s_st0, 16)
                    for q in range(NR):
                        pe.wait_ge(s_toep[q], 16 * TC)
                for gl in range(RG):
                    g = RG * r + gl
                    bank, slot = gl // 4, gl % 4
                    last = slot == 3
                    if kind == "u":
                        ins = pe.transpose(ps[0:64, bank, P * slot:P * (slot + 1)],
                                           h5[:, g].rearrange("p j q -> p (j q)"), ident)
                    elif kind == "k":
                        ins = pe.matmul(ps[0:GP, bank, P * slot:P * (slot + 1)], bl[:, g, TC - 1, :],
                                        cl[:, g, 0:TC, :], start=True, stop=True)
                    elif kind == "m":
                        ins = pe.transpose(ps[:, bank, P * slot:P * (slot + 1)],
                                           bl[:, g].rearrange("p s q -> p (s q)"), ident)
                    elif kind == "i":
                        ins = pe.matmul(ps[:, bank, UC * slot:UC * (slot + 1)], minb[r % 2][:, gl, :], u2[:, g, :],
                                        start=True, stop=True)
                    else:
                        out = ps[0:CH + NB, bank, P * slot:P * (slot + 1)]
                        pe.matmul(out, u2[:, g, 0:CH + NB], toep[:, g, :], start=True, stop=False)
                        ins = pe.matmul(out, hx[:, g, :], cl[:, g, 1:TC + 1, :], start=False, stop=True)
                ins.then_inc(s_mm, 1)
            wait_copied(pe, ROUNDS[-1])
            for j in range(5):
                rows = P if j < 4 else NB
                z = z5[:, j, :] if j < 4 else at(MS, D, 0, NB)
                pe.wait_ge(s_gelu, j + 1)
                if j >= 2:
                    pe.wait_ge(s_zc, j - 1)
                for k in range(KD):
                    ins = pe.transpose(psum[:, 2 * (j % 2) + k // 4, P * (k % 4):P * (k % 4) + rows],
                                       z[:, P * k:P * (k + 1)], ident[0:rows, 0:rows])
                ins.then_inc(s_zt, 1)
                pe.wait_ge(s_zc, j + 1)
                for q in range(4):
                    m = 4 * j + q
                    if m < 3:
                        pe.wait_ge(*((s_wglu, 16), (s_lw, LATE_GLU), (s_wglu, 48))[m])
                    if m >= 2:
                        pe.wait_ge(s_ga, m - 1)
                    wglu = wglu_at[q].rearrange("p (k n) -> p k n", k=KD)
                    for k in range(KD):
                        ins = pe.matmul(psum[0:rows, 4 + m % 2, :], zt[j % 2][:, k, 0:rows],
                                        wglu[:, k, :], start=(k == 0), stop=(k == KD - 1))
                    ins.then_inc(s_gm, 1)

            def peer_prep(t):
                R = rows_of(t)
                h = at(HT + (t % 2) * D, D, 0, R)
                pe.wait_ge(s_ph, t + 1)
                if t:
                    pe.wait_ge(s_pqc, 4 * t)
                for k in range(KD):
                    ins = pe.transpose(psum[:, 2 + k // 4, P * (k % 4):P * (k % 4) + R], h[:, P * k:P * (k + 1)],
                                       ident[0:R, 0:R])
                ins.then_inc(s_pt, 1)

                def queries(m):
                    if m < 2:
                        pe.wait_ge(s_ptc, t + 1)
                    else:
                        pe.wait_ge(s_pqc, 4 * t + m - 1)
                    if m == 0 and t % 5 == 0:
                        pe.wait_ge(s_pw, 48 * (t // 5 + 1))
                    if m == 2 and t % 5 == 0:
                        pe.wait_ge(s_lw, LATE_Q[t // 5])
                    for q in range(4):
                        for k in range(KD):
                            ins = pe.matmul(psum[:, 2 + m % 2, P * q:P * q + R],
                                            wq[:, m, k, P * q:P * (q + 1)], htr[:, k, 0:R],
                                            start=(k == 0), stop=(k == KD - 1))
                    ins.then_inc(s_pq, 1)

                def scores(m):
                    n_ = 4 * t + m
                    pe.wait_ge(s_pqc, n_ + 1)
                    if n_ >= 2:
                        pe.wait_ge(s_psc, n_ - 1)
                    for q in range(4):
                        ins = pe.matmul(psum[0:R, 4 + m % 2, P * q:P * (q + 1)], qt[:, 4 * m + q, 0:R],
                                        keys[:, 4 * m + q, :], start=True, stop=True)
                    ins.then_inc(s_ps, 1)

                if t % 5 == 0:
                    for m in range(4):
                        queries(m)
                        scores(m)
                else:
                    queries(0)
                    for m in range(1, 4):
                        queries(m)
                        scores(m - 1)
                    scores(3)

            def peer_values(t):
                R = rows_of(t)
                base = group_base(t, 1)
                acc = [psum[0:R, c, :] for c in range(2)]
                if t:
                    pe.wait_ge(s_yr, t)
                for c in range(2):
                    pe.matmul(acc[c], ident[64:65, 0:R], zrow, start=True, stop=False, skip_group_check=True)

                def product(r):
                    for c in range(2):
                        ins = pe.matmul(acc[c], diag[:, r, 0:R], ring[r][:, 512 * c:512 * (c + 1)], start=False,
                                        stop=False, skip_group_check=True)
                    ins.then_inc(freed[r], 1)

                if t % 5 < 4:
                    with pe.Fori(0, PH) as i:
                        for g in range(2):
                            for m, r in enumerate(V_PE):
                                pe.wait_ge(landed[r], 32 * i + 16 * (base + g + 1))
                                pe.wait_ge(s_dg, 2 * len(V_PE) * i + (diag_base(t) + len(V_PE) * g + m + 1))
                                product(r)
                else:
                    for r in range(RING):
                        pe.wait_ge(landed[r], 16 * (base + 1))
                        pe.wait_ge(s_dg, diag_base(t) + r + 1)
                        product(r)
                for c in range(2):
                    ins = pe.matmul(acc[c], ident[64:65, 0:R], zrow, start=False, stop=True, skip_group_check=True)
                ins.then_inc(s_yp, 1)

            def peer_pe(layer):
                t0 = 5 * layer
                peer_prep(t0)
                if t0 == 0:
                    mod_products(MOD_TWO, NMB, MOD_PLACES[2])
                for b in range(5):
                    if b < 4:
                        peer_prep(t0 + b + 1)
                    peer_values(t0 + b)

            def input_transposes(j):
                R = rows5(j)
                if j >= 2:
                    pe.wait_ge(s_tqhc, j - 1)
                for m in range(2):
                    pe.wait_ge(s_hin, 2 * j + m + 1)
                    h = at(MH + m * D, D, 0, R)
                    for k in range(KD):
                        ins = pe.transpose(psum[:, 2 * m + k // 4, P * (k % 4):P * (k % 4) + R],
                                           h[:, P * k:P * (k + 1)], ident[0:R, 0:R])
                    ins.then_inc(s_tx, 1)

            def input_products(j):
                R = rows5(j)
                if j:
                    pe.wait_ge(s_kvr, 2 * j)
                for m, (w, n_) in enumerate(((wdkv, KVC), (wdq, QL))):
                    pe.wait_ge(s_txc, 2 * j + m + 1)
                    for k in range(KD):
                        ins = pe.matmul(psum[0:R, 4 + m, 0:n_], mht[m][:, k, 0:R], w[:, k, :], start=(k == 0),
                                        stop=(k == KD - 1))
                    ins.then_inc(s_pr, 1)

            def head_queries(j):
                R = rows5(j)
                kvr = at(KVR + (j % 2) * KVC, KVC, 0, R)
                pe.wait_ge(s_kvr, 2 * j + 1)
                if j:
                    pe.wait_ge(s_tlc, 2 * j)
                for c in range(2):
                    pe.transpose(psum[:, 6, P * c:P * c + R], kvr[:, P * c:P * (c + 1)], ident[0:R, 0:R])
                pe.transpose(psum[0:QKD, 6, 2 * P:2 * P + R], kvr[:, KVC - QKD:KVC], ident[0:R, 0:R]
                             ).then_inc(s_tl, 1)
                pe.wait_ge(s_kvr, 2 * j + 2)
                for k in range(QL // P):
                    ins = pe.transpose(psum[:, 7, P * k:P * k + R], at(MCQ + P * k, P, 0, R), ident[0:R, 0:R])
                ins.then_inc(s_tl, 1)
                pe.wait_ge(s_tlc, 2 * j + 2)
                pe.wait_ge(s_txc, 2 * min(j + 2, 5))
                if j:
                    pe.wait_ge(s_tqhc, j)
                cqt = at(MCQT, QL).rearrange("p (k t) -> p k t", k=4)
                for c in range(3):
                    for k in range(QL // P):
                        ins = pe.matmul(psum[0:R, c, :], cqt[:, k, 0:R], wuq[:, k, 512 * c:512 * (c + 1)],
                                        start=(k == 0), stop=(k == QL // P - 1))
                ins.then_inc(s_q, 1)

            def head_transposes(j):
                R = rows5(j)
                pe.wait_ge(s_qr, j + 1)
                for h in range(NH):
                    ins = pe.transpose(psum[0:QKD, h // 4, P * (h % 4):P * (h % 4) + R],
                                       at(MQ + QKD * h, QKD, 0, R), ident[0:R, 0:R])
                ins.then_inc(s_tqh, 1)

            def attention_pe():
                pe.wait_ge(s_mw, 144)
                input_transposes(0)
                input_products(0)
                for j in range(5):
                    if j < 4:
                        input_transposes(j + 1)
                    head_queries(j)
                    if j < 4:
                        input_products(j + 1)
                    head_transposes(j)
                pe.wait_ge(s_lw, LATE_HEADS)
                pe.wait_ge(s_tqhc, 5)
                for c in range(2):
                    for h in range(NH):
                        ins = pe.matmul(psum[:, 5, (c * NH + h) * NB:(c * NH + h + 1) * NB],
                                        wkt[:, h, P * c:P * (c + 1)], qts[0:NOPE, h, :], start=True, stop=True)
                ins.then_inc(s_ql, 1)
                pe.wait_ge(s_tlc, 10)
                for q in range(NH // 2):
                    if q >= 4:
                        pe.wait_ge(s_kta, q - 3)
                        pe.wait_ge(s_ktv, q - 3)
                    for c in range(2):
                        ins = pe.matmul(psum[:, q % 4, :], wk[:, c, P * q:P * (q + 1)], ckvt[:, c, 0:SEQ],
                                        start=(c == 0), stop=(c == 1))
                    ins.then_inc(s_ktp, 1)
                pe.wait_ge(s_qlc, 1)
                for i in range(NTILE):
                    if i >= 2:
                        pe.wait_ge(s_vc, i - 1)
                    for n_ in range(2):
                        for c in range(2):
                            ins = pe.matmul(psum[:, 4 + 2 * (i % 2) + n_, :], ckvt[:, c, P * i:P * (i + 1)],
                                            wv[:, c, 512 * n_:512 * (n_ + 1)], start=(c == 0), stop=(c == 1))
                    ins.then_inc(s_vp, 1)
                pe.wait_ge(s_kta, NH // 2)
                pe.wait_ge(s_ktv, NH // 2)
                pe.wait_ge(s_ktr, 1)
                pe.wait_ge(s_vc, NTILE)
                for n_ in range(NTILE * NH + 2):
                    if n_ < NTILE * NH:
                        i, h = divmod(n_, NH)
                        w = P * (i + 1)
                        if n_ >= 2:
                            pe.wait_ge(s_e2, n_ - 1)
                        pe.matmul(psum[:, n_ % 2, 0:w], qtm[0:QKD, h, P * i:w], kt_[0:QKD, h, 0:w], start=True,
                                  stop=False, skip_group_check=True)
                        pe.matmul(psum[:, n_ % 2, P * i:w], ident, at(MASK, P), start=False, stop=True,
                                  skip_group_check=True).then_inc(s_S, 1)
                    if 1 <= n_ <= NTILE * NH:
                        m = n_ - 1
                        pe.wait_ge(s_e2, m + 1)
                        if m >= 2:
                            pe.wait_ge(s_Tc, m - 1)
                        for k in range(m // NH + 1):
                            ins = pe.transpose(psum[:, 2 + m % 2, P * k:P * (k + 1)],
                                               at(PP + (m % 2) * SEQ + P * k, P), ident)
                        ins.then_inc(s_T, 1)
                    if n_ >= 2:
                        m = n_ - 2
                        i, h = divmod(m, NH)
                        u = m // 8
                        pe.wait_ge(s_Tc, m + 1)
                        if u >= 2 and m % 8 == 0:
                            pe.wait_ge(s_on, u - 1)
                        for k in range(i + 1):
                            ins = pe.matmul(psum[:, 4 + u % 2, VH * (m % 8):VH * (m % 8 + 1)],
                                            at(PTT + (m % 2) * SEQ + P * k, P), vv[:, k, VH * h:VH * (h + 1)],
                                            start=(k == 0), stop=(k == i))
                        ins.then_inc(s_pv, 1)
                        if h == 0 and i:
                            project(i - 1)
                project(3)
                for b in range(NB + 1):
                    if b < NB:
                        ck = CK[b % 2]
                        pe.wait_ge(s_ck[b % 2], 32 * (b // 2 + 1))
                        for q in range(5):
                            if q < 4:
                                pe.wait_ge(s_ctv if q % 2 else s_cta, 2 * b + q // 2) if 2 * b + q // 2 else None
                                for c in range(2):
                                    for r in range(4):
                                        pe.transpose(psum[:, 2 * (q % 2) + c, P * r:P * (r + 1)],
                                                     at(ck + (4 * q + r) * KVL + P * c, P), ident)
                                for r in range(4):
                                    ins = pe.transpose(psum[0:ROPE, 4 + q % 2, P * r:P * (r + 1)],
                                                       at(ck + ROWK + (4 * q + r) * ROPE, ROPE), ident)
                                ins.then_inc(s_ct, 1)
                            if q:
                                cache_scores(b, q - 1)
                        cache_scores(b, 4)
                    if b >= 1:
                        c_ = b - 1
                        sc = at(SCS[c_ % 2], NKEY, 0, NH)
                        pe.wait_ge(s_ce, c_ + 1)
                        pe.wait_ge(s_csc, 5 * min(b + 1, NB))
                        for r in range(17):
                            n_ = P if r < 16 else NB
                            ins = pe.transpose(psum[0:n_, 6, NH * r:NH * (r + 1)], sc[:, P * r:P * r + n_],
                                               ident[0:NH, 0:NH])
                        ins.then_inc(s_cT, 1)
                        pe.wait_ge(s_cTc, c_ + 1)
                        if c_:
                            pe.wait_ge(s_coc, c_)
                        ck = CK[c_ % 2]
                        for r in range(16):
                            pe.matmul(psum[0:NH, 7, 0:KVL], pts[:, r, :], at(ck + r * KVL, KVL), start=(r == 0),
                                      stop=False)
                        pe.matmul(psum[0:NH, 7, 0:KVL], pts[0:NB, 16, :], at(KVR, KVL, 0, NB), start=False,
                                  stop=True).then_inc(s_cpv, 1)
                        pe.wait_ge(s_col, c_ + 1)
                        for c in range(2):
                            ins = pe.transpose(psum[:, 7, KVL + NH * c:KVL + NH * (c + 1)],
                                               at(OL + P * c, P, 0, NH), ident[0:NH, 0:NH])
                        ins.then_inc(s_cot, 1)
                pe.wait_ge(s_coc, NB)
                for h in range(NH):
                    for c in range(2):
                        ins = pe.matmul(psum[0:NB, h // 8, VH * (h % 8):VH * (h % 8 + 1)], olt[:, c, h, :],
                                        wv[:, c, VH * h:VH * (h + 1)], start=(c == 0), stop=(c == 1))
                ins.then_inc(s_os, 1)
                project(4)

            def cache_scores(b, q):
                m = 5 * b + q
                if m >= 2:
                    pe.wait_ge(s_csc, m - 1)
                if m == 0:
                    pe.wait_ge(s_x3, 4)
                if q == 0 and b >= 2:
                    pe.wait_ge(s_coc, b - 1)
                if q < 4:
                    pe.wait_ge(s_ctv if q % 2 else s_cta, 2 * b + q // 2 + 1)
                    keys_, rot = (kts[:, :, 512 * q:512 * (q + 1)], krts[NOPE:QKD, 512 * q:512 * (q + 1)])
                    out = psum[0:NH, 6 + m % 2, :]
                else:
                    keys_, rot = ckvt[:, :, SEQ:SEQ + NB], at(KRT + SEQ, NB, NOPE, QKD)
                    out = psum[0:NH, 6 + m % 2, 0:NB]
                for c in range(2):
                    pe.matmul(out, qlt[:, c, b, :], keys_[:, c], start=(c == 0), stop=False)
                pe.matmul(out, qts[NOPE:QKD, :, b], rot, start=False, stop=True).then_inc(s_cs, 1)

            def project(j):
                R = rows5(j)
                pe.wait_ge(s_on, 2 * (j + 1) if j < 4 else 9)
                if j:
                    pe.wait_ge(s_x3, j)
                for k in range(KD):
                    ins = pe.transpose(psum[:, 6 + k // 4, P * (k % 4):P * (k % 4) + R], at(OO + P * k, P, 0, R),
                                       ident[0:R, 0:R])
                ins.then_inc(s_ot, 1)
                pe.wait_ge(s_otc, j + 1)
                pe.wait_ge(s_mw, 144 + 48)
                ot = at(OTT, D).rearrange("p (k t) -> p k t", k=KD)
                for n_ in range(2):
                    for k in range(KD):
                        ins = pe.matmul(psum[0:R, 6 + n_, :], ot[:, k, 0:R], wo[:, k, 512 * n_:512 * (n_ + 1)],
                                        start=(k == 0), stop=(k == KD - 1))
                ins.then_inc(s_yy, 1)

            peer_pe(0)
            attention_pe()
            peer_pe(1)


def host_inputs(i):
    f = lambda x: np.ascontiguousarray(x)
    i = {k: np.asarray(v) for k, v in i.items()}
    arr = {}
    c9 = np.concatenate([i["c_prompt"], i["c_sample"]], 0)
    arr["c_t"] = f(c9.T.reshape(KD, P, NC9).transpose(1, 0, 2)).reshape(P, KD * NC9)
    arr["consts"] = np.concatenate([np.eye(P), np.tile(np.arange(TOPK), (P, 1)),
                                    np.arange(P)[:, None] // 16 == np.arange(NB)[None]], 1).astype(np.float32)
    w = np.concatenate([i["w_mod"][0], i["w_mod"][1], i["w_mod_kv"], i["w_mod_final"]], 1)
    arr["w_mod"] = f(w.reshape(KD, P, NMB, MB).transpose(2, 1, 0, 3)).reshape(NMB, P, KD * MB)
    arr["b_mod"] = np.concatenate([i["b_mod"][0], i["b_mod"][1], i["b_mod_kv"], i["b_mod_final"]]).reshape(NMB, MB)
    twice = lambda x: np.concatenate([x, x], 0)
    cols = [twice(i["ssm_a_re"][0].T), twice(i["ssm_a_im"][0].T), np.broadcast_to(i["ssm_log_dt"][0][None], (P, G))]
    for n in ("ssm_b_re", "ssm_b_im"):
        cols.append(twice(i[n][0].transpose(1, 0, 2).reshape(N, G * GP)))
    for n in ("ssm_c_re", "ssm_c_im"):
        cols.append(twice(i[n][0].transpose(2, 0, 1).reshape(N, G * GP)))
    arr["s5_par"] = f(np.concatenate(cols, 1))
    arr["x_prompt"] = i["x_prompt"][0]
    arr["x_sample"] = i["x_sample"][:, 0]
    arr["g_norm"] = i["g_norm"].reshape(4, D)
    arr["ssm_d"] = i["ssm_d"].reshape(1, D)
    st = np.stack([i["state_ssm_re"][0], i["state_ssm_im"][0]])
    arr["state_x"] = f(st.transpose(0, 3, 2, 1)).reshape(P, G, NB)
    arr["state_g"] = f(st.reshape(2, NB, G // 2, 2, N).transpose(3, 4, 0, 2, 1)).reshape(P, G * NB)
    wg = i["ssm_w_glu"][0].reshape(KD, P, 2, 4, 256)
    arr["w_glu"] = f(wg.transpose(1, 3, 0, 2, 4)).reshape(P, KD * 2 * D)
    arr["peer_wq"] = f(i["peer_w_q"].reshape(2, KD, P, 4, HQ // 4).transpose(0, 2, 3, 1, 4)).reshape(2, P, KD * HQ)
    arr["peer_keys"] = f(i["peer_keys"].transpose(0, 4, 1, 2, 3)).reshape(2, P, 2 * PH * P)
    for l in range(2):
        arr[f"peer_u{l}"], arr[f"peer_v{l}"] = i["peer_u"][l], i["peer_v"][l]
    arr["w_dkv"] = f(np.concatenate([i["w_dkv"], i["w_kr"]], 1).reshape(KD, P, KVL + ROPE).transpose(1, 0, 2)
                     ).reshape(P, -1)
    arr["w_dq"] = f(i["w_dq"][0].reshape(KD, P, QL).transpose(1, 0, 2)).reshape(P, -1)
    arr["w_uq"] = f(i["w_uq"][0].reshape(QL // P, P, NH * QKD).transpose(1, 0, 2)).reshape(P, -1)
    ukv = i["w_ukv"].reshape(2, P, NH, NOPE + VH)
    arr["w_k"] = f(ukv[..., :NOPE].transpose(1, 0, 2, 3)).reshape(P, -1)
    arr["w_v"] = f(ukv[..., NOPE:].transpose(1, 0, 2, 3)).reshape(P, -1)
    arr["w_kt"] = f(i["w_ukv"][..., :NOPE].transpose(2, 1, 0)).reshape(NOPE, -1)
    arr["w_o"] = f(i["w_o"][0].reshape(KD, P, D).transpose(1, 0, 2)).reshape(P, -1)
    inv = (np.float32(10000.0) ** (-np.arange(0, ROPE, 2, dtype=np.float32) / np.float32(ROPE))).astype(np.float32)
    pos = np.concatenate([np.arange(SEQ), np.full(P, PAST)]).astype(np.float32)
    ang = pos[:, None] * inv
    cs = np.stack([np.cos(ang), np.sin(ang)], 1).astype(np.float32).reshape(5, P, ROPE).transpose(1, 0, 2)
    mask = np.where(np.arange(P)[None] <= np.arange(P)[:, None], 0, -1e30)
    smask = np.tile(np.where(np.eye(NB) > 0, 0, -1e30).reshape(1, -1), (P, 1))
    arr["rope_mask"] = np.concatenate([cs.reshape(P, -1), mask, smask, np.arange(P)[:, None] % 8], 1
                                      ).astype(np.float32)
    arr["pages"] = f(np.repeat(i["page_table"], 8, 1).T).astype(np.int32)
    arr["g_ckv"], arr["g_cq"] = i["g_ckv"].reshape(1, KVL), i["g_cq"].reshape(1, QL)
    arr["g_kv_norm"], arr["g_final"] = i["g_kv_norm"].reshape(1, D), i["g_final"].reshape(1, D)
    arr["cache_kv"] = i["cache_kv_latent"].reshape(-1, 16 * KVL)
    arr["cache_kr"] = i["cache_k_rope"].reshape(-1, 16 * ROPE)
    return arr


def kernel(**inputs):
    from concourse import bacc
    from concourse.bass_utils import run_bass_kernel_spmd

    arrays = host_inputs(inputs)
    nc = bacc.Bacc("TRN2", target_bir_lowering=False, num_devices=1)
    a = {n: nc.dram_tensor(n, x.shape, mybir.dt.from_np(x.dtype), kind="ExternalInput").ap()
         for n, x in arrays.items()}
    outs = {"out_ssm_p": (P, G), "out_ssm_s": (P, G * NB), "out_kv_p": (SEQ, KVL), "out_kr_p": (SEQ, ROPE),
            "out_kv_s": (NB, KVL), "out_kr_s": (NB, ROPE), "out_y_p": (SEQ, D), "out_y_s": (NB, D)}
    for n, shape in outs.items():
        a[n] = nc.dram_tensor(n, shape, F32, kind="ExternalOutput").ap()
    program(nc, a)
    r = run_bass_kernel_spmd(nc, [arrays], core_ids=[0]).results[0]
    p = r["out_ssm_p"].reshape(2, N, 2, G // 2).transpose(2, 3, 0, 1).reshape(2, 1, 1, G, N)
    s = r["out_ssm_s"].reshape(2, N, 2, G // 2, NB).transpose(2, 4, 3, 0, 1).reshape(2, 1, NB, G, N)
    return (r["out_y_p"].reshape(1, SEQ, D), r["out_y_s"].reshape(NB, 1, D), p[0], p[1],
            r["out_kv_p"].reshape(1, SEQ, KVL), r["out_kr_p"].reshape(1, SEQ, ROPE), s[0], s[1],
            r["out_kv_s"].reshape(NB, 1, KVL), r["out_kr_s"].reshape(NB, 1, ROPE))
```
